# Optimizing a Trainium2 kernel written in Bass

```python
import jax, jax.numpy as jnp
from jax import lax
import numpy as np

D_MODEL = 1024
BATCH = 1
SEQ = 512
DEPTH = 1

PLE_DIM = 256
ATTN_HEADS = 8
HEAD_DIM = 64
ATTN_WIDTH = ATTN_HEADS * HEAD_DIM
IDX_HEADS = 4
IDX_DIM = 64
TOPK_MAX = 256
Q_BLOCK = 128
CONV_WIDTH = D_MODEL // 2
CONV_KERNEL = 31
MIX_WIDTH = ATTN_WIDTH + CONV_WIDTH
IN_SIZES = (ATTN_WIDTH, HEAD_DIM, HEAD_DIM, IDX_HEADS * IDX_DIM, IDX_DIM, IDX_HEADS, 2 * CONV_WIDTH)
IN_WIDTH = sum(IN_SIZES)
IN_SPLITS = tuple(int(s) for s in np.cumsum(IN_SIZES)[:-1])
N_EXPERTS = 32
TOP_K = 4
D_EXPERT = D_MODEL
SWIGLU_LIMIT = 7.0
SWIGLU_ALPHA = 1.702
MOE_BLOCK = 256
ROPE_THETA = 10000.0
EPS = 1e-6

kernel_name = 'hybrid_dsa_conformer_moe_block'

def rms_norm(x, g):
    xf = x.astype(jnp.float32)
    y = xf * lax.rsqrt(jnp.mean(xf * xf, axis=-1, keepdims=True) + EPS)
    return (y * g.astype(jnp.float32)).astype(x.dtype)

def layer_norm(x, g, b):
    xf = x.astype(jnp.float32)
    mu = jnp.mean(xf, axis=-1, keepdims=True)
    var = jnp.mean(jnp.square(xf - mu), axis=-1, keepdims=True)
    y = (xf - mu) * lax.rsqrt(var + EPS)
    return (y * g.astype(jnp.float32) + b.astype(jnp.float32)).astype(x.dtype)

def rope_tables(seq, dim):
    inv = ROPE_THETA ** (-jnp.arange(0, dim, 2, dtype=jnp.float32) / dim)
    ang = jnp.arange(seq, dtype=jnp.float32)[:, None] * inv[None, :]
    return jnp.cos(ang), jnp.sin(ang)

def apply_rope(x, cos, sin):
    extra = x.ndim - 3
    c = cos.reshape((cos.shape[0],) + (1,) * extra + (cos.shape[1],))
    s = sin.reshape((sin.shape[0],) + (1,) * extra + (sin.shape[1],))
    x1, x2 = jnp.split(x.astype(jnp.float32), 2, axis=-1)
    return jnp.concatenate([x1 * c - x2 * s, x2 * c + x1 * s], axis=-1).astype(x.dtype)

def dsa_attention(q, k, v, q_idx, k_idx, w_idx):
    B, S = q.shape[0], q.shape[1]
    n_sel = min(TOPK_MAX, S // 4)
    nb = S // Q_BLOCK
    key_pos = jnp.arange(S, dtype=jnp.int32)
    k_idx_f = k_idx.astype(jnp.float32)

    def to_blocks(a):
        return a.reshape((B, nb, Q_BLOCK) + a.shape[2:]).swapaxes(0, 1)

    def one_block(args):
        qb, qib, wb, tb = args
        s = jnp.einsum('bqhd,bsd->bqhs', qib.astype(jnp.float32), k_idx_f) * (IDX_DIM ** -0.5)
        score = jnp.einsum('bqhs,bqh->bqs', jax.nn.relu(s), wb.astype(jnp.float32)) * (IDX_HEADS ** -0.5)
        causal = key_pos[None, :] <= tb[:, None]
        score = jnp.where(causal[None], score, -jnp.inf)
        _, idx = lax.top_k(score, n_sel)
        valid = idx <= tb[None, :, None]
        k_sel = jax.vmap(lambda kb, ib: kb[ib])(k, idx)
        v_sel = jax.vmap(lambda vb, ib: vb[ib])(v, idx)
        logits = jnp.einsum('bqhd,bqkd->bqhk', qb, k_sel).astype(jnp.float32) * (HEAD_DIM ** -0.5)
        logits = jnp.where(valid[:, :, None, :], logits, -jnp.inf)
        probs = jax.nn.softmax(logits, axis=-1).astype(v.dtype)
        return jnp.einsum('bqhk,bqkd->bqhd', probs, v_sel)

    pos_blocks = key_pos.reshape(nb, Q_BLOCK)
    out = lax.map(one_block, (to_blocks(q), to_blocks(q_idx), to_blocks(w_idx), pos_blocks))
    return out.swapaxes(0, 1).reshape(B, S, ATTN_HEADS * HEAD_DIM)

def conformer_conv(u, glu_b, dw_w, dw_b, ln_g, ln_b):
    a, g = jnp.split(u + glu_b, 2, axis=-1)
    h = a * jax.nn.sigmoid(g)
    h = lax.conv_general_dilated(
        h, dw_w[:, None, :].astype(h.dtype), window_strides=(1,),
        padding=[(CONV_KERNEL - 1, 0)], dimension_numbers=('NWC', 'WIO', 'NWC'),
        feature_group_count=CONV_WIDTH) + dw_b
    h = layer_norm(h, ln_g, ln_b)
    return jax.nn.silu(h)

def moe(x, w_router, b_router, w_up, b_up, w_down, b_down):
    N = x.shape[0]
    logits = (x @ w_router).astype(jnp.float32) + b_router.astype(jnp.float32)
    top_v, top_e = lax.top_k(logits, TOP_K)
    gates = jax.nn.softmax(top_v, axis=-1)
    A = N * TOP_K
    e_flat = top_e.reshape(A)
    tok_flat = jnp.arange(A, dtype=jnp.int32) // TOP_K
    gate_flat = gates.reshape(A)
    order = jnp.argsort(e_flat)
    e_sorted = e_flat[order]
    counts = jnp.bincount(e_flat, length=N_EXPERTS)
    padded = (counts + MOE_BLOCK - 1) // MOE_BLOCK * MOE_BLOCK
    start = jnp.cumsum(counts) - counts
    cum_padded = jnp.cumsum(padded)
    pstart = cum_padded - padded
    dest = pstart[e_sorted] + jnp.arange(A, dtype=jnp.int32) - start[e_sorted]
    n_blocks = (A + N_EXPERTS * (MOE_BLOCK - 1) + MOE_BLOCK - 1) // MOE_BLOCK
    P = n_blocks * MOE_BLOCK
    row_tok = jnp.zeros((P,), jnp.int32).at[dest].set(tok_flat[order])
    row_gate = jnp.zeros((P,), jnp.float32).at[dest].set(gate_flat[order])
    block_start = jnp.arange(n_blocks, dtype=jnp.int32) * MOE_BLOCK
    block_exp = jnp.minimum(jnp.searchsorted(cum_padded, block_start, side='right'), N_EXPERTS - 1)

    def expert_block(args):
        e, toks = args
        h = x[toks] @ w_up[e] + b_up[e]
        gt, lin = jnp.split(h, 2, axis=-1)
        gt = jnp.minimum(gt, SWIGLU_LIMIT)
        lin = jnp.clip(lin, -SWIGLU_LIMIT, SWIGLU_LIMIT)
        act = gt * jax.nn.sigmoid(SWIGLU_ALPHA * gt) * (lin + 1.0)
        return act @ w_down[e] + b_down[e]

    y_rows = lax.map(expert_block, (block_exp, row_tok.reshape(n_blocks, MOE_BLOCK)))
    y_rows = y_rows.reshape(P, x.shape[1]).astype(jnp.float32) * row_gate[:, None]
    return jax.ops.segment_sum(y_rows, row_tok, num_segments=N).astype(x.dtype)

def setup_inputs(seed: int = 0) -> dict:
    key = jax.random.key(seed)
    ks = jax.random.split(key, 21)
    f32 = jnp.float32

    def nrm(k, shape, scale):
        return jax.random.normal(k, shape, f32) * scale

    def gain(k, shape):
        return 1.0 + 0.05 * jax.random.normal(k, shape, f32)

    return {
        'x': nrm(ks[0], (BATCH, SEQ, D_MODEL), 1.0),
        'p': nrm(ks[1], (DEPTH, BATCH, SEQ, PLE_DIM), 1.0),
        'w_in': nrm(ks[2], (DEPTH, D_MODEL, IN_WIDTH), D_MODEL ** -0.5),
        'w_out': nrm(ks[3], (DEPTH, MIX_WIDTH, D_MODEL), MIX_WIDTH ** -0.5),
        'g_mix': gain(ks[4], (DEPTH, D_MODEL)),
        'g_ffn': gain(ks[5], (DEPTH, D_MODEL)),
        'conv_glu_b': nrm(ks[6], (DEPTH, 2 * CONV_WIDTH), 0.02),
        'conv_dw_w': nrm(ks[7], (DEPTH, CONV_KERNEL, CONV_WIDTH), CONV_KERNEL ** -0.5),
        'conv_dw_b': nrm(ks[8], (DEPTH, CONV_WIDTH), 0.02),
        'conv_ln_g': gain(ks[9], (DEPTH, CONV_WIDTH)),
        'conv_ln_b': nrm(ks[10], (DEPTH, CONV_WIDTH), 0.02),
        'w_router': nrm(ks[11], (DEPTH, D_MODEL, N_EXPERTS), D_MODEL ** -0.5),
        'b_router': nrm(ks[12], (DEPTH, N_EXPERTS), 0.01),
        'w_up': nrm(ks[13], (DEPTH, N_EXPERTS, D_MODEL, 2 * D_EXPERT), D_MODEL ** -0.5),
        'b_up': nrm(ks[14], (DEPTH, N_EXPERTS, 2 * D_EXPERT), 0.02),
        'w_down': nrm(ks[15], (DEPTH, N_EXPERTS, D_EXPERT, D_MODEL), D_EXPERT ** -0.5),
        'b_down': nrm(ks[16], (DEPTH, N_EXPERTS, D_MODEL), 0.02),
        'w_ple_proj': nrm(ks[17], (DEPTH, PLE_DIM, D_MODEL), PLE_DIM ** -0.5),
        'w_ple_gate': nrm(ks[18], (DEPTH, D_MODEL, D_MODEL), D_MODEL ** -0.5),
        'g_ple': gain(ks[19], (DEPTH, D_MODEL)),
        'g_final': gain(ks[20], (D_MODEL,)),
    }

def reference(x, p, w_in, w_out, g_mix, g_ffn, conv_glu_b, conv_dw_w, conv_dw_b, conv_ln_g,
              conv_ln_b, w_router, b_router, w_up, b_up, w_down, b_down, w_ple_proj,
              w_ple_gate, g_ple, g_final):
    B, S, D = x.shape
    cos_a, sin_a = rope_tables(S, HEAD_DIM)
    cos_i, sin_i = rope_tables(S, IDX_DIM)
    h = x
    for i in range(DEPTH):
        u = rms_norm(h, g_mix[i]) @ w_in[i]
        q, k, v, qi, ki, wi, cu = jnp.split(u, IN_SPLITS, axis=-1)
        q = apply_rope(q.reshape(B, S, ATTN_HEADS, HEAD_DIM), cos_a, sin_a)
        k = apply_rope(k, cos_a, sin_a)
        qi = apply_rope(qi.reshape(B, S, IDX_HEADS, IDX_DIM), cos_i, sin_i)
        ki = apply_rope(ki, cos_i, sin_i)
        attn = dsa_attention(q, k, v, qi, ki, wi)
        conv = conformer_conv(cu, conv_glu_b[i], conv_dw_w[i], conv_dw_b[i],
                              conv_ln_g[i], conv_ln_b[i])
        h = h + jnp.concatenate([attn, conv], axis=-1) @ w_out[i]
        y = moe(rms_norm(h, g_ffn[i]).reshape(B * S, D), w_router[i], b_router[i],
                w_up[i], b_up[i], w_down[i], b_down[i])
        h = h + y.reshape(B, S, D)
        gate = jax.nn.sigmoid((rms_norm(h, g_ple[i]) @ w_ple_gate[i]).astype(jnp.float32))
        h = h + ((p[i] @ w_ple_proj[i]).astype(jnp.float32) * gate).astype(h.dtype)
    return rms_norm(h, g_final)


_drawn_inputs = setup_inputs


def setup_inputs(seed=0):
    import zlib

    import numpy as np

    out = dict(_drawn_inputs(seed))
    spreads = {}
    factors = {'b_up': 5.931, 'b_down': 6.826, 'g_ple': 7.082}
    for name, (base, spread) in spreads.items():
        noise = np.random.default_rng([zlib.crc32(name.encode()), seed]).standard_normal(out[name].shape)
        drawn = base * np.exp(spread * noise) if base else spread * noise
        out[name] = __import__('jax').numpy.asarray(drawn.astype(out[name].dtype))
    for name, factor in factors.items():
        out[name] = (out[name] * factor).astype(out[name].dtype)
    return out
```

```python
from contextlib import ExitStack

import concourse.bass as bass
from concourse import mybir
import numpy as np

F32 = mybir.dt.float32
F32R = mybir.dt.float32r
I32 = mybir.dt.int32
ALU = mybir.AluOpType
ACT = mybir.ActivationFunctionType
AX = mybir.AxisListType

P = 128
SEQ, D = 512, 1024
NT = SEQ // P
NK = D // P
PLE = 256
HEADS, HD = 8, 64
IDX_HEADS = 4
CONV_W, TAPS = 512, 31
NJ = CONV_W // P
IN_W = HEADS * HD + 2 * HD + IDX_HEADS * HD + HD + IDX_HEADS + 2 * CONV_W
ATT_W = IN_W - 2 * CONV_W
REST_W = ATT_W - 512
N_SEL = min(256, SEQ // 4)
NE, TOP = 32, 4
LIMIT, ALPHA, EPS = 7.0, 1.702, 1e-6
NEG = -1e30
TAKEN = -3e38
SKIP = 4096.0
BLK = 128
NB = SEQ // BLK
RAW, SPLIT = 8, 3
RAW1 = 4
C0 = 12
UPC, DNC = 8, 4
PER = UPC + DNC
RUN = PER * NE
TAIL = 5

IDENT, TRI, ONES, IOTA, CAUS, COS, SIN, TOK, EYE = 0, 128, 256, 384, 512, 640, 768, 896, 900
NCONST = 932


def build(nc, x, p, w_in, w_out, g_mix, g_ffn, conv_glu_b, conv_dw_w, conv_dw_b, conv_ln_g, conv_ln_b,
          w_router, b_router, w_up, b_up, w_down, b_down, w_ple_proj, w_ple_gate, g_ple, g_final,
          consts, out):
    ctx = ExitStack()
    with ctx:
        def sb(name, shape, dt=F32, stack=ctx):
            return stack.enter_context(nc.sbuf_tensor(name, shape, dt))

        def sem(name):
            return ctx.enter_context(nc.semaphore(name))

        xn_rows = nc.dram_tensor("xn_rows", [SEQ, D], F32, kind="Internal").ap()
        y_rows = nc.dram_tensor("y_rows", [TOP * SEQ, D], F32, kind="Internal").ap()

        cst = sb("cst", [P, NCONST])
        par = sb("par", [P, 144])
        gbc = sb("gbc", [P, D])
        h = sb("h", [P, NT, D])
        raw_a = sb("raw_a", [P, RAW1, 2048])
        w_hi = sb("w_hi", [P, SPLIT, 2048], F32R)
        w_lo = sb("w_lo", [P, SPLIT, 2048], F32R)
        pos = sb("pos", [P, NT, NB * NE])
        info = sb("info", [P, NT, NE, 3])
        st = sb("st", [P, 24])
        flag = sb("flag", [P, 1], I32)
        brt = sb("brt", [P, NE])

        with ExitStack() as s1:
            t_hi = sb("t_hi", [P, NK, SEQ], F32R, s1)
            t_lo = sb("t_lo", [P, NK, SEQ], F32R, s1)
            reg_a = sb("reg_a", [P, 4224], F32, s1)
            r_t = sb("r_t", [P, NK, SEQ], F32, s1)
            tmp = sb("tmp", [P, 2, 1024], F32, s1)
            rl = sb("rl", [P, 4, 512], F32, s1)
            lg = sb("lg", [P, 2, 512], F32, s1)
            uv = sb("uv", [P, NT, 68], F32, s1)
            work = sb("work", [P, 1152], F32, s1)
            mx = sb("mx", [P, 3, 32], F32, s1)
            m8 = sb("m8", [P, 8], F32, s1)
            attn = sb("attn", [P, 512], F32, s1)
            stage = sb("stage", [P, 128], F32, s1)
            stage2 = sb("stage2", [20, 128], F32, s1)
            wr = sb("wr", [P, NK, NE], F32, s1)
        xn = reg_a[:, 0:4096].rearrange("p (t n) -> p t n", t=NT)
        roped = xn
        PADW = 30 + SEQ
        hpad = reg_a[:, 0:4 * PADW].rearrange("p (j n) -> p j n", j=NJ)
        acc = reg_a[:, 4 * PADW:4 * PADW + 2048].rearrange("p (j n) -> p j n", j=NJ)
        sg = tmp[:, :, :].rearrange("p a (b n) -> p (a b) n", b=2)
        probs, probs_t = rl[:, 0:2, :], rl[:, 2:4, :]

        with ExitStack() as s2:
            raw_b = sb("raw_b", [P, RAW - RAW1, 2048], F32, s2)
            g_sb = sb("g_sb", [P, D], F32, s2)
            l_sb = sb("l_sb", [P, D], F32, s2)
            s_sb = sb("s_sb", [P, D], F32, s2)
            a_hi = sb("a_hi", [P, NK, P], F32R, s2)
            x_hi = sb("x_hi", [P, 2, NK, P], F32R, s2)
            x_lo = sb("x_lo", [P, 2, NK, P], F32R, s2)
            onehot = sb("onehot", [P, NT, BLK], F32, s2)
            xg = sb("xg", [P, D], F32, s2)
            y_sb = sb("y_sb", [P, D], F32, s2)
            a_lo = sb("a_lo", [P, NK, P], F32R, s2)
            sel = sb("sel", [64, P], F32R, s2)
            pos_e = sb("pos_e", [P, NT], F32, s2)
            gidx = sb("gidx", [P, 1], I32, s2)
            didx = sb("didx", [P, 2, 1], I32, s2)
            dsti = sb("dsti", [P, 2, 1], I32, s2)
            gate = sb("gate", [P, 2, 1], F32, s2)
            sb("apart", [P, 640], F32, s2)
            bup = sb("bup", [64, 2048], F32R, s2)
        with ExitStack() as s3:
            s3.enter_context(nc.sbuf_tensor("hold", [P, RAW - RAW1, 2048], F32))
            z_hi = sb("z_hi", [P, NK, SEQ], F32R, s3)
            z_lo = sb("z_lo", [P, NK, SEQ], F32R, s3)
            p_hi = z_hi[:, 0:2, :]
            p_lo = z_lo[:, 0:2, :]
            p_sb = sb("p_sb", [P, NT, PLE], F32, s3)
            xn3 = sb("xn3", [P, 2, D], F32, s3)
            sq3 = sb("sq3", [P, D], F32, s3)
        pp = raw_b[:, 1:3, :].rearrange("p a (b n) -> p (a b) n", b=2)
        yb = raw_b[:, 3, :].rearrange("p (a n) -> p a n", a=2)
        rt = lg[:, :, :].rearrange("p a n -> p (a n)")
        gt_t = tmp[0:NE, 0, 0:SEQ]
        bdn = tmp[0:NE, 1, :]
        bup_raw = rl[0:64, :, :].rearrange("p a n -> p (a n)")

        ps = ctx.enter_context(nc.psum_tensor("ps", [P, 8, 512], F32))

        ident = cst[:, IDENT:IDENT + P]
        ones = cst[:, ONES:ONES + P]

        s_cst, s_stage, s_gbc, s_p = sem("s_cst"), sem("s_stage"), sem("s_gbc"), sem("s_p")
        s_x = [sem(f"s_x{t}") for t in range(NT)]
        s_wr, s_bup, s_bdn = sem("s_wr"), sem("s_bup"), sem("s_bdn")
        raw_in = [sem(f"raw_in{i}") for i in range(RAW)]
        hi_done, lo_done, used = sem("hi_done"), sem("lo_done"), sem("used")
        dve_seq, ppg_done = sem("dve_seq"), sem("ppg_done")
        sq_done, ms_done, rs_done, xn_done = sem("sq_done"), sem("ms_done"), sem("rs_done"), sem("xn_done")
        tp_done, thi_done, tlo_done = sem("tp_done"), sem("thi_done"), sem("tlo_done")
        par_tp, par_in = sem("par_tp"), sem("par_in")
        uv_done, rope_done, rtp_done, rt_done = sem("uv_done"), sem("rope_done"), sem("rtp_done"), sem("rt_done")
        si_done, rl_done = sem("si_done"), sem("rl_done")
        glu_sig, glu_done = sem("glu_sig"), sem("glu_done")
        s_done, lg_done, exp_done, pt_done, pte_done, pv_done = (sem(n) for n in (
            "s_done", "lg_done", "exp_done", "pt_done", "pte_done", "pv_done"))
        an_done, atp_done, ahi_done, alo_done = sem("an_done"), sem("atp_done"), sem("ahi_done"), sem("alo_done")
        tap_done, cs_done, cc_done, csq_done, cv_done = (sem(n) for n in (
            "tap_done", "cs_done", "cc_done", "csq_done", "cv_done"))
        cr_done, crs_done, cz_done, csg_done, mix_done, mhi_done, mlo_done = (sem(n) for n in (
            "cr_done", "crs_done", "cz_done", "csg_done", "mix_done", "mhi_done", "mlo_done"))
        h1_done = sem("h1_done")
        xn_out = sem("xn_out")
        rlog_done, rex_in, rex_out, sel_done, pos_done, gates_done = (sem(n) for n in (
            "rlog_done", "rex_in", "rex_out", "sel_done", "pos_done", "gates_done"))
        gtp_done, gte_done, bd_done = sem("gtp_done"), sem("gte_done"), sem("bd_done")
        tab_done, flag_done = sem("tab_done"), sem("flag_done")
        buphi_done, bup_done = sem("buphi_done"), sem("bup_done")
        pos_e_in, pool_waits = sem("pos_e_in"), sem("pool_waits")
        oh_done, list_done, idx_done, xg_in, sel_in = (sem(n) for n in (
            "oh_done", "list_done", "idx_done", "xg_in", "sel_in"))
        xt_done, xhi_done, xlo_done = sem("xt_done"), sem("xhi_done"), sem("xlo_done")
        up_free, gl_done, gl2_done, sig_done, act_done = (sem(n) for n in (
            "up_free", "gl_done", "gl2_done", "sig_done", "act_done"))
        at_done, athi_done, atlo_done = sem("at_done"), sem("athi_done"), sem("atlo_done")
        dn_free, y_done, y_out = sem("dn_free"), sem("y_done"), sem("y_out")
        s_yb = [sem("s_yb0"), sem("s_yb1")]
        yadd_done, ptp_done, pphi_done, pplo_done = (sem(n) for n in ("yadd_done", "ptp_done", "pphi_done", "pplo_done"))
        h3_done, fin_done = sem("h3_done"), sem("fin_done")
        s_out = [sem("s_out0"), sem("s_out1")]

        block = ctx.enter_context(nc.Block())

        def up_chunk(base, e, u, first=False):
            return base + u if first else base - DNC + PER * e + u

        def dn_chunk(base, e, d, last=False):
            return base - DNC + PER * (e + 1) + (0 if last else UPC) + d

        def slot8(e_par, part, first=False, last=False):
            if first:
                return part
            return (-DNC + PER * e_par + part) % (2 * PER)

        def raw_slot(s):
            s %= RAW
            return raw_a[:, s, :] if s < RAW1 else raw_b[:, s - RAW1, :]

        def raw_before(s):
            return C0 // RAW1 if s % RAW < RAW1 else 0

        def steps(eng, one):
            one(0, 0)
            one(1, 1)
            with eng.Fori(1, NE // 2 - 1) as j:
                one(2 * j, 0)
                one(2 * j + 1, 1)
            one(NE - 2, 0)
            one(NE - 1, 1)

        def passes(eng, run):
            run(0)
            eng.wait_ge(flag_done, 1)
            more = eng.value_load(flag[0:1, 0:1], min_val=0, max_val=1)
            with eng.If(more > 0):
                with eng.Fori(1, NB) as b:
                    run(b)
            return more

        @block.sync
        def _(sp):
            sp.dma_start(cst[:, :], consts).then_inc(s_cst, 16)
            for t in range(NT):
                sp.dma_start(h[:, t, :], x[0, t * P:(t + 1) * P, :]).then_inc(s_x[t], 16)
            sp.dma_start(gbc[:, :], g_mix[0:1, :].broadcast_to([P, D])).then_inc(s_gbc, 16)
            sp.dma_start(stage[0:TAPS * NJ, :], conv_dw_w[0].rearrange("k (j c) -> (k j) c", j=NJ)).then_inc(s_stage, 16)
            for n, (v, r0, r) in enumerate(((conv_glu_b, 0, 8), (conv_dw_b, 8, 4), (conv_ln_g, 12, 4), (conv_ln_b, 16, 4))):
                sp.dma_start(stage2[r0:r0 + r, :], v[0].rearrange("(j c) -> j c", j=r)).then_inc(s_stage, 16)

            def load1(c):
                s = c % RAW1
                if c < 4:
                    dst = raw_a[:, s, 0:2 * ATT_W].rearrange("p (a n) -> p a n", a=2)
                    src = w_in[0, c * 256:(c + 1) * 256, 0:ATT_W]
                elif c < 8:
                    dst = raw_a[:, s, :].rearrange("p (a n) -> p a n", a=2)
                    src = w_in[0, (c - 4) * 256:(c - 3) * 256, ATT_W:IN_W]
                else:
                    dst = raw_a[:, s, :].rearrange("p (a n) -> p a n", a=2)
                    src = w_out[0, (c - 8) * 256:(c - 7) * 256, :]
                if c >= RAW1:
                    sp.wait_ge(lo_done, c - RAW1 + 1)
                sp.dma_start(dst, src.rearrange("(a p) n -> p a n", p=P)).then_inc(raw_in[s], 16)

            for c in range(C0):
                load1(c)
                if c == 3:
                    sp.dma_start(wr[:, :, :], w_router[0].rearrange("(k p) n -> p k n", p=P)).then_inc(s_wr, 16)
                    sp.dma_start(brt[:, :], b_router[0:1, :].broadcast_to([P, NE])).then_inc(s_wr, 16)
                    sp.wait_ge(xn_done, NT)
                    sp.dma_start(gbc[:, :], g_ffn[0:1, :].broadcast_to([P, D])).then_inc(s_gbc, 16)

            w_up_c = w_up[0].rearrange("e (k p) n -> (e k) p n", p=P)
            w_dn_c = w_down[0].rearrange("e (c a p) n -> (e c) p a n", p=P, a=2)

            def run(b):
                base = C0 + b * RUN

                def ups(e, par, first=False):
                    for u in range(UPC):
                        ring = slot8(par, u, first)
                        if first and isinstance(b, int):
                            if u < RAW1:
                                sp.wait_ge(lo_done, C0 - RAW1 + u + 1)
                            elif u == RAW1:
                                sp.wait_ge(used, C0)
                        else:
                            sp.wait_ge(lo_done, up_chunk(base, e, u, first) - RAW + 1)
                        sp.dma_start(raw_slot(ring), w_up_c[bass.ds(e * UPC + u, 1), :, :].rearrange("o p n -> (o p) n")
                                     ).then_inc(raw_in[ring % RAW], 16)

                def downs(e, par, last=False):
                    for d in range(DNC):
                        ring = slot8(par, (0 if last else UPC) + d)
                        sp.wait_ge(lo_done, dn_chunk(base, e, d, last) - RAW + 1)
                        sp.dma_start(raw_slot(ring).rearrange("p (a n) -> p a n", a=2),
                                     w_dn_c[bass.ds(e * DNC + d, 1), :, :, :].rearrange("o p a n -> (o p) a n")
                                     ).then_inc(raw_in[ring % RAW], 16)

                def one(e, par):
                    first = isinstance(e, int) and e == 0
                    ups(e, par, first)
                    if not first:
                        downs(e - 1, par)

                steps(sp, one)
                downs(NE - 1, 0, True)

            more = passes(sp, run)
            base = sp.snap(more * ((NB - 1) * RUN))
            for i in range(TAIL):
                sp.wait_ge(lo_done, base + (C0 + RUN + i - RAW + 1))
                src = w_ple_proj[0] if i == 0 else w_ple_gate[0, (i - 1) * 256:i * 256, :]
                sp.dma_start(raw_slot(i).rearrange("p (a n) -> p a n", a=2),
                             src.rearrange("(a p) n -> p a n", p=P)).then_inc(raw_in[i % RAW], 16)
            ybase = sp.snap(more * ((NB - 1) * NE))
            sp.wait_ge(lo_done, base + (C0 + RUN))
            sp.wait_ge(act_done, ybase + NE)
            sp.dma_start(gbc[:, :], g_ple[0:1, :].broadcast_to([P, D])).then_inc(s_gbc, 16)
            sp.wait_ge(y_out, ybase * 16 + 16 * NE)
            sp.dma_start(p_sb[:, :, :], p[0, 0].rearrange("(t p) n -> p t n", p=P)).then_inc(s_p, 16)
            yv = y_rows.rearrange("(k t p) n -> t k p n", k=TOP, p=P)
            for n in range(NT * TOP):
                if n >= 2:
                    sp.wait_ge(yadd_done, n - 1)
                sp.dma_start(yb[:, n % 2, :], yv[n // TOP, n % TOP]).then_inc(s_yb[n % 2], 16)
            sp.wait_ge(xn_done, 3 * NT)
            sp.dma_start(gbc[:, :], g_final.rearrange("(a n) -> a n", a=1).broadcast_to([P, D])).then_inc(s_gbc, 16)
            for t in range(NT):
                sp.wait_ge(fin_done, t + 1)
                sp.dma_start(out[0, t * P:(t + 1) * P, :], xn3[:, t % 2, :]).then_inc(s_out[t % 2], 16)
            for q in s_out:
                sp.wait_ge(q, 16 * NT // 2)

        @block.gpsimd
        def _(pool):
            def wait(s, value):
                pool.wait_ge(s, value)
                pool.sem_inc(pool_waits)

            def run(b):
                s0 = b * NE
                base = C0 + b * RUN

                def prep(e, par, first=False):
                    if isinstance(e, int) and e == 0 and isinstance(b, int):
                        wait(tab_done, 1)
                        wait(bup_done, 1)
                        wait(bd_done, 1)
                    else:
                        wait(list_done, s0 + e)
                    nc.gpsimd.tensor_copy(pos_e[:, :], pos[:, :, bass.ds(s0 + e, 1)].rearrange("p t o -> p (t o)")).then_inc(pos_e_in, 1)
                    wait(pos_e_in, s0 + e + 1)
                    for t in range(NT):
                        i = nc.gpsimd.tensor_scalar(onehot[:, t, :], cst[:, IOTA:IOTA + P], pos_e[:, t:t + 1], None, ALU.is_equal)
                    i.then_inc(oh_done, 1)

                def gather(e, par):
                    wait(idx_done, s0 + e + 1)
                    if not (isinstance(e, int) and e == 0 and isinstance(b, int)):
                        wait(xt_done, (s0 + e) * 2)
                    else:
                        wait(xn_out, 16 * NT)
                    pool.indirect_dma_start(xg[:, :], None, xn_rows, bass.IndirectOffsetOnAxis(ap=gidx[:, 0:1], axis=0),
                                            bounds_check=SEQ - 1, oob_is_err=False).then_inc(xg_in, 16)

                def selector(e, par):
                    if not (isinstance(e, int) and e == 0 and isinstance(b, int)):
                        c = base if isinstance(e, int) and e == 0 else up_chunk(base, e - 1, UPC, isinstance(e, int) and e == 1)
                        wait(used, c)
                    nc.gpsimd.tensor_copy(sel[:, :], cst[0:64, bass.ds(EYE + e, 1)].broadcast_to([64, P])).then_inc(sel_in, 1)

                def scatter(e, par):
                    wait(y_done, s0 + e + 1)
                    pool.indirect_dma_start(y_rows, bass.IndirectOffsetOnAxis(ap=dsti[:, par, 0:1], axis=0), y_sb[:, :], None,
                                            bounds_check=TOP * SEQ - 1, oob_is_err=False).then_inc(y_out, 16)

                def one(e, par):
                    if not (isinstance(e, int) and e == NE - 1):
                        prep(e + 1, 1 - par)
                    if not (isinstance(e, int) and e < 2):
                        scatter(e - 2, par)
                    if not (isinstance(e, int) and e == NE - 1):
                        gather(e + 1, 1 - par)
                        selector(e + 1, 1 - par)

                prep(0, 0)
                gather(0, 0)
                selector(0, 0)
                steps(pool, one)
                scatter(NE - 2, 0)
                scatter(NE - 1, 1)

            passes(pool, run)

        @block.scalar
        def _(act):
            def squares(src, n0):
                for t in range(NT):
                    if n0 == 0:
                        act.wait_ge(s_x[t], 16)
                    elif n0 == 1:
                        act.wait_ge(h1_done, t + 1)
                    junk = (rl[:, 0:2, :] if n0 == 0 else lg[:, :, :]).rearrange("p a n -> p (a n)")
                    nc.scalar.activation(junk, src[:, t, :], ACT.Square, accum_out=st[:, t:t + 1]).then_inc(sq_done, 1)
                    act.wait_ge(sq_done, n0 * NT + t + 1)

            def root(n):
                act.wait_ge(ms_done, n)
                nc.scalar.activation(st[:, 8:12], st[:, 4:8], ACT.Sqrt).then_inc(rs_done, 1)

            def hi(c, slot, raw, count, width=2048, fresh=False):
                act.wait_ge(raw_in[slot[0]], count)
                if not fresh:
                    act.wait_ge(used, c - SPLIT + 1)
                nc.scalar.activation(w_hi[:, slot[1], 0:width], raw[:, 0:width], ACT.Copy).then_inc(hi_done, 1)

            def hi1(c):
                hi(c, (c % RAW1, c % SPLIT), raw_a[:, c % RAW1, :], 16 * (c // RAW1 + 1),
                   2 * ATT_W if c < 4 else 2048, c < SPLIT)

            squares(h, 0)
            root(1)
            for c in range(3):
                hi1(c)
            for n in range(2 * NT):
                act.wait_ge(tp_done, n + 1)
                t, k0 = n // 2, 4 * (n % 2)
                nc.scalar.activation(t_hi[:, k0:k0 + 4, t * P:(t + 1) * P],
                                     ps[:, n, :].rearrange("p (k c) -> p k c", k=4), ACT.Copy).then_inc(thi_done, 1)
            act.wait_ge(par_tp, 1)
            nc.scalar.activation(par[:, 0:124], ps[:, 0, 0:124], ACT.Copy).then_inc(par_in, 1)
            nc.scalar.activation(par[:, 124:144], ps[:, 0, 128:148], ACT.Copy).then_inc(par_in, 1)
            for c in range(3, 6):
                hi1(c)
            act.wait_ge(used, 4)
            nc.scalar.activation(uv[:, :, 0:64], ps[:, 4:8, 64:128], ACT.Copy).then_inc(uv_done, 1)
            nc.scalar.activation(uv[:, :, 64:68], ps[:, 4:8, 448:452], ACT.Copy).then_inc(uv_done, 1)
            hi1(6)
            for n, bl in enumerate((4, 5, 6, 7, 0, 1, 2, 3)):
                act.wait_ge(rtp_done, n + 1)
                nc.scalar.activation(r_t[:, bl, :], ps[:, (n + 4) % 8, :], ACT.Copy).then_inc(rt_done, 1)
            for t in range(1, NT):
                for hh in range(IDX_HEADS):
                    n = (t - 1) * IDX_HEADS + hh
                    act.wait_ge(si_done, n + 1)
                    if t > 1:
                        act.wait_ge(cc_done, (t - 2) * IDX_HEADS + hh + 1)
                    nc.scalar.activation(rl[:, hh, 0:(t + 1) * P], ps[:, 4 + hh, 0:(t + 1) * P], ACT.Relu).then_inc(rl_done, 1)
            hi1(7)
            act.wait_ge(par_in, 2)
            for j in range(NJ):
                act.wait_ge(used, 8)
                nc.scalar.activation(sg[:, j, :], ps[:, 4 + j, :], ACT.Sigmoid, bias=par[:, 128 + j:129 + j]).then_inc(glu_sig, 1)
            for c in (8, 9, 10):
                hi1(c)

            def pt_copy(n):
                act.wait_ge(pt_done, n + 1)
                if n >= 2:
                    act.wait_ge(pv_done, n - 1)
                kk = (n // HEADS + 1) * P
                nc.scalar.activation(probs_t[:, n % 2, 0:kk], ps[:, 2 + n % 2, 0:kk], ACT.Copy).then_inc(pte_done, 1)

            def attn_hi(t):
                act.wait_ge(atp_done, t + 1)
                nc.scalar.activation(t_hi[:, 0:4, t * P:(t + 1) * P],
                                     ps[:, 6, :].rearrange("p (k c) -> p k c", k=4), ACT.Copy).then_inc(ahi_done, 1)

            for n in range(32):
                kk = (n // HEADS + 1) * P
                act.wait_ge(lg_done, n + 1)
                if n >= 2:
                    act.wait_ge(pt_done, n - 1)
                nc.scalar.activation(probs[:, n % 2, 0:kk], lg[:, n % 2, 0:kk], ACT.Exp, bias=mx[:, 1, n:n + 1],
                                     scale=HD ** -0.5, accum_out=mx[:, 2, n:n + 1]).then_inc(exp_done, 1)
                if n >= 1:
                    pt_copy(n - 1)
                if n % HEADS == 4 and n > HEADS:
                    attn_hi(n // HEADS - 1)
            pt_copy(31)
            attn_hi(NT - 1)
            for j in range(NJ):
                act.wait_ge(cv_done, j + 1)
                nc.scalar.activation(sg[:, j, :], acc[:, j, :], ACT.Square).then_inc(csq_done, 1)
            act.wait_ge(cr_done, 1)
            nc.scalar.activation(lg[:, 0, :], lg[:, 1, :], ACT.Sqrt).then_inc(crs_done, 1)
            for j in range(NJ):
                act.wait_ge(cz_done, j + 1)
                nc.scalar.activation(sg[:, j, :], acc[:, j, :], ACT.Sigmoid).then_inc(csg_done, 1)
            for j in range(NJ):
                act.wait_ge(mix_done, j + 1)
                nc.scalar.activation(t_hi[:, NJ + j, :], acc[:, j, :], ACT.Copy).then_inc(mhi_done, 1)
            hi1(11)
            act.wait_ge(pv_done, 32)
            for q in range(2):
                act.dma_start(bup_raw[q * NE:(q + 1) * NE, :], b_up[0]).then_inc(s_bup, 16)
            act.dma_start(bdn, b_down[0]).then_inc(s_bdn, 16)
            squares(h, 1)
            root(2)
            for t in range(NT):
                act.wait_ge(xn_done, NT + t + 1)
                act.dma_start(xn_rows[t * P:(t + 1) * P, :], xn[:, t, :]).then_inc(xn_out, 16)
            for n in range(2 * NT):
                act.wait_ge(tp_done, 2 * NT + n + 1)
                t, k0 = n // 2, 4 * (n % 2)
                nc.scalar.activation(r_t[:, k0:k0 + 4, t * P:(t + 1) * P],
                                     ps[:, n, :].rearrange("p (k c) -> p k c", k=4), ACT.Copy).then_inc(thi_done, 1)
            act.wait_ge(rex_in, 1)
            nc.scalar.activation(rt[:, 128:256], rt[:, 128:256], ACT.Exp).then_inc(rex_out, 1)
            act.wait_ge(gtp_done, 1)
            nc.scalar.activation(gt_t, ps[0:NE, 2, :], ACT.Copy).then_inc(gte_done, 1)
            act.wait_ge(s_bup, 32)
            act.wait_ge(flag_done, 1)
            nc.scalar.activation(bup[:, :], bup_raw, ACT.Copy).then_inc(buphi_done, 1)

            def run(b):
                s0 = b * NE
                base = C0 + b * RUN
                blocks = RUN // RAW

                def split(m, ring, turn):
                    s = ring % RAW
                    hi(base + m, (s, ring % SPLIT), raw_slot(s), 16 * (raw_before(s) + 1 + blocks * b + turn))

                def one(e, par, j=None):
                    def sp_chunk(part):
                        if isinstance(e, int):
                            m = part if e == 0 else PER * e - DNC + part
                            split(m, m % 24, m // RAW)
                        else:
                            m0 = PER * par - DNC + part
                            split(PER * e - DNC + part, m0 % 24, 3 * j + m0 // RAW)

                    first = isinstance(e, int) and e == 0
                    lastp = isinstance(e, int) and e == NE - 1
                    for u in range(UPC):
                        sp_chunk(u)
                        if u == 2 and not (isinstance(e, int) and e < 2):
                            y_copy(e - 2, par)
                        if u == 5 and not first:
                            a_hi_copy(e - 1)
                    if first:
                        if not lastp:
                            x_hi_copy(e + 1, 1 - par)
                        sig(e)
                        return
                    sp_chunk(UPC)
                    if not lastp:
                        x_hi_copy(e + 1, 1 - par)
                    for d in range(1, DNC):
                        sp_chunk(UPC + d)
                    sig(e)

                def y_copy(e, par):
                    act.wait_ge(used, dn_chunk(base, e, DNC - 1, isinstance(e, int) and e == NE - 1) + 1)
                    if not (isinstance(e, int) and e == 0 and isinstance(b, int)):
                        act.wait_ge(y_out, 16 * (s0 + e))
                    nc.scalar.activation(y_sb[:, :], ps[:, 4:6, :].rearrange("p a n -> p (a n)"), ACT.Copy).then_inc(y_done, 1)

                def a_hi_copy(e):
                    for q in range(2):
                        act.wait_ge(at_done, (s0 + e) * 2 + q + 1)
                        nc.scalar.activation(a_hi[:, 4 * q:4 * q + 4, :],
                                             ps[:, 6 + q, :].rearrange("p (k c) -> p k c", k=4), ACT.Copy).then_inc(athi_done, 1)

                def x_hi_copy(e, par):
                    for q in range(2):
                        act.wait_ge(xt_done, (s0 + e) * 2 + q + 1)
                        nc.scalar.activation(x_hi[:, par, 4 * q:4 * q + 4, :],
                                             ps[:, 6 + q, :].rearrange("p (k c) -> p k c", k=4), ACT.Copy).then_inc(xhi_done, 1)

                def sig(e):
                    act.wait_ge(gl_done, s0 + e + 1)
                    nc.scalar.activation(s_sb[:, :], g_sb[:, :], ACT.Sigmoid, scale=ALPHA).then_inc(sig_done, 1)

                x_hi_copy(0, 0)
                one(0, 0)
                one(1, 1)
                with act.Fori(1, NE // 2 - 1) as j:
                    one(2 * j, 0, j)
                    one(2 * j + 1, 1, j)
                one(NE - 2, 0)
                one(NE - 1, 1)
                for d in range(DNC):
                    m = PER * NE - DNC + d
                    split(m, m % 24, m // RAW)
                    if d == 2:
                        y_copy(NE - 2, 0)
                        a_hi_copy(NE - 1)
                y_copy(NE - 1, 1)

            more = passes(act, run)

            base = act.snap(more * ((NB - 1) * RUN))
            turns = act.snap(more * (16 * (NB - 1) * RUN // RAW))

            def hi3(i):
                s = i % RAW
                hi(base + (C0 + RUN + i), (s, i % SPLIT), raw_slot(s), turns + 16 * (raw_before(s) + 1 + RUN // RAW))

            hi3(0)
            for n in range(2):
                act.wait_ge(ptp_done, n + 1)
                nc.scalar.activation(p_hi[:, n, :], ps[:, 6 + n, :], ACT.Copy).then_inc(pphi_done, 1)
            hi3(1)
            hi3(2)
            for t in range(NT):
                act.wait_ge(used, base + (C0 + RUN + 1))
                nc.scalar.activation(pp[:, t, :], ps[:, 2 * t:2 * t + 2, :].rearrange("p a n -> p (a n)"), ACT.Copy).then_inc(ppg_done, 1)
            for t in range(NT):
                act.wait_ge(yadd_done, TOP * (t + 1))
                nc.scalar.activation(sq3[:, :], h[:, t, :], ACT.Square, accum_out=st[:, t:t + 1]).then_inc(sq_done, 1)
                act.wait_ge(sq_done, 2 * NT + t + 1)
            root(3)
            for n in range(2 * NT):
                act.wait_ge(tp_done, 4 * NT + n + 1)
                t, k0 = n // 2, 4 * (n % 2)
                nc.scalar.activation(z_hi[:, k0:k0 + 4, t * P:(t + 1) * P],
                                     ps[:, n, :].rearrange("p (k c) -> p k c", k=4), ACT.Copy).then_inc(thi_done, 1)
            hi3(3)
            hi3(4)
            for t in range(NT):
                act.wait_ge(used, base + (C0 + RUN + TAIL))
                if t >= 2:
                    act.wait_ge(h3_done, t - 1)
                nc.scalar.activation(xn3[:, t % 2, :], ps[:, 2 * t:2 * t + 2, :].rearrange("p a n -> p (a n)"),
                                     ACT.Sigmoid).then_inc(ppg_done, 1)
            for t in range(NT):
                act.wait_ge(h3_done, t + 1)
                nc.scalar.activation(sq3[:, :], h[:, t, :], ACT.Square, accum_out=st[:, t:t + 1]).then_inc(sq_done, 1)
                act.wait_ge(sq_done, 3 * NT + t + 1)
            root(4)

        @block.vector
        def _(dve):
            seq = [0]

            def link(ins):
                seq[0] += 1
                ins.then_inc(dve_seq, 1)
                dve.wait_ge(dve_seq, seq[0])

            V = nc.vector

            def rms(n):
                dve.wait_ge(sq_done, n * NT)
                link(V.tensor_scalar(st[:, 12:16], st[:, 0:4], 1.0 / D, EPS, ALU.mult, ALU.add))
                V.reciprocal(st[:, 4:8], st[:, 12:16]).then_inc(ms_done, 1)
                dve.wait_ge(rs_done, n)

            def lo(c, slot, raw, width=2048):
                dve.wait_ge(hi_done, c + 1)
                V.tensor_tensor(w_lo[:, slot, 0:width], raw[:, 0:width], w_hi[:, slot, 0:width].bitcast(F32),
                                ALU.subtract).then_inc(lo_done, 1)

            def lo1(c):
                lo(c, c % SPLIT, raw_a[:, c % RAW1, :], 2 * ATT_W if c < 4 else 2048)

            dve.wait_ge(s_gbc, 16)
            rms(1)
            for t in range(NT):
                V.scalar_tensor_tensor(out=xn[:, t, :], in0=h[:, t, :], scalar=st[:, 8 + t:9 + t], in1=gbc[:, :],
                                       op0=ALU.mult, op1=ALU.mult).then_inc(xn_done, 1)
            for c in range(3):
                lo1(c)
            for n in range(2 * NT):
                dve.wait_ge(thi_done, n + 1)
                t, k0 = n // 2, 4 * (n % 2)
                V.tensor_tensor(t_lo[:, k0:k0 + 4, t * P:(t + 1) * P], ps[:, n, :].rearrange("p (k c) -> p k c", k=4),
                                t_hi[:, k0:k0 + 4, t * P:(t + 1) * P].bitcast(F32), ALU.subtract).then_inc(tlo_done, 1)
            for c in range(3, 6):
                lo1(c)

            def rope(bank, col, heads, at):
                src = ps[:, bank:bank + NT, col:col + heads * HD].rearrange("p t (g d) -> p t g d", d=HD)
                dst = roped[:, :, at:at + heads * HD].rearrange("p t (g d) -> p t g d", d=HD)
                m1 = tmp[:, 0, 0:NT * heads * 32].rearrange("p (t g d) -> p t g d", t=NT, d=32)
                m2 = tmp[:, 1, 0:NT * heads * 32].rearrange("p (t g d) -> p t g d", t=NT, d=32)
                cs, sn = (cst[:, o:o + 128].rearrange("p (t d) -> p t d", t=NT).unsqueeze(2).broadcast_to([P, NT, heads, 32])
                          for o in (COS, SIN))
                x1, x2 = src[:, :, :, 0:32], src[:, :, :, 32:64]
                V.tensor_tensor(m1, x1, cs, ALU.mult)
                link(V.tensor_tensor(m2, x2, sn, ALU.mult))
                link(V.tensor_tensor(dst[:, :, :, 0:32], m1, m2, ALU.subtract))
                V.tensor_tensor(m1, x2, cs, ALU.mult)
                link(V.tensor_tensor(m2, x1, sn, ALU.mult))
                link(V.tensor_tensor(dst[:, :, :, 32:64], m1, m2, ALU.add))

            def twice(at):
                return V.tensor_copy(roped[:, :, at + HD:at + 2 * HD], roped[:, :, at:at + HD])

            dve.wait_ge(used, 4)
            dve.wait_ge(tp_done, 2 * NT)
            dve.wait_ge(uv_done, 2)
            rope(4, 128, 5, 640)
            rope(4, 0, 1, 512)
            twice(512).then_inc(rope_done, 1)
            twice(896).then_inc(rope_done, 1)
            rope(0, 0, 8, 0)
            V.engine_nop().then_inc(rope_done, 1)
            lo1(6)
            OFF = (None, 0, 256, 640)
            dve.wait_ge(uv_done, 2)
            for t in range(1, NT):
                kk = (t + 1) * P
                wk = work[:, OFF[t]:OFF[t] + kk]
                for hh in range(IDX_HEADS):
                    dve.wait_ge(rl_done, (t - 1) * IDX_HEADS + hh + 1)
                    if hh == 0:
                        i = V.tensor_scalar(wk, rl[:, 0, 0:kk], uv[:, t, 64:65], None, ALU.mult)
                    else:
                        i = V.scalar_tensor_tensor(out=wk, in0=rl[:, hh, 0:kk], scalar=uv[:, t, 64 + hh:65 + hh], in1=wk,
                                                   op0=ALU.mult, op1=ALU.add)
                    i.then_inc(cc_done, 1)
                    dve.wait_ge(cc_done, (t - 1) * IDX_HEADS + hh + 1)
                link(V.tensor_tensor(work[:, OFF[t] + kk - P:OFF[t] + kk], work[:, OFF[t] + kk - P:OFF[t] + kk],
                                     cst[:, CAUS:CAUS + P], ALU.add))
            for t in range(1, NT):
                kk = (t + 1) * P
                wk = work[:, OFF[t]:OFF[t] + kk]
                for r in range(N_SEL // 8):
                    link(V.max(m8[:, :], wk))
                    link(V.match_replace(wk, m8[:, :], wk, TAKEN))
                link(V.tensor_scalar(wk, wk, 0.5 * (TAKEN + NEG), NEG, ALU.is_gt, ALU.mult))
                if t == 1:
                    lo1(7)
            dve.wait_ge(rtp_done, 8)
            V.memset(hpad[:, :, 0:30], 0.0)
            dve.wait_ge(used, 8)
            for j in range(NJ):
                dve.wait_ge(glu_sig, j + 1)
                V.scalar_tensor_tensor(out=hpad[:, j, 30:30 + SEQ], in0=ps[:, j, :], scalar=par[:, 124 + j:125 + j],
                                       in1=sg[:, j, :], op0=ALU.add, op1=ALU.mult).then_inc(glu_done, 1)
            for c in (8, 9, 10):
                lo1(c)
            dve.wait_ge(glu_done, NJ)

            def tap(k):
                for j in range(NJ):
                    w = par[:, k * NJ + j:k * NJ + j + 1]
                    if k == 0:
                        i = V.tensor_scalar(acc[:, j, :], hpad[:, j, 0:SEQ], w, par[:, 132 + j:133 + j], ALU.mult, ALU.add)
                    else:
                        dve.wait_ge(tap_done, (k - 1) * NJ + j + 1)
                        i = V.scalar_tensor_tensor(out=acc[:, j, :], in0=hpad[:, j, k:k + SEQ], scalar=w, in1=acc[:, j, :],
                                                   op0=ALU.mult, op1=ALU.add)
                    i.then_inc(tap_done, 1)

            def attn_norm(t):
                dve.wait_ge(pv_done, HEADS * (t + 1))
                dve.wait_ge(exp_done, HEADS * (t + 1))
                link(V.reciprocal(mx[:, 2, t * HEADS:(t + 1) * HEADS], mx[:, 2, t * HEADS:(t + 1) * HEADS]))
                if t >= 1:
                    dve.wait_ge(atp_done, t)
                V.tensor_tensor(attn[:, :].rearrange("p (h d) -> p h d", d=HD),
                                ps[:, 4 + t % 2, :].rearrange("p (h d) -> p h d", d=HD),
                                mx[:, 2, t * HEADS:(t + 1) * HEADS].unsqueeze(2).broadcast_to([P, HEADS, HD]),
                                ALU.mult).then_inc(an_done, 1)

            def attn_lo(t):
                dve.wait_ge(ahi_done, t + 1)
                V.tensor_tensor(t_lo[:, 0:4, t * P:(t + 1) * P], ps[:, 6, :].rearrange("p (k c) -> p k c", k=4),
                                t_hi[:, 0:4, t * P:(t + 1) * P].bitcast(F32), ALU.subtract).then_inc(alo_done, 1)

            for n in range(32):
                t, kk = n // HEADS, (n // HEADS + 1) * P
                dve.wait_ge(s_done, n + 1)
                if n >= 2:
                    dve.wait_ge(exp_done, n - 1)
                mask = cst[:, CAUS:CAUS + P] if t == 0 else work[:, OFF[t]:OFF[t] + kk]
                link(V.tensor_tensor_reduce(lg[:, n % 2, 0:kk], ps[:, n % 2, 0:kk], mask, 1.0, TAKEN, ALU.add, ALU.max,
                                            mx[:, 0, n:n + 1]))
                V.tensor_scalar(mx[:, 1, n:n + 1], mx[:, 0, n:n + 1], -(HD ** -0.5), None, ALU.mult).then_inc(lg_done, 1)
                if n < TAPS:
                    tap(n)
                if n % HEADS == 3 and n > HEADS:
                    attn_norm(t - 1)
                if n % HEADS == 6 and n > HEADS:
                    attn_lo(t - 1)
            attn_norm(NT - 1)
            attn_lo(NT - 1)
            dve.wait_ge(cs_done, 1)
            for j in range(NJ):
                V.scalar_tensor_tensor(out=acc[:, j, :], in0=ps[:, 7, :], scalar=-1.0 / CONV_W, in1=acc[:, j, :],
                                       op0=ALU.mult, op1=ALU.add).then_inc(cv_done, 1)
            dve.wait_ge(cs_done, 2)
            dve.wait_ge(exp_done, 32)
            link(V.tensor_scalar(lg[:, 0, :], ps[:, 6, :], 1.0 / CONV_W, EPS, ALU.mult, ALU.add))
            V.reciprocal(lg[:, 1, :], lg[:, 0, :]).then_inc(cr_done, 1)
            dve.wait_ge(crs_done, 1)
            dve.wait_ge(csq_done, NJ)
            for j in range(NJ):
                link(V.tensor_tensor(acc[:, j, :], acc[:, j, :], lg[:, 0, :], ALU.mult))
                V.tensor_scalar(acc[:, j, :], acc[:, j, :], par[:, 136 + j:137 + j], par[:, 140 + j:141 + j],
                                ALU.mult, ALU.add).then_inc(cz_done, 1)
            for j in range(NJ):
                dve.wait_ge(csg_done, j + 1)
                V.tensor_tensor(acc[:, j, :], acc[:, j, :], sg[:, j, :], ALU.mult).then_inc(mix_done, 1)
            for j in range(NJ):
                dve.wait_ge(mhi_done, j + 1)
                V.tensor_tensor(t_lo[:, NJ + j, :], acc[:, j, :], t_hi[:, NJ + j, :].bitcast(F32),
                                ALU.subtract).then_inc(mlo_done, 1)
            lo1(11)
            dve.wait_ge(used, C0)
            for t in range(NT):
                V.tensor_tensor(h[:, t, :], h[:, t, :], ps[:, 2 * t:2 * t + 2, :].rearrange("p a n -> p (a n)"),
                                ALU.add).then_inc(h1_done, 1)
            dve.wait_ge(s_gbc, 32)
            rms(2)
            for t in range(NT):
                V.scalar_tensor_tensor(out=xn[:, t, :], in0=h[:, t, :], scalar=st[:, 8 + t:9 + t], in1=gbc[:, :],
                                       op0=ALU.mult, op1=ALU.mult).then_inc(xn_done, 1)

            def r4(o):
                return rt[:, o:o + 128].rearrange("p (t e) -> p t e", t=NT)

            lgt, ex, gt, eq, cum, chosen = (r4(o) for o in (0, 128, 256, 384, 512, 640))
            top = work[:, 0:32].rearrange("p (t e) -> p t e", t=NT)
            cnt, tot = work[:, 32:36], work[:, 36:40]
            bc = lambda v: v.broadcast_to([P, NT, NE])
            dve.wait_ge(rlog_done, 1)
            dve.wait_ge(s_wr, 32)
            link(V.tensor_tensor(lgt, ps[:, 0, 0:128].rearrange("p (t e) -> p t e", t=NT),
                                 brt[:, :].unsqueeze(1).broadcast_to([P, NT, NE]), ALU.add))
            for t in range(NT):
                i = V.max(top[:, t, :], lgt[:, t, :])
            link(i)
            V.tensor_tensor(ex, lgt, bc(top[:, :, 0:1]), ALU.subtract).then_inc(rex_in, 1)
            V.tensor_tensor(eq, lgt, bc(top[:, :, 3:4]), ALU.is_equal)
            link(V.tensor_tensor(gt, lgt, bc(top[:, :, 3:4]), ALU.is_gt))
            V.reduce_sum(cnt, gt, AX.X)
            for t in range(NT):
                i = V.tensor_tensor_scan(cum[:, t, :], ones[:, 0:NE], eq[:, t, :], 0.0, ALU.mult, ALU.add)
            link(i)
            link(V.tensor_tensor(cum, cum, bc(cnt.unsqueeze(2)), ALU.add))
            link(V.scalar_tensor_tensor(out=eq, in0=cum, scalar=float(TOP), in1=eq, op0=ALU.is_le, op1=ALU.mult))
            link(V.tensor_tensor(chosen, gt, eq, ALU.add))
            V.engine_nop().then_inc(sel_done, 1)
            for t in range(NT):
                i = V.tensor_tensor_scan(cum[:, t, :], ones[:, 0:NE], chosen[:, t, :], 0.0, ALU.mult, ALU.add)
            dve.wait_ge(rex_out, 1)
            link(V.tensor_tensor(ex, ex, chosen, ALU.mult))
            link(V.reduce_sum(tot, ex, AX.X))
            link(V.reciprocal(tot, tot))
            V.tensor_tensor(info[:, :, :, 2], ex, bc(tot.unsqueeze(2)), ALU.mult)
            V.tensor_scalar(gt, cum, float(SEQ), -float(SEQ) - SKIP, ALU.mult, ALU.add)
            V.tensor_copy(info[:, :, :, 0], bc(cst[:, TOK:TOK + NT].unsqueeze(2)))
            link(V.tensor_tensor(ex, ex, bc(tot.unsqueeze(2)), ALU.mult))
            V.tensor_tensor(info[:, :, :, 1], gt, bc(cst[:, TOK:TOK + NT].unsqueeze(2)), ALU.add).then_inc(gates_done, 1)
            dve.wait_ge(pos_done, 1)
            V.tensor_scalar(work[:, 64:96], ps[:, 1, 128:160], 1.0, None, ALU.mult)
            link(V.scalar_tensor_tensor(out=cum, in0=ps[:, 1, 0:128].rearrange("p (t e) -> p t e", t=NT), scalar=1.0,
                                        in1=chosen, op0=ALU.add, op1=ALU.mult))
            for b in range(NB):
                i = V.tensor_scalar(pos[:, :, b * NE:(b + 1) * NE], cum, -1.0 - BLK * b, None, ALU.add)
            i.then_inc(tab_done, 1)
            link(V.reduce_max(work[:, 96:97], work[:, 64:96], AX.X))
            V.tensor_scalar(flag[:, :], work[:, 96:97], BLK + 0.5, None, ALU.is_gt).then_inc(flag_done, 1)
            dve.wait_ge(buphi_done, 1)
            V.tensor_tensor(bup[32:64, :], bup_raw[32:64, :], bup[32:64, :].bitcast(F32), ALU.subtract).then_inc(bup_done, 1)
            dve.wait_ge(bd_done, 1)
            for t in range(NT):
                i = V.tensor_tensor(h[:, t, :], h[:, t, :], ps[:, 2 * t:2 * t + 2, :].rearrange("p a n -> p (a n)"), ALU.add)
            i.then_inc(up_free, 1)

            def run(b):
                s0 = b * NE
                base = C0 + b * RUN

                def indices(e, par):
                    dve.wait_ge(list_done, s0 + e + 1)
                    if not (isinstance(e, int) and e == 0 and isinstance(b, int)):
                        dve.wait_ge(xg_in, 16 * (s0 + e))
                    V.tensor_copy(gidx[:, :], ps[:, 6, 0:1])
                    V.tensor_scalar(didx[:, par, :], ps[:, 6, 1:2], SKIP, None, ALU.add)
                    V.tensor_copy(gate[:, par, :], ps[:, 6, 2:3]).then_inc(idx_done, 1)

                def x_lo_copy(e, par):
                    for q in range(2):
                        dve.wait_ge(xhi_done, (s0 + e) * 2 + q + 1)
                        V.tensor_tensor(x_lo[:, par, 4 * q:4 * q + 4, :], ps[:, 6 + q, :].rearrange("p (k c) -> p k c", k=4),
                                        x_hi[:, par, 4 * q:4 * q + 4, :].bitcast(F32), ALU.subtract).then_inc(xlo_done, 1)

                def a_lo_copy(e):
                    for q in range(2):
                        dve.wait_ge(athi_done, (s0 + e) * 2 + q + 1)
                        V.tensor_tensor(a_lo[:, 4 * q:4 * q + 4, :], ps[:, 6 + q, :].rearrange("p (k c) -> p k c", k=4),
                                        a_hi[:, 4 * q:4 * q + 4, :].bitcast(F32), ALU.subtract).then_inc(atlo_done, 1)

                def glu_in(e, par, first=False):
                    dve.wait_ge(used, up_chunk(base, e, UPC, first))
                    V.tensor_scalar(g_sb[:, :], ps[:, 0:2, :].rearrange("p a n -> p (a n)"), LIMIT, None,
                                    ALU.min).then_inc(gl_done, 1)
                    V.tensor_scalar(l_sb[:, :], ps[:, 2:4, :].rearrange("p a n -> p (a n)"), -LIMIT, LIMIT,
                                    ALU.max, ALU.min).then_inc(up_free, 1)
                    if isinstance(e, int) and e < 2 and isinstance(b, int):
                        pass
                    else:
                        dve.wait_ge(y_out, 16 * (s0 + e - 1))
                    V.tensor_copy(dsti[:, par, :], didx[:, par, :])
                    dve.wait_ge(up_free, s0 + e + 2)
                    V.scalar_tensor_tensor(out=l_sb[:, :], in0=l_sb[:, :], scalar=1.0, in1=g_sb[:, :],
                                           op0=ALU.add, op1=ALU.mult).then_inc(gl2_done, 1)

                def glu_out(e, par):
                    dve.wait_ge(sig_done, s0 + e + 1)
                    dve.wait_ge(gl2_done, s0 + e + 1)
                    V.scalar_tensor_tensor(out=l_sb[:, :], in0=l_sb[:, :], scalar=gate[:, par, :], in1=s_sb[:, :],
                                           op0=ALU.mult, op1=ALU.mult).then_inc(act_done, 1)

                def one(e, par):
                    first = isinstance(e, int) and e == 0
                    lastp = isinstance(e, int) and e == NE - 1

                    def split(part):
                        ring = part if first else (PER * par - DNC + part) % 24
                        lo(base + part if first else base + PER * e - DNC + part, ring % SPLIT, raw_slot(ring))

                    for u in range(UPC):
                        split(u)
                        if u == 3 and not lastp:
                            indices(e + 1, 1 - par)
                        if u == 5 and not first:
                            a_lo_copy(e - 1)
                    if first:
                        x_lo_copy(e + 1, 1 - par)
                        glu_in(e, par, True)
                        glu_out(e, par)
                        return
                    split(UPC)
                    if not lastp:
                        x_lo_copy(e + 1, 1 - par)
                    split(UPC + 1)
                    split(UPC + 2)
                    glu_in(e, par)
                    split(UPC + 3)
                    glu_out(e, par)

                indices(0, 0)
                x_lo_copy(0, 0)
                steps(dve, one)
                for d in range(DNC):
                    m = PER * NE - DNC + d
                    lo(base + m, m % SPLIT, raw_slot(m))
                    if d == 2:
                        a_lo_copy(NE - 1)

            more = passes(dve, run)

            base = dve.snap(more * ((NB - 1) * RUN))

            def lo3(i):
                lo(base + (C0 + RUN + i), i % SPLIT, raw_slot(i))

            lo3(0)
            for n in range(2):
                dve.wait_ge(pphi_done, n + 1)
                V.tensor_tensor(p_lo[:, n, :], ps[:, 6 + n, :], p_hi[:, n, :].bitcast(F32), ALU.subtract).then_inc(pplo_done, 1)
            lo3(1)
            lo3(2)
            for n in range(NT * TOP):
                dve.wait_ge(s_yb[n % 2], 16 * (n // 2 + 1))
                if n % TOP:
                    dve.wait_ge(yadd_done, n)
                V.tensor_tensor(h[:, n // TOP, :], h[:, n // TOP, :], yb[:, n % 2, :], ALU.add).then_inc(yadd_done, 1)
            dve.wait_ge(s_gbc, 48)
            rms(3)
            for t in range(NT):
                if t >= 2:
                    dve.wait_ge(tp_done, 4 * NT + 2 * (t - 1))
                V.scalar_tensor_tensor(out=xn3[:, t % 2, :], in0=h[:, t, :], scalar=st[:, 8 + t:9 + t], in1=gbc[:, :],
                                       op0=ALU.mult, op1=ALU.mult).then_inc(xn_done, 1)
            for n in range(2 * NT):
                dve.wait_ge(thi_done, 4 * NT + n + 1)
                t, k0 = n // 2, 4 * (n % 2)
                V.tensor_tensor(z_lo[:, k0:k0 + 4, t * P:(t + 1) * P], ps[:, n, :].rearrange("p (k c) -> p k c", k=4),
                                z_hi[:, k0:k0 + 4, t * P:(t + 1) * P].bitcast(F32), ALU.subtract).then_inc(tlo_done, 1)
            lo3(3)
            lo3(4)
            for t in range(NT):
                dve.wait_ge(ppg_done, NT + t + 1)
                link(V.tensor_tensor(pp[:, t, :], pp[:, t, :], xn3[:, t % 2, :], ALU.mult))
                V.tensor_tensor(h[:, t, :], h[:, t, :], pp[:, t, :], ALU.add).then_inc(h3_done, 1)
            dve.wait_ge(s_gbc, 64)
            rms(4)
            for t in range(NT):
                if t >= 2:
                    dve.wait_ge(s_out[t % 2], 16 * (t // 2))
                V.scalar_tensor_tensor(out=xn3[:, t % 2, :], in0=h[:, t, :], scalar=st[:, 8 + t:9 + t], in1=gbc[:, :],
                                       op0=ALU.mult, op1=ALU.mult).then_inc(fin_done, 1)

        @block.tensor
        def _(pe):
            mm = nc.tensor.matmul

            def three(outs, l_hi, l_lo, r_hi, r_lo, start, stop):
                for o, r in zip(outs, r_hi):
                    mm(o, l_hi, r, start=start, stop=False)
                for o, r in zip(outs, r_lo):
                    mm(o, l_hi, r, start=False, stop=False)
                for o, r in zip(outs, r_hi):
                    i = mm(o, l_lo, r, start=False, stop=stop)
                return i

            def transposes(src, t):
                for k in range(NK):
                    i = nc.tensor.transpose(ps[:, 2 * t + k // 4, (k % 4) * P:(k % 4 + 1) * P],
                                            src[:, k * P:(k + 1) * P], ident)
                    if k % 4 == 3:
                        i.then_inc(tp_done, 1)

            pe.wait_ge(s_cst, 16)
            for t in range(NT):
                pe.wait_ge(xn_done, t + 1)
                transposes(xn[:, t, :], t)
            pe.wait_ge(s_stage, 16 * 5)
            pe.wait_ge(tlo_done, 1)
            nc.tensor.transpose(ps[:, 0, 0:124], stage[0:124, :], cst[0:124, IDENT:IDENT + 124])
            nc.tensor.transpose(ps[:, 0, 128:148], stage2[:, :], cst[0:20, IDENT:IDENT + 20]).then_inc(par_tp, 1)
            pe.wait_ge(tlo_done, 2 * NT)
            pe.wait_ge(par_in, 2)
            for c in range(4):
                pe.wait_ge(lo_done, c + 1)
                for a in range(2):
                    k, s, o = 2 * c + a, c % SPLIT, a * ATT_W
                    for t in range(NT):
                        tt = slice(t * P, (t + 1) * P)
                        i = three([ps[:, t, :], ps[:, 4 + t, 0:REST_W]], t_hi[:, k, tt], t_lo[:, k, tt],
                                  [w_hi[:, s, o:o + 512], w_hi[:, s, o + 512:o + ATT_W]],
                                  [w_lo[:, s, o:o + 512], w_lo[:, s, o + 512:o + ATT_W]], k == 0, k == NK - 1)
                i.then_inc(used, 1)
            pe.wait_ge(uv_done, 2)
            for n, bl in enumerate((4, 5, 6, 7, 0, 1, 2, 3)):
                pe.wait_ge(rope_done, 2 if n < 4 else 3)
                bank = (n + 4) % 8
                for t in range(NT):
                    i = nc.tensor.transpose(ps[:, bank, t * P:(t + 1) * P], roped[:, t, bl * P:(bl + 1) * P], ident)
                i.then_inc(rtp_done, 1)
            for t in range(1, NT):
                for hh in range(IDX_HEADS):
                    half = slice(64 * (hh % 2), 64 * (hh % 2) + 64)
                    pe.wait_ge(rt_done, 4)
                    if t > 1:
                        pe.wait_ge(rl_done, (t - 2) * IDX_HEADS + hh + 1)
                    mm(ps[:, 4 + hh, 0:(t + 1) * P], r_t[half, 5 + hh // 2, t * P:(t + 1) * P],
                       r_t[half, 7, 0:(t + 1) * P], start=True, stop=True).then_inc(si_done, 1)
            pe.wait_ge(rt_done, 8)
            pe.wait_ge(rl_done, 3 * IDX_HEADS)
            for c in range(4, 8):
                pe.wait_ge(lo_done, c + 1)
                for a in range(2):
                    k, s = 2 * (c - 4) + a, c % SPLIT
                    for j in range(8):
                        o = a * 1024 + j * P
                        i = three([ps[:, j, :]], w_hi[:, s, o:o + P], w_lo[:, s, o:o + P],
                                  [t_hi[:, k, :]], [t_lo[:, k, :]], k == 0, k == NK - 1)
                i.then_inc(used, 1)

            def scores(n):
                t, hh = n // HEADS, n % HEADS
                half = slice(64 * (hh % 2), 64 * (hh % 2) + 64)
                if n >= 2:
                    pe.wait_ge(lg_done, n - 1)
                mm(ps[:, n % 2, 0:(t + 1) * P], r_t[half, hh // 2, t * P:(t + 1) * P], r_t[half, 4, 0:(t + 1) * P],
                   start=True, stop=True).then_inc(s_done, 1)

            def probs_transposed(n):
                pe.wait_ge(exp_done, n + 1)
                if n >= 2:
                    pe.wait_ge(pte_done, n - 1)
                for kb in range(n // HEADS + 1):
                    i = nc.tensor.transpose(ps[:, 2 + n % 2, kb * P:(kb + 1) * P], probs[:, n % 2, kb * P:(kb + 1) * P], ident)
                i.then_inc(pt_done, 1)

            def values(n):
                t, hh = n // HEADS, n % HEADS
                pe.wait_ge(pte_done, n + 1)
                if hh == 0 and t >= 2:
                    pe.wait_ge(an_done, t - 1)
                for kb in range(t + 1):
                    i = mm(ps[:, 4 + t % 2, hh * HD:(hh + 1) * HD], probs_t[:, n % 2, kb * P:(kb + 1) * P], uv[:, kb, 0:HD],
                           start=(kb == 0), stop=(kb == t))
                i.then_inc(pv_done, 1)

            def attn_transposed(t):
                pe.wait_ge(an_done, t + 1)
                if t >= 1:
                    pe.wait_ge(alo_done, t)
                for k in range(4):
                    i = nc.tensor.transpose(ps[:, 6, k * P:(k + 1) * P], attn[:, k * P:(k + 1) * P], ident)
                i.then_inc(atp_done, 1)

            pe.wait_ge(glu_done, NJ)
            for n in range(32):
                scores(n)
                if n >= 1:
                    probs_transposed(n - 1)
                if n >= 2:
                    values(n - 2)
                if n % HEADS == 4 and n > HEADS:
                    attn_transposed(n // HEADS - 1)
            probs_transposed(31)
            values(30)
            values(31)
            attn_transposed(NT - 1)
            pe.wait_ge(tap_done, TAPS * NJ)
            for j in range(NJ):
                i = mm(ps[:, 7, :], ones, acc[:, j, :], start=(j == 0), stop=(j == NJ - 1))
            i.then_inc(cs_done, 1)
            pe.wait_ge(alo_done, NT)
            for j in range(NJ):
                pe.wait_ge(csq_done, j + 1)
                i = mm(ps[:, 6, :], ones, sg[:, j, :], start=(j == 0), stop=(j == NJ - 1))
            i.then_inc(cs_done, 1)
            pe.wait_ge(cr_done, 1)
            pe.wait_ge(ahi_done, NT)
            for c in range(8, 12):
                pe.wait_ge(lo_done, c + 1)
                for a in range(2):
                    k, s = 2 * (c - 8) + a, c % SPLIT
                    if k >= NJ:
                        pe.wait_ge(mlo_done, k - NJ + 1)
                    for t in range(NT):
                        tt = slice(t * P, (t + 1) * P)
                        o = a * 1024
                        i = three([ps[:, 2 * t, :], ps[:, 2 * t + 1, :]], t_hi[:, k, tt], t_lo[:, k, tt],
                                  [w_hi[:, s, o:o + 512], w_hi[:, s, o + 512:o + 1024]],
                                  [w_lo[:, s, o:o + 512], w_lo[:, s, o + 512:o + 1024]], k == 0, k == NK - 1)
                i.then_inc(used, 1)
            for t in range(NT):
                pe.wait_ge(xn_done, NT + t + 1)
                transposes(xn[:, t, :], t)
            pe.wait_ge(thi_done, 4 * NT)
            pe.wait_ge(s_wr, 32)
            for t in range(NT):
                for k in range(NK):
                    i = mm(ps[:, 0, t * NE:(t + 1) * NE], r_t[:, k, t * P:(t + 1) * P], wr[:, k, :],
                           start=(k == 0), stop=(k == NK - 1))
            i.then_inc(rlog_done, 1)
            pe.wait_ge(sel_done, 1)
            chosen = rt[:, 640:768].rearrange("p (t e) -> p t e", t=NT)
            for t in range(NT):
                for u in range(t + 1):
                    mm(ps[:, 1, t * NE:(t + 1) * NE], cst[:, TRI:TRI + P] if u == t else ones, chosen[:, u, :],
                       start=(u == 0), stop=(u == t))
            for u in range(NT):
                i = mm(ps[:, 1, 128:160], ones, chosen[:, u, :], start=(u == 0), stop=(u == NT - 1))
            i.then_inc(pos_done, 1)
            pe.wait_ge(gates_done, 1)
            for t in range(NT):
                i = nc.tensor.transpose(ps[0:NE, 2, t * P:(t + 1) * P], rt[:, 128 + t * NE:128 + (t + 1) * NE], ident)
            i.then_inc(gtp_done, 1)
            pe.wait_ge(gte_done, 1)
            pe.wait_ge(tab_done, 1)
            pe.wait_ge(s_bdn, 16)
            for t in range(NT):
                for q in range(2):
                    i = mm(ps[:, 2 * t + q, :], gt_t[:, t * P:(t + 1) * P], bdn[:, q * 512:(q + 1) * 512], start=True, stop=True)
            i.then_inc(bd_done, 1)

            def run(b):
                s0 = b * NE
                base = C0 + b * RUN

                def listing(e):
                    pe.wait_ge(oh_done, s0 + e + 1)
                    for t in range(NT):
                        i = mm(ps[:, 6, 0:3], onehot[:, t, :], info[:, t, bass.ds(e, 1), :].rearrange("p o c -> p (o c)"),
                               start=(t == 0), stop=(t == NT - 1))
                    i.then_inc(list_done, 1)

                def x_transposed(e):
                    pe.wait_ge(xg_in, 16 * (s0 + e + 1))
                    for k in range(NK):
                        i = nc.tensor.transpose(ps[:, 6 + k // 4, (k % 4) * P:(k % 4 + 1) * P], xg[:, k * P:(k + 1) * P], ident)
                        if k % 4 == 3:
                            i.then_inc(xt_done, 1)

                def a_transposed(e):
                    pe.wait_ge(act_done, s0 + e + 1)
                    for k in range(NK):
                        i = nc.tensor.transpose(ps[:, 6 + k // 4, (k % 4) * P:(k % 4 + 1) * P], l_sb[:, k * P:(k + 1) * P], ident)
                        if k % 4 == 3:
                            i.then_inc(at_done, 1)

                def up(e, par, u, c, ring):
                    pe.wait_ge(lo_done, c + 1)
                    s = ring % SPLIT
                    cols = [slice(n * 512, (n + 1) * 512) for n in range(4)]
                    three([ps[:, n, :] for n in range(4)], x_hi[:, par, u, :], x_lo[:, par, u, :],
                          [w_hi[:, s, n] for n in cols], [w_lo[:, s, n] for n in cols], False, u == UPC - 1).then_inc(used, 1)

                def down(d, c, ring):
                    pe.wait_ge(lo_done, c + 1)
                    s = ring % SPLIT
                    for a in range(2):
                        k = 2 * d + a
                        cols = [slice(a * 1024 + n * 512, a * 1024 + (n + 1) * 512) for n in range(2)]
                        i = three([ps[:, 4 + n, :] for n in range(2)], a_hi[:, k, :], a_lo[:, k, :],
                                  [w_hi[:, s, n] for n in cols], [w_lo[:, s, n] for n in cols], k == 0, k == NK - 1)
                    i.then_inc(used, 1)

                def downs(e, par, last=False):
                    pe.wait_ge(atlo_done, 2 * (s0 + e + 1))
                    if not (isinstance(e, int) and e == 0 and isinstance(b, int)):
                        pe.wait_ge(y_done, s0 + e)
                    for d in range(DNC):
                        down(d, dn_chunk(base, e, d, last), slot8(par, (0 if last else UPC) + d))

                def one(e, par):
                    first = isinstance(e, int) and e == 0
                    lastp = isinstance(e, int) and e == NE - 1
                    pe.wait_ge(up_free, s0 + e + 1)
                    pe.wait_ge(xlo_done, 2 * (s0 + e + 1))
                    pe.wait_ge(sel_in, s0 + e + 1)
                    for n in range(4):
                        mm(ps[:, n, :], sel[:, :], bup[:, n * 512:(n + 1) * 512], start=True, stop=False)
                    for u in range(UPC):
                        ring = slot8(par, u, first)
                        up(e, par, u, up_chunk(base, e, u, first), ring)
                        if u == 0 and not lastp:
                            listing(e + 1)
                        if u == 2 and not first:
                            if not lastp:
                                pe.wait_ge(idx_done, s0 + e + 2)
                            a_transposed(e - 1)
                        if u == 5 and not lastp:
                            if first:
                                pe.wait_ge(idx_done, s0 + e + 2)
                            else:
                                pe.wait_ge(atlo_done, 2 * (s0 + e))
                            x_transposed(e + 1)
                    if not first:
                        downs(e - 1, par)

                if isinstance(b, int):
                    pe.wait_ge(up_free, 1)
                    pe.wait_ge(bup_done, 1)
                else:
                    pe.wait_ge(atlo_done, 2 * s0)
                listing(0)
                pe.wait_ge(idx_done, s0 + 1)
                x_transposed(0)
                pe.wait_ge(xlo_done, 2 * (s0 + 1))
                steps(pe, one)
                a_transposed(NE - 1)
                downs(NE - 1, 0, True)

            more = passes(pe, run)

            base = pe.snap(more * ((NB - 1) * RUN))
            ybase = pe.snap(more * ((NB - 1) * NE))
            pe.wait_ge(s_p, 16)
            pe.wait_ge(atlo_done, ybase * 2 + 2 * NE)
            for n in range(2):
                for t in range(NT):
                    i = nc.tensor.transpose(ps[:, 6 + n, t * P:(t + 1) * P], p_sb[:, t, n * P:(n + 1) * P], ident)
                i.then_inc(ptp_done, 1)
            pe.wait_ge(pplo_done, 2)
            pe.wait_ge(y_done, ybase + NE)
            pe.wait_ge(up_free, ybase + (NE + 1))

            def tail(i0, k, a, l_hi, l_lo, first, last):
                s = i0 % SPLIT
                for t in range(NT):
                    tt = slice(t * P, (t + 1) * P)
                    cols = [slice(a * 1024 + n * 512, a * 1024 + (n + 1) * 512) for n in range(2)]
                    i = three([ps[:, 2 * t + n, :] for n in range(2)], l_hi[:, k, tt], l_lo[:, k, tt],
                              [w_hi[:, s, n] for n in cols], [w_lo[:, s, n] for n in cols], first, last)
                return i

            pe.wait_ge(lo_done, base + (C0 + RUN + 1))
            tail(0, 0, 0, p_hi, p_lo, True, False)
            i = tail(0, 1, 1, p_hi, p_lo, False, True)
            i.then_inc(used, 1)
            pe.wait_ge(ppg_done, NT)
            for t in range(NT):
                pe.wait_ge(xn_done, 2 * NT + t + 1)
                transposes(xn3[:, t % 2, :], t)
            pe.wait_ge(tlo_done, 4 * NT)
            for c in range(4):
                pe.wait_ge(lo_done, base + (C0 + RUN + 2 + c))
                for a in range(2):
                    i = tail(1 + c, 2 * c + a, a, z_hi, z_lo, c + a == 0, c == 3 and a == 1)
                i.then_inc(used, 1)


def constants():
    c = np.zeros((P, NCONST), np.float32)
    r = np.arange(P)
    c[:, IDENT:IDENT + P] = np.eye(P)
    c[:, TRI:TRI + P] = r[:, None] < r[None, :]
    c[:, ONES:ONES + P] = 1.0
    c[:, IOTA:IOTA + P] = r[None, :]
    c[:, CAUS:CAUS + P] = np.where(r[None, :] <= r[:, None], 0.0, NEG)
    inv = np.float32(10000.0) ** (-np.arange(0, HD, 2, dtype=np.float32) / np.float32(HD))
    ang = (np.arange(SEQ, dtype=np.float32)[:, None] * inv[None, :]).astype(np.float32)
    for o, f in ((COS, np.cos), (SIN, np.sin)):
        c[:, o:o + P] = f(ang).reshape(NT, P, 32).transpose(1, 0, 2).reshape(P, NT * 32)
    c[:, TOK:TOK + NT] = np.arange(NT)[None, :] * P + r[:, None]
    c[0:64, EYE:EYE + NE] = (np.arange(64)[:, None] % NE) == np.arange(NE)[None, :]
    return c


_INS = ["x", "p", "w_in", "w_out", "g_mix", "g_ffn", "conv_glu_b", "conv_dw_w", "conv_dw_b", "conv_ln_g", "conv_ln_b",
        "w_router", "b_router", "w_up", "b_up", "w_down", "b_down", "w_ple_proj", "w_ple_gate", "g_ple", "g_final"]


def kernel(**inputs):
    import numpy as _np
    import concourse.bacc as _bacc
    from concourse import mybir as _mybir
    from concourse.bass_utils import run_bass_kernel_spmd as _run

    nc = _bacc.Bacc("TRN2", target_bir_lowering=False, num_devices=1)
    arrays, args = {}, []
    for name in _INS + ["constants"]:
        a = constants() if name == "constants" else _np.ascontiguousarray(inputs[name])
        arrays[f"in_{name}_dram"] = a
        args.append(nc.dram_tensor(f"in_{name}_dram", a.shape, _mybir.dt.from_np(a.dtype), kind="ExternalInput").ap())
    args.append(nc.dram_tensor("out_0_dram", (1, SEQ, D), _mybir.dt.float32, kind="ExternalOutput").ap())
    build(nc, *args)
    r = _run(nc, [arrays], core_ids=[0])
    return r.results[0]["out_0_dram"]
```

```python
from contextlib import ExitStack

import concourse.bass as bass
from concourse import mybir
import numpy as np

F32 = mybir.dt.float32
F32R = mybir.dt.float32r
I32 = mybir.dt.int32
ALU = mybir.AluOpType
ACT = mybir.ActivationFunctionType
AX = mybir.AxisListType

P = 128
SEQ, D = 512, 1024
NT = SEQ // P
NK = D // P
PLE = 256
HEADS, HD = 8, 64
IDX_HEADS = 4
CONV_W, TAPS = 512, 31
NJ = CONV_W // P
IN_W = HEADS * HD + 2 * HD + IDX_HEADS * HD + HD + IDX_HEADS + 2 * CONV_W
ATT_W = IN_W - 2 * CONV_W
REST_W = ATT_W - 512
N_SEL = min(256, SEQ // 4)
NE, TOP = 32, 4
LIMIT, ALPHA, EPS = 7.0, 1.702, 1e-6
NEG = -1e30
TAKEN = -3e38
SKIP = 4096.0
BLK = 128
NB = SEQ // BLK
RAW, SPLIT = 8, 3
RAW1 = 4
C0 = 12
UPC, DNC = 8, 4
PER = UPC + DNC
RUN = PER * NE
TAIL = 5

BIAS = (0, 2, 4, 0)
PROJ = (0, 2, 6, 4)

IDENT, TRI, ONES, IOTA, CAUS, COS, SIN, TOK, EYE = 0, 128, 256, 384, 512, 640, 768, 896, 900
NCONST = 932


def build(nc, x, p, w_in, w_out, g_mix, g_ffn, conv_glu_b, conv_dw_w, conv_dw_b, conv_ln_g, conv_ln_b,
          w_router, b_router, w_up, b_up, w_down, b_down, w_ple_proj, w_ple_gate, g_ple, g_final,
          consts, out):
    ctx = ExitStack()
    with ctx:
        def sb(name, shape, dt=F32, stack=ctx):
            return stack.enter_context(nc.sbuf_tensor(name, shape, dt))

        def sem(name):
            return ctx.enter_context(nc.semaphore(name))

        xn_rows = nc.dram_tensor("xn_rows", [SEQ, D], F32, kind="Internal").ap()
        y_rows = nc.dram_tensor("y_rows", [TOP * SEQ, D], F32, kind="Internal").ap()

        cst = sb("cst", [P, NCONST])
        par = sb("par", [P, 144])
        gbc = sb("gbc", [P, D])
        h = sb("h", [P, NT, D])
        raw_a = sb("raw_a", [P, RAW1, 2048])
        w_hi = sb("w_hi", [P, SPLIT, 2048], F32R)
        w_lo = sb("w_lo", [P, SPLIT, 2048], F32R)
        pos = sb("pos", [P, NT, NB * NE])
        info = sb("info", [P, NT, NE, 3])
        st = sb("st", [P, 2, 16])
        flag = sb("flag", [P, 1], I32)
        brt = sb("brt", [P, NE])

        with ExitStack() as s1:
            t_hi = sb("t_hi", [P, NK, SEQ], F32R, s1)
            t_lo = sb("t_lo", [P, NK, SEQ], F32R, s1)
            reg_a = sb("reg_a", [P, 4224], F32, s1)
            r_t = sb("r_t", [P, NK, SEQ], F32, s1)
            tmp = sb("tmp", [P, 2, 1024], F32, s1)
            rl = sb("rl", [P, 4, 512], F32, s1)
            lg = sb("lg", [P, 2, 512], F32, s1)
            uv = sb("uv", [P, NT, 68], F32, s1)
            work = sb("work", [P, 1152], F32, s1)
            mx = sb("mx", [P, 3, 32], F32, s1)
            m8 = sb("m8", [P, 8], F32, s1)
            attn = sb("attn", [P, 512], F32, s1)
            stage = sb("stage", [P, 128], F32, s1)
            stage2 = sb("stage2", [20, 128], F32, s1)
            wr = sb("wr", [P, NK, NE], F32, s1)
            tri_r = sb("tri_r", [P, 2 * P], F32R, s1)
            chosen_r = sb("chosen_r", [P, NT, NE], F32R, s1)
        xn = reg_a[:, 0:4096].rearrange("p (t n) -> p t n", t=NT)
        roped = xn
        PADW = 30 + SEQ
        hpad = reg_a[:, 0:4 * PADW].rearrange("p (j n) -> p j n", j=NJ)
        acc = reg_a[:, 4 * PADW:4 * PADW + 2048].rearrange("p (j n) -> p j n", j=NJ)
        sg = tmp[:, :, :].rearrange("p a (b n) -> p (a b) n", b=2)
        probs, probs_t = rl[:, 0:2, :], rl[:, 2:4, :]

        bup_raw = r_t[0:64, 0:4, :].rearrange("p a n -> p (a n)")
        bdn_raw = r_t[0:64, 4:6, :].rearrange("p a n -> p (a n)")
        with ExitStack() as s1b:
            sb("under_tmp", [P, 4 * 4096 + 128], F32, s1b)
            bdn_hi = sb("bdn_hi", [64, D], F32R, s1b)
            bdn_lo = sb("bdn_lo", [64, D], F32R, s1b)
            sb("under_attn", [P, 2048 + 1024 + 272 + 1152 + 96 + 8], F32, s1b)
            gt_t = sb("gt_t", [64, SEQ], F32R, s1b)

        with ExitStack() as s2:
            raw_b = sb("raw_b", [P, RAW - RAW1, 2048], F32, s2)
            g_sb = sb("g_sb", [P, D], F32, s2)
            l_sb = sb("l_sb", [P, D], F32, s2)
            s_sb = sb("s_sb", [P, D], F32, s2)
            a_hi = sb("a_hi", [P, NK, P], F32R, s2)
            sb("under_r_t", [P, 128], F32, s2)
            onehot = sb("onehot", [P, NT, BLK], F32, s2)
            xg = sb("xg", [P, D], F32, s2)
            x_hi = sb("x_hi", [P, 2, NK, P], F32R, s2)
            x_lo = sb("x_lo", [P, 2, NK, P], F32R, s2)
            sb("under_rl", [P, 512], F32, s2)
            bup = sb("bup", [64, 2048], F32R, s2)
            y_sb = sb("y_sb", [P, D], F32, s2)
            a_lo = sb("a_lo", [P, NK, P], F32R, s2)
            sel = sb("sel", [64, P], F32R, s2)
            pos_e = sb("pos_e", [P, NT], F32, s2)
            gidx = sb("gidx", [P, 1], I32, s2)
            didx = sb("didx", [P, 2, 1], I32, s2)
            dsti = sb("dsti", [P, 2, 1], I32, s2)
            gate = sb("gate", [P, 2, 1], F32, s2)
        with ExitStack() as s3:
            s3.enter_context(nc.sbuf_tensor("hold", [P, RAW - RAW1, 2048], F32))
            xn3 = sb("xn3", [P, 2, D], F32, s3)
            sgm = sb("sgm", [P, D], F32, s3)
            sq3 = sb("sq3", [P, D], F32, s3)
            sb("under_p_sb", [P, 128], F32, s3)
            p_sb = sb("p_sb", [P, NT, PLE], F32, s3)
            sb("under_p_hi", [P, 512], F32, s3)
            p_hi = sb("p_hi", [P, PLE // P, SEQ], F32R, s3)
            p_lo = sb("p_lo", [P, PLE // P, SEQ], F32R, s3)
            w4_hi = sb("w4_hi", [P, 2048], F32R, s3)
            w4_lo = sb("w4_lo", [P, 2048], F32R, s3)
            z_hi = sb("z_hi", [P, 2, NK, P], F32R, s3)
            z_lo = sb("z_lo", [P, 2, NK, P], F32R, s3)
        pp = raw_b[:, 1:3, :].rearrange("p a (b n) -> p (a b) n", b=2)
        yb = [raw_b[:, 3, :].rearrange("p (a n) -> p a n", a=2), raw_a[:, 0, :].rearrange("p (a n) -> p a n", a=2)]
        gfin = raw_a[:, 1, 0:D]
        rt = lg[:, :, :].rearrange("p a n -> p (a n)")

        ps = ctx.enter_context(nc.psum_tensor("ps", [P, 8, 512], F32))

        ident = cst[:, IDENT:IDENT + P]
        ones = cst[:, ONES:ONES + P]

        s_cst, s_stage, s_gbc, s_p = sem("s_cst"), sem("s_stage"), sem("s_gbc"), sem("s_p")
        s_x = [sem(f"s_x{t}") for t in range(NT)]
        s_wr, s_bup, s_bdn = sem("s_wr"), sem("s_bup"), sem("s_bdn")
        raw_in = [sem(f"raw_in{i}") for i in range(RAW)]
        hi_done, lo_done, used = sem("hi_done"), sem("lo_done"), sem("used")
        dve_seq = sem("dve_seq")
        sq_done, ms_done, rs_done, xn_done = sem("sq_done"), sem("ms_done"), sem("rs_done"), sem("xn_done")
        tp_done, thi_done, tlo_done = sem("tp_done"), sem("thi_done"), sem("tlo_done")
        par_tp, par_in = sem("par_tp"), sem("par_in")
        uv_done, rope_done, rtp_done, rt_done = sem("uv_done"), sem("rope_done"), sem("rtp_done"), sem("rt_done")
        si_done, rl_done = sem("si_done"), sem("rl_done")
        glu_sig, glu_done = sem("glu_sig"), sem("glu_done")
        s_done, lg_done, exp_done, pt_done, pte_done, pv_done = (sem(n) for n in (
            "s_done", "lg_done", "exp_done", "pt_done", "pte_done", "pv_done"))
        an_done, atp_done, ahi_done, alo_done = sem("an_done"), sem("atp_done"), sem("ahi_done"), sem("alo_done")
        tap_done, cs_done, cc_done, csq_done, cv_done = (sem(n) for n in (
            "tap_done", "cs_done", "cc_done", "csq_done", "cv_done"))
        cr_done, crs_done, cz_done, csg_done, mix_done, mhi_done, mlo_done = (sem(n) for n in (
            "cr_done", "crs_done", "cz_done", "csg_done", "mix_done", "mhi_done", "mlo_done"))
        h1_done, out_done = sem("h1_done"), sem("out_done")
        xn_out = sem("xn_out")
        rlog_done, rex_in, rex_out, sel_done, pos_done, gates_done = (sem(n) for n in (
            "rlog_done", "rex_in", "rex_out", "sel_done", "pos_done", "gates_done"))
        gtp_done, gthi_done, gtlo_done = sem("gtp_done"), sem("gthi_done"), sem("gtlo_done")
        bdhi_done, bdlo_done, bd_done, bias_done = (sem(n) for n in ("bdhi_done", "bdlo_done", "bd_done", "bias_done"))
        xg_clear, tri_done = sem("xg_clear"), sem("tri_done")
        tab_done, flag_done = sem("tab_done"), sem("flag_done")
        buphi_done, bup_done = sem("buphi_done"), sem("bup_done")
        pos_e_in, pool_waits = sem("pos_e_in"), sem("pool_waits")
        oh_done, list_done, idx_done, xg_in, sel_in = (sem(n) for n in (
            "oh_done", "list_done", "idx_done", "xg_in", "sel_in"))
        xt_done, xhi_done, xlo_done = sem("xt_done"), sem("xhi_done"), sem("xlo_done")
        up_free, gl_done, gl2_done, sig_done, act_done = (sem(n) for n in (
            "up_free", "gl_done", "gl2_done", "sig_done", "act_done"))
        at_done, athi_done, atlo_done = sem("at_done"), sem("athi_done"), sem("atlo_done")
        dn_free, y_done, y_out = sem("dn_free"), sem("y_done"), sem("y_out")
        s_yb = [sem("s_yb0"), sem("s_yb1")]
        yadd_done, ptp_done, pphi_done, pplo_done = (sem(n) for n in ("yadd_done", "ptp_done", "pphi_done", "pplo_done"))
        s_gfin, w4hi_done, w4lo_done, proj_done, pp_done = (sem(n) for n in (
            "s_gfin", "w4hi_done", "w4lo_done", "proj_done", "pp_done"))
        sq3_done, ms3_done, rs3_done, xn3_done, zt_done, zhi_done, zlo_done, gated, sg3_done = (sem(n) for n in (
            "sq3_done", "ms3_done", "rs3_done", "xn3_done", "zt_done", "zhi_done", "zlo_done", "gated", "sg3_done"))
        h3_done, fin_done = sem("h3_done"), sem("fin_done")
        s_out = [sem("s_out0"), sem("s_out1")]

        block = ctx.enter_context(nc.Block())

        def up_chunk(base, e, u, first=False):
            return base + u if first else base - DNC + PER * e + u

        def dn_chunk(base, e, d, last=False):
            return base - DNC + PER * (e + 1) + (0 if last else UPC) + d

        def slot8(e_par, part, first=False, last=False):
            if first:
                return part
            return (-DNC + PER * e_par + part) % (2 * PER)

        def raw_slot(s):
            s %= RAW
            return raw_a[:, s, :] if s < RAW1 else raw_b[:, s - RAW1, :]

        def raw_before(s):
            return C0 // RAW1 if s % RAW < RAW1 else 0

        def steps(eng, one):
            one(0, 0)
            one(1, 1)
            with eng.Fori(1, NE // 2 - 1) as j:
                one(2 * j, 0)
                one(2 * j + 1, 1)
            one(NE - 2, 0)
            one(NE - 1, 1)

        def passes(eng, run):
            run(0)
            eng.wait_ge(flag_done, 1)
            more = eng.value_load(flag[0:1, 0:1], min_val=0, max_val=1)
            with eng.If(more > 0):
                with eng.Fori(1, NB) as b:
                    run(b)
            return more

        @block.sync
        def _(sp):
            sp.dma_start(cst[:, :], consts).then_inc(s_cst, 16)
            for t in range(NT):
                sp.dma_start(h[:, t, :], x[0, t * P:(t + 1) * P, :]).then_inc(s_x[t], 16)
            sp.dma_start(gbc[:, :], g_mix[0:1, :].broadcast_to([P, D])).then_inc(s_gbc, 16)
            sp.dma_start(stage[0:TAPS * NJ, :], conv_dw_w[0].rearrange("k (j c) -> (k j) c", j=NJ)).then_inc(s_stage, 16)
            for n, (v, r0, r) in enumerate(((conv_glu_b, 0, 8), (conv_dw_b, 8, 4), (conv_ln_g, 12, 4), (conv_ln_b, 16, 4))):
                sp.dma_start(stage2[r0:r0 + r, :], v[0].rearrange("(j c) -> j c", j=r)).then_inc(s_stage, 16)

            def load1(c):
                s = c % RAW1
                if c < 4:
                    dst = raw_a[:, s, 0:2 * ATT_W].rearrange("p (a n) -> p a n", a=2)
                    src = w_in[0, c * 256:(c + 1) * 256, 0:ATT_W]
                elif c < 8:
                    dst = raw_a[:, s, :].rearrange("p (a n) -> p a n", a=2)
                    src = w_in[0, (c - 4) * 256:(c - 3) * 256, ATT_W:IN_W]
                else:
                    dst = raw_a[:, s, :].rearrange("p (a n) -> p a n", a=2)
                    src = w_out[0, (c - 8) * 256:(c - 7) * 256, :]
                if c >= RAW1:
                    sp.wait_ge(lo_done, c - RAW1 + 1)
                sp.dma_start(dst, src.rearrange("(a p) n -> p a n", p=P)).then_inc(raw_in[s], 16)

            for c in range(C0):
                load1(c)
                if c == 3:
                    sp.dma_start(wr[:, :, :], w_router[0].rearrange("(k p) n -> p k n", p=P)).then_inc(s_wr, 16)
                    sp.dma_start(brt[:, :], b_router[0:1, :].broadcast_to([P, NE])).then_inc(s_wr, 16)
                    sp.wait_ge(xn_done, NT)
                    sp.dma_start(gbc[:, :], g_ffn[0:1, :].broadcast_to([P, D])).then_inc(s_gbc, 16)

            for t in range(NT):
                sp.wait_ge(xn_done, NT + t + 1)
                sp.dma_start(xn_rows[t * P:(t + 1) * P, :], xn[:, t, :]).then_inc(xn_out, 16)
            w_up_c = w_up[0].rearrange("e (k p) n -> (e k) p n", p=P)
            w_dn_c = w_down[0].rearrange("e (c a p) n -> (e c) p a n", p=P, a=2)

            def run(b):
                base = C0 + b * RUN

                def ups(e, par, first=False):
                    for u in range(UPC):
                        ring = slot8(par, u, first)
                        if first and isinstance(b, int):
                            if u < RAW1:
                                sp.wait_ge(lo_done, C0 - RAW1 + u + 1)
                            elif u == RAW1:
                                sp.wait_ge(used, C0)
                        else:
                            sp.wait_ge(lo_done, up_chunk(base, e, u, first) - RAW + 1)
                        sp.dma_start(raw_slot(ring), w_up_c[bass.ds(e * UPC + u, 1), :, :].rearrange("o p n -> (o p) n")
                                     ).then_inc(raw_in[ring % RAW], 16)

                def downs(e, par, last=False):
                    for d in range(DNC):
                        ring = slot8(par, (0 if last else UPC) + d)
                        sp.wait_ge(lo_done, dn_chunk(base, e, d, last) - RAW + 1)
                        sp.dma_start(raw_slot(ring).rearrange("p (a n) -> p a n", a=2),
                                     w_dn_c[bass.ds(e * DNC + d, 1), :, :, :].rearrange("o p a n -> (o p) a n")
                                     ).then_inc(raw_in[ring % RAW], 16)

                def one(e, par):
                    first = isinstance(e, int) and e == 0
                    ups(e, par, first)
                    if not first:
                        downs(e - 1, par)

                steps(sp, one)
                downs(NE - 1, 0, True)

            more = passes(sp, run)
            base = sp.snap(more * ((NB - 1) * RUN))
            ybase = sp.snap(more * ((NB - 1) * NE))
            sp.dma_start(gbc[:, :], g_ple[0:1, :].broadcast_to([P, D])).then_inc(s_gbc, 16)
            sp.wait_ge(xt_done, ybase * 2 + 2 * NE)
            sp.dma_start(p_sb[:, :, :], p[0, 0].rearrange("(t p) n -> p t n", p=P)).then_inc(s_p, 16)
            for i in range(TAIL):
                sp.wait_ge(lo_done, base + (C0 + RUN + i - RAW + 1))
                src = w_ple_proj[0] if i == 0 else w_ple_gate[0, (i - 1) * 256:i * 256, :]
                sp.dma_start(raw_slot(i).rearrange("p (a n) -> p a n", a=2),
                             src.rearrange("(a p) n -> p a n", p=P)).then_inc(raw_in[i % RAW], 16)
            sp.wait_ge(lo_done, base + (C0 + RUN + 2))
            sp.dma_start(gfin, g_final.rearrange("(a n) -> a n", a=1).broadcast_to([P, D])).then_inc(s_gfin, 16)
            sp.wait_ge(y_out, ybase * 16 + 16 * NE)
            yv = y_rows.rearrange("(g k t p) n -> t g p k n", g=2, k=2, p=P)
            for n in range(NT * 2):
                if n >= 2:
                    sp.wait_ge(yadd_done, 2 * (n - 1))
                sp.dma_start(yb[n % 2], yv[n // 2, n % 2]).then_inc(s_yb[n % 2], 16)
            for t in range(NT):
                sp.wait_ge(fin_done, t + 1)
                sp.dma_start(out[0, t * P:(t + 1) * P, :], pp[:, t, :]).then_inc(s_out[t % 2], 16)
            for q in s_out:
                sp.wait_ge(q, 16 * NT // 2)

        @block.gpsimd
        def _(pool):
            def wait(s, value):
                pool.wait_ge(s, value)
                pool.sem_inc(pool_waits)

            def run(b):
                s0 = b * NE
                base = C0 + b * RUN

                def prep(e, par, first=False):
                    if isinstance(e, int) and e == 0 and isinstance(b, int):
                        wait(rlog_done, 1)
                        nc.gpsimd.memset(xg[:, :], 0.0).then_inc(xg_clear, 1)
                        wait(tab_done, 1)
                    else:
                        wait(list_done, s0 + e)
                    nc.gpsimd.tensor_copy(pos_e[:, :], pos[:, :, bass.ds(s0 + e, 1)].rearrange("p t o -> p (t o)")).then_inc(pos_e_in, 1)
                    wait(pos_e_in, s0 + e + 1)
                    for t in range(NT):
                        i = nc.gpsimd.tensor_scalar(onehot[:, t, :], cst[:, IOTA:IOTA + P], pos_e[:, t:t + 1], None, ALU.is_equal)
                    i.then_inc(oh_done, 1)

                def gather(e, par):
                    wait(idx_done, s0 + e + 1)
                    if not (isinstance(e, int) and e == 0 and isinstance(b, int)):
                        wait(xt_done, (s0 + e) * 2)
                    else:
                        wait(xn_out, 16 * NT)
                        wait(xg_clear, 1)
                    pool.indirect_dma_start(xg[:, :], None, xn_rows, bass.IndirectOffsetOnAxis(ap=gidx[:, 0:1], axis=0),
                                            bounds_check=SEQ - 1, oob_is_err=False).then_inc(xg_in, 16)

                def selector(e, par):
                    if not (isinstance(e, int) and e == 0 and isinstance(b, int)):
                        c = base if isinstance(e, int) and e == 0 else up_chunk(base, e - 1, UPC, isinstance(e, int) and e == 1)
                        wait(used, c)
                    nc.gpsimd.tensor_copy(sel[:, :], cst[0:64, bass.ds(EYE + e, 1)].broadcast_to([64, P])).then_inc(sel_in, 1)

                def scatter(e, par):
                    wait(y_done, s0 + e + 1)
                    pool.indirect_dma_start(y_rows, bass.IndirectOffsetOnAxis(ap=dsti[:, par, 0:1], axis=0), y_sb[:, :], None,
                                            bounds_check=TOP * SEQ - 1, oob_is_err=False).then_inc(y_out, 16)

                def one(e, par):
                    if not (isinstance(e, int) and e == NE - 1):
                        prep(e + 1, 1 - par)
                    if not (isinstance(e, int) and e < 2):
                        scatter(e - 2, par)
                    if not (isinstance(e, int) and e == NE - 1):
                        gather(e + 1, 1 - par)
                        selector(e + 1, 1 - par)

                prep(0, 0)
                gather(0, 0)
                selector(0, 0)
                steps(pool, one)
                scatter(NE - 2, 0)
                scatter(NE - 1, 1)

            passes(pool, run)

        @block.scalar
        def _(act):
            def squares(src, n0):
                for t in range(NT):
                    if n0 == 0:
                        act.wait_ge(s_x[t], 16)
                    elif n0 == 1:
                        act.wait_ge(h1_done, t + 1)
                    junk = (rl[:, 0:2, :] if n0 == 0 else lg[:, :, :]).rearrange("p a n -> p (a n)")
                    if t:
                        act.wait_ge(sq_done, n0 * NT + t)
                    nc.scalar.activation(junk, src[:, t, :], ACT.Square, accum_out=st[:, 0, t:t + 1]).then_inc(sq_done, 1)
                    root(n0 * NT + t)

            def root(n):
                t = n % NT
                act.wait_ge(ms_done, n + 1)
                nc.scalar.activation(st[:, 0, 8 + t:9 + t], st[:, 0, 4 + t:5 + t], ACT.Sqrt).then_inc(rs_done, 1)

            def hi(c, slot, raw, count, width=2048, fresh=False):
                act.wait_ge(raw_in[slot[0]], count)
                if not fresh:
                    act.wait_ge(used, c - SPLIT + 1)
                nc.scalar.activation(w_hi[:, slot[1], 0:width], raw[:, 0:width], ACT.Copy).then_inc(hi_done, 1)

            def hi1(c):
                hi(c, (c % RAW1, c % SPLIT), raw_a[:, c % RAW1, :], 16 * (c // RAW1 + 1),
                   2 * ATT_W if c < 4 else 2048, c < SPLIT)

            squares(h, 0)
            for c in range(3):
                hi1(c)
            for n in range(2 * NT):
                act.wait_ge(tp_done, n + 1)
                t, k0 = n // 2, 4 * (n % 2)
                nc.scalar.activation(t_hi[:, k0:k0 + 4, t * P:(t + 1) * P],
                                     ps[:, n, :].rearrange("p (k c) -> p k c", k=4), ACT.Copy).then_inc(thi_done, 1)
            act.wait_ge(par_tp, 1)
            nc.scalar.activation(par[:, 0:124], ps[:, 0, 0:124], ACT.Copy).then_inc(par_in, 1)
            nc.scalar.activation(par[:, 124:144], ps[:, 0, 128:148], ACT.Copy).then_inc(par_in, 1)
            for c in range(3, 6):
                hi1(c)
            act.wait_ge(used, 4)
            nc.scalar.activation(uv[:, :, 0:64], ps[:, 4:8, 64:128], ACT.Copy).then_inc(uv_done, 1)
            nc.scalar.activation(uv[:, :, 64:68], ps[:, 4:8, 448:452], ACT.Copy).then_inc(uv_done, 1)
            hi1(6)
            for n, bl in enumerate((4, 5, 6, 7, 0, 1, 2, 3)):
                act.wait_ge(rtp_done, n + 1)
                nc.scalar.activation(r_t[:, bl, :], ps[:, (n + 4) % 8, :], ACT.Copy).then_inc(rt_done, 1)
            for t in range(1, NT):
                for hh in range(IDX_HEADS):
                    n = (t - 1) * IDX_HEADS + hh
                    act.wait_ge(si_done, n + 1)
                    if t > 1:
                        act.wait_ge(cc_done, (t - 2) * IDX_HEADS + hh + 1)
                    nc.scalar.activation(rl[:, hh, 0:(t + 1) * P], ps[:, 4 + hh, 0:(t + 1) * P], ACT.Relu).then_inc(rl_done, 1)
            hi1(7)
            act.wait_ge(par_in, 2)
            for j in range(NJ):
                act.wait_ge(used, 8)
                nc.scalar.activation(sg[:, j, :], ps[:, 4 + j, :], ACT.Sigmoid, bias=par[:, 128 + j:129 + j]).then_inc(glu_sig, 1)
            for c in (8, 9, 10):
                hi1(c)

            def pt_copy(n):
                act.wait_ge(pt_done, n + 1)
                if n >= 2:
                    act.wait_ge(pv_done, n - 1)
                kk = (n // HEADS + 1) * P
                nc.scalar.activation(probs_t[:, n % 2, 0:kk], ps[:, 2 + n % 2, 0:kk], ACT.Copy).then_inc(pte_done, 1)

            def attn_hi(t):
                act.wait_ge(atp_done, t + 1)
                nc.scalar.activation(t_hi[:, 0:4, t * P:(t + 1) * P],
                                     ps[:, 6, :].rearrange("p (k c) -> p k c", k=4), ACT.Copy).then_inc(ahi_done, 1)

            for n in range(32):
                kk = (n // HEADS + 1) * P
                act.wait_ge(lg_done, n + 1)
                if n >= 2:
                    act.wait_ge(pt_done, n - 1)
                nc.scalar.activation(probs[:, n % 2, 0:kk], lg[:, n % 2, 0:kk], ACT.Exp, bias=mx[:, 1, n:n + 1],
                                     scale=HD ** -0.5, accum_out=mx[:, 2, n:n + 1]).then_inc(exp_done, 1)
                if n >= 1:
                    pt_copy(n - 1)
                if n % HEADS == 4 and n > HEADS:
                    attn_hi(n // HEADS - 1)
            pt_copy(31)
            attn_hi(NT - 1)
            act.wait_ge(s_done, 32)
            for q in range(2):
                act.dma_start(bup_raw[q * NE:(q + 1) * NE, :], b_up[0]).then_inc(s_bup, 16)
                act.dma_start(bdn_raw[q * NE:(q + 1) * NE, :], b_down[0]).then_inc(s_bdn, 16)
            for j in range(NJ):
                act.wait_ge(cv_done, j + 1)
                nc.scalar.activation(sg[:, j, :], acc[:, j, :], ACT.Square).then_inc(csq_done, 1)
            act.wait_ge(cr_done, 1)
            nc.scalar.activation(lg[:, 0, :], lg[:, 1, :], ACT.Sqrt).then_inc(crs_done, 1)
            for j in range(NJ):
                act.wait_ge(cz_done, j + 1)
                nc.scalar.activation(sg[:, j, :], acc[:, j, :], ACT.Sigmoid).then_inc(csg_done, 1)
            for j in range(NJ):
                act.wait_ge(mix_done, j + 1)
                nc.scalar.activation(t_hi[:, NJ + j, :], acc[:, j, :], ACT.Copy).then_inc(mhi_done, 1)
            hi1(11)
            nc.scalar.activation(tri_r[:, :], cst[:, TRI:TRI + 2 * P], ACT.Copy).then_inc(tri_done, 1)
            act.wait_ge(s_bup, 32)
            nc.scalar.activation(bup[:, :], bup_raw, ACT.Copy).then_inc(buphi_done, 1)
            act.wait_ge(s_bdn, 32)
            nc.scalar.activation(bdn_hi[:, :], bdn_raw, ACT.Copy).then_inc(bdhi_done, 1)
            squares(h, 1)
            act.wait_ge(bup_done, 1)
            act.wait_ge(bdlo_done, 1)
            for n in range(2 * NT):
                act.wait_ge(tp_done, 2 * NT + n + 1)
                t, k0 = n // 2, 4 * (n % 2)
                nc.scalar.activation(r_t[:, k0:k0 + 4, t * P:(t + 1) * P],
                                     ps[:, n, :].rearrange("p (k c) -> p k c", k=4), ACT.Copy).then_inc(thi_done, 1)
            act.wait_ge(rex_in, 1)
            nc.scalar.activation(rt[:, 128:256], rt[:, 128:256], ACT.Exp).then_inc(rex_out, 1)
            act.wait_ge(gtp_done, 1)
            nc.scalar.activation(gt_t[:, :], ps[0:64, 2, :], ACT.Copy).then_inc(gthi_done, 1)

            def run(b):
                s0 = b * NE
                base = C0 + b * RUN
                blocks = RUN // RAW

                def split(m, ring, turn):
                    s = ring % RAW
                    hi(base + m, (s, ring % SPLIT), raw_slot(s), 16 * (raw_before(s) + 1 + blocks * b + turn))

                def one(e, par, j=None):
                    def sp_chunk(part):
                        if isinstance(e, int):
                            m = part if e == 0 else PER * e - DNC + part
                            split(m, m % 24, m // RAW)
                        else:
                            m0 = PER * par - DNC + part
                            split(PER * e - DNC + part, m0 % 24, 3 * j + m0 // RAW)

                    first = isinstance(e, int) and e == 0
                    lastp = isinstance(e, int) and e == NE - 1
                    for u in range(UPC):
                        if not (first and u < SPLIT):
                            sp_chunk(u)
                        if u == 2 and not (isinstance(e, int) and e < 2):
                            y_copy(e - 2, par)
                        if u == 5 and not first:
                            a_hi_copy(e - 1)
                    if first:
                        if not lastp:
                            x_hi_copy(e + 1, 1 - par)
                        sig(e)
                        return
                    sp_chunk(UPC)
                    if not lastp:
                        x_hi_copy(e + 1, 1 - par)
                    for d in range(1, DNC):
                        sp_chunk(UPC + d)
                    sig(e)

                def y_copy(e, par):
                    act.wait_ge(used, dn_chunk(base, e, DNC - 1, isinstance(e, int) and e == NE - 1) + 1)
                    if not (isinstance(e, int) and e == 0 and isinstance(b, int)):
                        act.wait_ge(y_out, 16 * (s0 + e))
                    nc.scalar.activation(y_sb[:, :], ps[:, 4:6, :].rearrange("p a n -> p (a n)"), ACT.Copy).then_inc(y_done, 1)

                def a_hi_copy(e):
                    for q in range(2):
                        act.wait_ge(at_done, (s0 + e) * 2 + q + 1)
                        nc.scalar.activation(a_hi[:, 4 * q:4 * q + 4, :],
                                             ps[:, 6 + q, :].rearrange("p (k c) -> p k c", k=4), ACT.Copy).then_inc(athi_done, 1)

                def x_hi_copy(e, par):
                    for q in range(2):
                        act.wait_ge(xt_done, (s0 + e) * 2 + q + 1)
                        nc.scalar.activation(x_hi[:, par, 4 * q:4 * q + 4, :],
                                             ps[:, 6 + q, :].rearrange("p (k c) -> p k c", k=4), ACT.Copy).then_inc(xhi_done, 1)

                def sig(e):
                    act.wait_ge(gl_done, s0 + e + 1)
                    nc.scalar.activation(s_sb[:, :], g_sb[:, :], ACT.Sigmoid, scale=ALPHA).then_inc(sig_done, 1)

                for u in range(SPLIT):
                    split(u, u, 0)
                x_hi_copy(0, 0)
                one(0, 0)
                one(1, 1)
                with act.Fori(1, NE // 2 - 1) as j:
                    one(2 * j, 0, j)
                    one(2 * j + 1, 1, j)
                one(NE - 2, 0)
                one(NE - 1, 1)
                for d in range(DNC):
                    m = PER * NE - DNC + d
                    split(m, m % 24, m // RAW)
                    if d == 2:
                        y_copy(NE - 2, 0)
                        a_hi_copy(NE - 1)
                y_copy(NE - 1, 1)

            more = passes(act, run)

            base = act.snap(more * ((NB - 1) * RUN))
            turns = act.snap(more * (16 * (NB - 1) * RUN // RAW))

            def hi3(i):
                s = i % RAW
                hi(base + (C0 + RUN + i), (s, i % SPLIT), raw_slot(s), turns + 16 * (raw_before(s) + 1 + RUN // RAW))

            hi3(0)
            for n in range(2):
                act.wait_ge(ptp_done, n + 1)
                nc.scalar.activation(p_hi[:, n, :], ps[:, 6 + n, :], ACT.Copy).then_inc(pphi_done, 1)
            hi3(1)
            hi3(2)
            act.wait_ge(raw_in[4], turns + 16 * (raw_before(4) + 1 + RUN // RAW))
            nc.scalar.activation(w4_hi[:, :], raw_slot(4), ACT.Copy).then_inc(w4hi_done, 1)
            def proj_copy(t):
                if t < NT - 1:
                    act.wait_ge(proj_done, t + 1)
                else:
                    act.wait_ge(used, base + (C0 + RUN + 1))
                nc.scalar.activation(pp[:, t, :], ps[:, PROJ[t]:PROJ[t] + 2, :].rearrange("p a n -> p (a n)"), ACT.Copy).then_inc(pp_done, 1)

            def tile_norm(n, t, f):
                if n:
                    act.wait_ge(sq3_done, n)
                nc.scalar.activation(sq3[:, :], h[:, t, :], ACT.Square, accum_out=st[:, f, t:t + 1]).then_inc(sq3_done, 1)
                act.wait_ge(ms3_done, n + 1)
                nc.scalar.activation(st[:, f, 8 + t:9 + t], st[:, f, 4 + t:5 + t], ACT.Sqrt).then_inc(rs3_done, 1)

            def norm_in(n, t):
                act.wait_ge(yadd_done, TOP * (t + 1))
                tile_norm(n, t, 0)

            def norm_out(n, t):
                act.wait_ge(h3_done, t + 1)
                tile_norm(n, t, 1)

            def z_copy(t):
                if t >= 2:
                    act.wait_ge(gated, t - 1)
                for q in range(2):
                    act.wait_ge(zt_done, 2 * t + q + 1)
                    nc.scalar.activation(z_hi[:, t % 2, 4 * q:4 * q + 4, :],
                                         ps[:, 4 + 2 * (t % 2) + q, :].rearrange("p (k c) -> p k c", k=4), ACT.Copy).then_inc(zhi_done, 1)

            def sigmoid(t):
                act.wait_ge(gated, t + 1)
                if t:
                    act.wait_ge(h3_done, t)
                g0 = 2 * (t % 2)
                nc.scalar.activation(sgm[:, :], ps[:, g0:g0 + 2, :].rearrange("p a n -> p (a n)"), ACT.Sigmoid).then_inc(sg3_done, 1)

            for t in range(NT - 1):
                proj_copy(t)
            norm_in(0, 0)
            proj_copy(NT - 1)
            z_copy(0)
            hi3(3)
            norm_in(1, 1)
            z_copy(1)
            norm_in(2, 2)
            sigmoid(0)
            norm_out(3, 0)
            z_copy(2)
            norm_in(4, 3)
            sigmoid(1)
            norm_out(5, 1)
            z_copy(3)
            sigmoid(2)
            norm_out(6, 2)
            sigmoid(3)
            norm_out(7, 3)

        @block.vector
        def _(dve):
            seq = [0]

            def link(ins):
                seq[0] += 1
                ins.then_inc(dve_seq, 1)
                dve.wait_ge(dve_seq, seq[0])

            V = nc.vector

            def rms(n, t, f, sums, inverses, roots):
                dve.wait_ge(sums, n + 1)
                link(V.tensor_scalar(st[:, f, 12 + t:13 + t], st[:, f, t:t + 1], 1.0 / D, EPS, ALU.mult, ALU.add))
                V.reciprocal(st[:, f, 4 + t:5 + t], st[:, f, 12 + t:13 + t]).then_inc(inverses, 1)
                dve.wait_ge(roots, n + 1)

            def normed(dst, t, f, gain):
                return V.scalar_tensor_tensor(out=dst, in0=h[:, t, :], scalar=st[:, f, 8 + t:9 + t], in1=gain,
                                              op0=ALU.mult, op1=ALU.mult)

            def lo(c, slot, raw, width=2048):
                dve.wait_ge(hi_done, c + 1)
                V.tensor_tensor(w_lo[:, slot, 0:width], raw[:, 0:width], w_hi[:, slot, 0:width].bitcast(F32),
                                ALU.subtract).then_inc(lo_done, 1)

            def lo1(c):
                lo(c, c % SPLIT, raw_a[:, c % RAW1, :], 2 * ATT_W if c < 4 else 2048)

            dve.wait_ge(s_gbc, 16)
            for t in range(NT):
                rms(t, t, 0, sq_done, ms_done, rs_done)
                normed(xn[:, t, :], t, 0, gbc[:, :]).then_inc(xn_done, 1)
            for c in range(3):
                lo1(c)
            for n in range(2 * NT):
                dve.wait_ge(thi_done, n + 1)
                t, k0 = n // 2, 4 * (n % 2)
                V.tensor_tensor(t_lo[:, k0:k0 + 4, t * P:(t + 1) * P], ps[:, n, :].rearrange("p (k c) -> p k c", k=4),
                                t_hi[:, k0:k0 + 4, t * P:(t + 1) * P].bitcast(F32), ALU.subtract).then_inc(tlo_done, 1)
            for c in range(3, 6):
                lo1(c)

            def rope(bank, col, heads, at):
                src = ps[:, bank:bank + NT, col:col + heads * HD].rearrange("p t (g d) -> p t g d", d=HD)
                dst = roped[:, :, at:at + heads * HD].rearrange("p t (g d) -> p t g d", d=HD)
                m1 = tmp[:, 0, 0:NT * heads * 32].rearrange("p (t g d) -> p t g d", t=NT, d=32)
                m2 = tmp[:, 1, 0:NT * heads * 32].rearrange("p (t g d) -> p t g d", t=NT, d=32)
                cs, sn = (cst[:, o:o + 128].rearrange("p (t d) -> p t d", t=NT).unsqueeze(2).broadcast_to([P, NT, heads, 32])
                          for o in (COS, SIN))
                x1, x2 = src[:, :, :, 0:32], src[:, :, :, 32:64]
                V.tensor_tensor(m1, x1, cs, ALU.mult)
                link(V.tensor_tensor(m2, x2, sn, ALU.mult))
                link(V.tensor_tensor(dst[:, :, :, 0:32], m1, m2, ALU.subtract))
                V.tensor_tensor(m1, x2, cs, ALU.mult)
                link(V.tensor_tensor(m2, x1, sn, ALU.mult))
                link(V.tensor_tensor(dst[:, :, :, 32:64], m1, m2, ALU.add))

            def twice(at):
                return V.tensor_copy(roped[:, :, at + HD:at + 2 * HD], roped[:, :, at:at + HD])

            dve.wait_ge(used, 4)
            dve.wait_ge(tp_done, 2 * NT)
            dve.wait_ge(uv_done, 2)
            rope(4, 128, 5, 640)
            rope(4, 0, 1, 512)
            twice(512).then_inc(rope_done, 1)
            twice(896).then_inc(rope_done, 1)
            rope(0, 0, 8, 0)
            V.engine_nop().then_inc(rope_done, 1)
            lo1(6)
            OFF = (None, 0, 256, 640)
            dve.wait_ge(uv_done, 2)
            for t in range(1, NT):
                kk = (t + 1) * P
                wk = work[:, OFF[t]:OFF[t] + kk]
                for hh in range(IDX_HEADS):
                    dve.wait_ge(rl_done, (t - 1) * IDX_HEADS + hh + 1)
                    if hh == 0:
                        i = V.tensor_scalar(wk, rl[:, 0, 0:kk], uv[:, t, 64:65], None, ALU.mult)
                    else:
                        i = V.scalar_tensor_tensor(out=wk, in0=rl[:, hh, 0:kk], scalar=uv[:, t, 64 + hh:65 + hh], in1=wk,
                                                   op0=ALU.mult, op1=ALU.add)
                    i.then_inc(cc_done, 1)
                    dve.wait_ge(cc_done, (t - 1) * IDX_HEADS + hh + 1)
                link(V.tensor_tensor(work[:, OFF[t] + kk - P:OFF[t] + kk], work[:, OFF[t] + kk - P:OFF[t] + kk],
                                     cst[:, CAUS:CAUS + P], ALU.add))
            for t in range(1, NT):
                kk = (t + 1) * P
                wk = work[:, OFF[t]:OFF[t] + kk]
                for r in range(N_SEL // 8):
                    link(V.max(m8[:, :], wk))
                    link(V.match_replace(wk, m8[:, :], wk, TAKEN))
                link(V.tensor_scalar(wk, wk, 0.5 * (TAKEN + NEG), NEG, ALU.is_gt, ALU.mult))
                if t == 1:
                    lo1(7)
            dve.wait_ge(rtp_done, 8)
            V.memset(hpad[:, :, 0:30], 0.0)
            dve.wait_ge(used, 8)
            for j in range(NJ):
                dve.wait_ge(glu_sig, j + 1)
                V.scalar_tensor_tensor(out=hpad[:, j, 30:30 + SEQ], in0=ps[:, j, :], scalar=par[:, 124 + j:125 + j],
                                       in1=sg[:, j, :], op0=ALU.add, op1=ALU.mult).then_inc(glu_done, 1)
            for c in (8, 9, 10):
                lo1(c)
            dve.wait_ge(glu_done, NJ)

            def tap(k):
                for j in range(NJ):
                    w = par[:, k * NJ + j:k * NJ + j + 1]
                    if k == 0:
                        i = V.tensor_scalar(acc[:, j, :], hpad[:, j, 0:SEQ], w, par[:, 132 + j:133 + j], ALU.mult, ALU.add)
                    else:
                        dve.wait_ge(tap_done, (k - 1) * NJ + j + 1)
                        i = V.scalar_tensor_tensor(out=acc[:, j, :], in0=hpad[:, j, k:k + SEQ], scalar=w, in1=acc[:, j, :],
                                                   op0=ALU.mult, op1=ALU.add)
                    i.then_inc(tap_done, 1)

            def attn_norm(t):
                dve.wait_ge(pv_done, HEADS * (t + 1))
                dve.wait_ge(exp_done, HEADS * (t + 1))
                link(V.reciprocal(mx[:, 2, t * HEADS:(t + 1) * HEADS], mx[:, 2, t * HEADS:(t + 1) * HEADS]))
                if t >= 1:
                    dve.wait_ge(atp_done, t)
                V.tensor_tensor(attn[:, :].rearrange("p (h d) -> p h d", d=HD),
                                ps[:, 4 + t % 2, :].rearrange("p (h d) -> p h d", d=HD),
                                mx[:, 2, t * HEADS:(t + 1) * HEADS].unsqueeze(2).broadcast_to([P, HEADS, HD]),
                                ALU.mult).then_inc(an_done, 1)

            def attn_lo(t):
                dve.wait_ge(ahi_done, t + 1)
                V.tensor_tensor(t_lo[:, 0:4, t * P:(t + 1) * P], ps[:, 6, :].rearrange("p (k c) -> p k c", k=4),
                                t_hi[:, 0:4, t * P:(t + 1) * P].bitcast(F32), ALU.subtract).then_inc(alo_done, 1)

            for n in range(32):
                t, kk = n // HEADS, (n // HEADS + 1) * P
                dve.wait_ge(s_done, n + 1)
                if n >= 2:
                    dve.wait_ge(exp_done, n - 1)
                mask = cst[:, CAUS:CAUS + P] if t == 0 else work[:, OFF[t]:OFF[t] + kk]
                link(V.tensor_tensor_reduce(lg[:, n % 2, 0:kk], ps[:, n % 2, 0:kk], mask, 1.0, TAKEN, ALU.add, ALU.max,
                                            mx[:, 0, n:n + 1]))
                V.tensor_scalar(mx[:, 1, n:n + 1], mx[:, 0, n:n + 1], -(HD ** -0.5), None, ALU.mult).then_inc(lg_done, 1)
                if n < TAPS:
                    tap(n)
                if n % HEADS == 3 and n > HEADS:
                    attn_norm(t - 1)
                if n % HEADS == 6 and n > HEADS:
                    attn_lo(t - 1)
            attn_norm(NT - 1)
            attn_lo(NT - 1)
            dve.wait_ge(cs_done, 1)
            for j in range(NJ):
                V.scalar_tensor_tensor(out=acc[:, j, :], in0=ps[:, 7, :], scalar=-1.0 / CONV_W, in1=acc[:, j, :],
                                       op0=ALU.mult, op1=ALU.add).then_inc(cv_done, 1)
            dve.wait_ge(cs_done, 2)
            dve.wait_ge(exp_done, 32)
            link(V.tensor_scalar(lg[:, 0, :], ps[:, 6, :], 1.0 / CONV_W, EPS, ALU.mult, ALU.add))
            V.reciprocal(lg[:, 1, :], lg[:, 0, :]).then_inc(cr_done, 1)
            dve.wait_ge(crs_done, 1)
            dve.wait_ge(csq_done, NJ)
            for j in range(NJ):
                link(V.tensor_tensor(acc[:, j, :], acc[:, j, :], lg[:, 0, :], ALU.mult))
                V.tensor_scalar(acc[:, j, :], acc[:, j, :], par[:, 136 + j:137 + j], par[:, 140 + j:141 + j],
                                ALU.mult, ALU.add).then_inc(cz_done, 1)
            for j in range(NJ):
                dve.wait_ge(csg_done, j + 1)
                V.tensor_tensor(acc[:, j, :], acc[:, j, :], sg[:, j, :], ALU.mult).then_inc(mix_done, 1)
            for j in range(NJ):
                dve.wait_ge(mhi_done, j + 1)
                V.tensor_tensor(t_lo[:, NJ + j, :], acc[:, j, :], t_hi[:, NJ + j, :].bitcast(F32),
                                ALU.subtract).then_inc(mlo_done, 1)
            lo1(11)
            dve.wait_ge(buphi_done, 1)
            V.tensor_tensor(bup[32:64, :], bup_raw[32:64, :], bup[32:64, :].bitcast(F32), ALU.subtract).then_inc(bup_done, 1)
            dve.wait_ge(bdhi_done, 1)
            V.tensor_tensor(bdn_lo[:, :], bdn_raw, bdn_hi[:, :].bitcast(F32), ALU.subtract).then_inc(bdlo_done, 1)
            for t in range(NT + 1):
                if t < NT:
                    if t < NT - 1:
                        dve.wait_ge(out_done, t + 1)
                    else:
                        dve.wait_ge(used, C0)
                    V.tensor_tensor(h[:, t, :], h[:, t, :], ps[:, 2 * t:2 * t + 2, :].rearrange("p a n -> p (a n)"),
                                    ALU.add).then_inc(h1_done, 1)
                if t == 1:
                    dve.wait_ge(s_gbc, 32)
                if t >= 1:
                    rms(NT + t - 1, t - 1, 0, sq_done, ms_done, rs_done)
                    normed(xn[:, t - 1, :], t - 1, 0, gbc[:, :]).then_inc(xn_done, 1)

            def r4(o):
                return rt[:, o:o + 128].rearrange("p (t e) -> p t e", t=NT)

            lgt, ex, gt, eq, cum = (r4(o) for o in (0, 128, 256, 384, 512))
            chosen = chosen_r[:, :, :].bitcast(F32)
            twin = rt[:, 768:1024].rearrange("p (t a e) -> p t a e", t=NT, a=2)
            top = work[:, 0:32].rearrange("p (t e) -> p t e", t=NT)
            cnt, tot = work[:, 32:36], work[:, 36:40]
            bc = lambda v: v.broadcast_to([P, NT, NE])
            dve.wait_ge(rlog_done, 1)
            dve.wait_ge(s_wr, 32)
            link(V.tensor_tensor(lgt, ps[:, 0, 0:128].rearrange("p (t e) -> p t e", t=NT),
                                 brt[:, :].unsqueeze(1).broadcast_to([P, NT, NE]), ALU.add))
            for t in range(NT):
                i = V.max(top[:, t, :], lgt[:, t, :])
            link(i)
            V.tensor_tensor(ex, lgt, bc(top[:, :, 0:1]), ALU.subtract).then_inc(rex_in, 1)
            V.tensor_tensor(eq, lgt, bc(top[:, :, 3:4]), ALU.is_equal)
            link(V.tensor_tensor(gt, lgt, bc(top[:, :, 3:4]), ALU.is_gt))
            V.reduce_sum(cnt, gt, AX.X)
            for t in range(NT):
                i = V.tensor_tensor_scan(cum[:, t, :], ones[:, 0:NE], eq[:, t, :], 0.0, ALU.mult, ALU.add)
            link(i)
            link(V.tensor_tensor(cum, cum, bc(cnt.unsqueeze(2)), ALU.add))
            link(V.scalar_tensor_tensor(out=eq, in0=cum, scalar=float(TOP), in1=eq, op0=ALU.is_le, op1=ALU.mult))
            link(V.tensor_tensor(chosen_r[:, :, :], gt, eq, ALU.add))
            V.engine_nop().then_inc(sel_done, 1)
            for t in range(NT):
                i = V.tensor_tensor_scan(cum[:, t, :], ones[:, 0:NE], chosen[:, t, :], 0.0, ALU.mult, ALU.add)
            dve.wait_ge(rex_out, 1)
            link(V.tensor_tensor(ex, ex, chosen, ALU.mult))
            link(V.reduce_sum(tot, ex, AX.X))
            link(V.reciprocal(tot, tot))
            V.tensor_tensor(info[:, :, :, 2], ex, bc(tot.unsqueeze(2)), ALU.mult)
            V.tensor_scalar(gt, cum, float(SEQ), -float(SEQ) - SKIP, ALU.mult, ALU.add)
            V.tensor_scalar(info[:, :, :, 0], bc(cst[:, TOK:TOK + NT].unsqueeze(2)), -SKIP, None, ALU.add)
            V.tensor_tensor(twin[:, :, 0, :], ex, bc(tot.unsqueeze(2)), ALU.mult)
            link(V.tensor_tensor(twin[:, :, 1, :], ex, bc(tot.unsqueeze(2)), ALU.mult))
            V.tensor_tensor(info[:, :, :, 1], gt, bc(cst[:, TOK:TOK + NT].unsqueeze(2)), ALU.add).then_inc(gates_done, 1)
            dve.wait_ge(pos_done, 1)
            V.tensor_scalar(work[:, 64:96], ps[:, 1, 128:160], 1.0, None, ALU.mult)
            link(V.scalar_tensor_tensor(out=cum, in0=ps[:, 1, 0:128].rearrange("p (t e) -> p t e", t=NT), scalar=1.0,
                                        in1=chosen, op0=ALU.add, op1=ALU.mult))
            for b in range(NB):
                i = V.tensor_scalar(pos[:, :, b * NE:(b + 1) * NE], cum, -1.0 - BLK * b, None, ALU.add)
            i.then_inc(tab_done, 1)
            link(V.reduce_max(work[:, 96:97], work[:, 64:96], AX.X))
            V.tensor_scalar(flag[:, :], work[:, 96:97], BLK + 0.5, None, ALU.is_gt).then_inc(flag_done, 1)
            dve.wait_ge(gthi_done, 1)
            V.tensor_tensor(gt_t[32:64, :], ps[32:64, 2, :], gt_t[32:64, :].bitcast(F32), ALU.subtract).then_inc(gtlo_done, 1)

            def gates_bias(t):
                dve.wait_ge(bd_done, t + 1)
                V.tensor_tensor(h[:, t, :], h[:, t, :], ps[:, BIAS[t]:BIAS[t] + 2, :].rearrange("p a n -> p (a n)"),
                                ALU.add).then_inc(bias_done if t < NT - 1 else up_free, 1)

            def run(b):
                s0 = b * NE
                base = C0 + b * RUN

                def indices(e, par):
                    dve.wait_ge(list_done, s0 + e + 1)
                    if not (isinstance(e, int) and e == 0 and isinstance(b, int)):
                        dve.wait_ge(xg_in, 16 * (s0 + e))
                    V.tensor_scalar(gidx[:, :], ps[:, 6, 0:1], SKIP, None, ALU.add)
                    V.tensor_scalar(didx[:, par, :], ps[:, 6, 1:2], SKIP, None, ALU.add)
                    V.tensor_copy(gate[:, par, :], ps[:, 6, 2:3]).then_inc(idx_done, 1)

                def x_lo_copy(e, par):
                    for q in range(2):
                        dve.wait_ge(xhi_done, (s0 + e) * 2 + q + 1)
                        V.tensor_tensor(x_lo[:, par, 4 * q:4 * q + 4, :], ps[:, 6 + q, :].rearrange("p (k c) -> p k c", k=4),
                                        x_hi[:, par, 4 * q:4 * q + 4, :].bitcast(F32), ALU.subtract).then_inc(xlo_done, 1)

                def a_lo_copy(e):
                    for q in range(2):
                        dve.wait_ge(athi_done, (s0 + e) * 2 + q + 1)
                        V.tensor_tensor(a_lo[:, 4 * q:4 * q + 4, :], ps[:, 6 + q, :].rearrange("p (k c) -> p k c", k=4),
                                        a_hi[:, 4 * q:4 * q + 4, :].bitcast(F32), ALU.subtract).then_inc(atlo_done, 1)

                def glu_in(e, par, first=False):
                    dve.wait_ge(used, up_chunk(base, e, UPC, first))
                    V.tensor_scalar(g_sb[:, :], ps[:, 0:2, :].rearrange("p a n -> p (a n)"), LIMIT, None,
                                    ALU.min).then_inc(gl_done, 1)
                    V.tensor_scalar(l_sb[:, :], ps[:, 2:4, :].rearrange("p a n -> p (a n)"), -LIMIT, LIMIT,
                                    ALU.max, ALU.min).then_inc(up_free, 1)
                    if isinstance(e, int) and e < 2 and isinstance(b, int):
                        pass
                    else:
                        dve.wait_ge(y_out, 16 * (s0 + e - 1))
                    V.tensor_copy(dsti[:, par, :], didx[:, par, :])
                    dve.wait_ge(up_free, s0 + e + 2)
                    V.scalar_tensor_tensor(out=l_sb[:, :], in0=l_sb[:, :], scalar=1.0, in1=g_sb[:, :],
                                           op0=ALU.add, op1=ALU.mult).then_inc(gl2_done, 1)

                def glu_out(e, par):
                    dve.wait_ge(sig_done, s0 + e + 1)
                    dve.wait_ge(gl2_done, s0 + e + 1)
                    V.scalar_tensor_tensor(out=l_sb[:, :], in0=l_sb[:, :], scalar=gate[:, par, :], in1=s_sb[:, :],
                                           op0=ALU.mult, op1=ALU.mult).then_inc(act_done, 1)

                def one(e, par):
                    first = isinstance(e, int) and e == 0
                    lastp = isinstance(e, int) and e == NE - 1

                    def split(part):
                        ring = part if first else (PER * par - DNC + part) % 24
                        lo(base + part if first else base + PER * e - DNC + part, ring % SPLIT, raw_slot(ring))

                    for u in range(UPC):
                        if not (first and u < SPLIT):
                            split(u)
                        if u == 3 and not lastp:
                            indices(e + 1, 1 - par)
                        if u == 5 and not first:
                            a_lo_copy(e - 1)
                    if first:
                        x_lo_copy(e + 1, 1 - par)
                        glu_in(e, par, True)
                        glu_out(e, par)
                        return
                    split(UPC)
                    if not lastp:
                        x_lo_copy(e + 1, 1 - par)
                    split(UPC + 1)
                    split(UPC + 2)
                    glu_in(e, par)
                    split(UPC + 3)
                    glu_out(e, par)

                indices(0, 0)
                if isinstance(b, int):
                    for t in range(NT):
                        gates_bias(t)
                lo(base, 0, raw_slot(0))
                x_lo_copy(0, 0)
                for u in range(1, SPLIT):
                    lo(base + u, u, raw_slot(u))
                steps(dve, one)
                for d in range(DNC):
                    m = PER * NE - DNC + d
                    lo(base + m, m % SPLIT, raw_slot(m))
                    if d == 2:
                        a_lo_copy(NE - 1)

            more = passes(dve, run)

            base = dve.snap(more * ((NB - 1) * RUN))

            def lo3(i):
                lo(base + (C0 + RUN + i), i % SPLIT, raw_slot(i))

            lo3(0)
            for n in range(2):
                dve.wait_ge(pphi_done, n + 1)
                V.tensor_tensor(p_lo[:, n, :], ps[:, 6 + n, :], p_hi[:, n, :].bitcast(F32), ALU.subtract).then_inc(pplo_done, 1)
            lo3(1)
            lo3(2)
            dve.wait_ge(w4hi_done, 1)
            V.tensor_tensor(w4_lo[:, :], raw_slot(4), w4_hi[:, :].bitcast(F32), ALU.subtract).then_inc(w4lo_done, 1)

            def y_add(n, t):
                for q in range(TOP):
                    m = 2 * t + q // 2
                    dve.wait_ge(s_yb[m % 2], 16 * (m // 2 + 1))
                    if q:
                        dve.wait_ge(yadd_done, TOP * t + q)
                    V.tensor_tensor(h[:, t, :], h[:, t, :], yb[m % 2][:, q % 2, :], ALU.add).then_inc(yadd_done, 1)
                rms(n, t, 0, sq3_done, ms3_done, rs3_done)
                if t >= 2:
                    dve.wait_ge(zt_done, 2 * (t - 1))
                normed(xn3[:, t % 2, :], t, 0, gbc[:, :]).then_inc(xn3_done, 1)

            def z_lo_copy(t):
                for q in range(2):
                    dve.wait_ge(zhi_done, 2 * t + q + 1)
                    V.tensor_tensor(z_lo[:, t % 2, 4 * q:4 * q + 4, :], ps[:, 4 + 2 * (t % 2) + q, :].rearrange("p (k c) -> p k c", k=4),
                                    z_hi[:, t % 2, 4 * q:4 * q + 4, :].bitcast(F32), ALU.subtract).then_inc(zlo_done, 1)

            def finish(n, t):
                dve.wait_ge(sg3_done, t + 1)
                dve.wait_ge(pp_done, t + 1)
                link(V.tensor_tensor(pp[:, t, :], pp[:, t, :], sgm[:, :], ALU.mult))
                V.tensor_tensor(h[:, t, :], h[:, t, :], pp[:, t, :], ALU.add).then_inc(h3_done, 1)
                rms(n, t, 1, sq3_done, ms3_done, rs3_done)
                normed(pp[:, t, :], t, 1, gfin).then_inc(fin_done, 1)

            dve.wait_ge(s_gbc, 48)
            y_add(0, 0)
            z_lo_copy(0)
            lo3(3)
            y_add(1, 1)
            z_lo_copy(1)
            y_add(2, 2)
            dve.wait_ge(s_gfin, 16)
            finish(3, 0)
            z_lo_copy(2)
            y_add(4, 3)
            finish(5, 1)
            z_lo_copy(3)
            finish(6, 2)
            finish(7, 3)

        @block.tensor
        def _(pe):
            mm = nc.tensor.matmul

            def three(outs, l_hi, l_lo, r_hi, r_lo, start, stop):
                for o, r in zip(outs, r_hi):
                    mm(o, l_hi, r, start=start, stop=False)
                for o, r in zip(outs, r_lo):
                    mm(o, l_hi, r, start=False, stop=False)
                for o, r in zip(outs, r_hi):
                    i = mm(o, l_lo, r, start=False, stop=stop)
                return i

            def transposes(src, t):
                for k in range(NK):
                    i = nc.tensor.transpose(ps[:, 2 * t + k // 4, (k % 4) * P:(k % 4 + 1) * P],
                                            src[:, k * P:(k + 1) * P], ident)
                    if k % 4 == 3:
                        i.then_inc(tp_done, 1)

            pe.wait_ge(s_cst, 16)
            for t in range(NT):
                pe.wait_ge(xn_done, t + 1)
                transposes(xn[:, t, :], t)
            pe.wait_ge(s_stage, 16 * 5)
            pe.wait_ge(tlo_done, 1)
            nc.tensor.transpose(ps[:, 0, 0:124], stage[0:124, :], cst[0:124, IDENT:IDENT + 124])
            nc.tensor.transpose(ps[:, 0, 128:148], stage2[:, :], cst[0:20, IDENT:IDENT + 20]).then_inc(par_tp, 1)
            pe.wait_ge(tlo_done, 2 * NT)
            pe.wait_ge(par_in, 2)
            for c in range(4):
                pe.wait_ge(lo_done, c + 1)
                for a in range(2):
                    k, s, o = 2 * c + a, c % SPLIT, a * ATT_W
                    for t in range(NT):
                        tt = slice(t * P, (t + 1) * P)
                        i = three([ps[:, t, :], ps[:, 4 + t, 0:REST_W]], t_hi[:, k, tt], t_lo[:, k, tt],
                                  [w_hi[:, s, o:o + 512], w_hi[:, s, o + 512:o + ATT_W]],
                                  [w_lo[:, s, o:o + 512], w_lo[:, s, o + 512:o + ATT_W]], k == 0, k == NK - 1)
                i.then_inc(used, 1)
            pe.wait_ge(uv_done, 2)
            for n, bl in enumerate((4, 5, 6, 7, 0, 1, 2, 3)):
                pe.wait_ge(rope_done, 2 if n < 4 else 3)
                bank = (n + 4) % 8
                for t in range(NT):
                    i = nc.tensor.transpose(ps[:, bank, t * P:(t + 1) * P], roped[:, t, bl * P:(bl + 1) * P], ident)
                i.then_inc(rtp_done, 1)
            for t in range(1, NT):
                for hh in range(IDX_HEADS):
                    half = slice(64 * (hh % 2), 64 * (hh % 2) + 64)
                    pe.wait_ge(rt_done, 4)
                    if t > 1:
                        pe.wait_ge(rl_done, (t - 2) * IDX_HEADS + hh + 1)
                    mm(ps[:, 4 + hh, 0:(t + 1) * P], r_t[half, 5 + hh // 2, t * P:(t + 1) * P],
                       r_t[half, 7, 0:(t + 1) * P], start=True, stop=True).then_inc(si_done, 1)
            pe.wait_ge(rt_done, 8)
            pe.wait_ge(rl_done, 3 * IDX_HEADS)
            for c in range(4, 8):
                pe.wait_ge(lo_done, c + 1)
                for a in range(2):
                    k, s = 2 * (c - 4) + a, c % SPLIT
                    for j in range(8):
                        o = a * 1024 + j * P
                        i = three([ps[:, j, :]], w_hi[:, s, o:o + P], w_lo[:, s, o:o + P],
                                  [t_hi[:, k, :]], [t_lo[:, k, :]], k == 0, k == NK - 1)
                i.then_inc(used, 1)

            def scores(n):
                t, hh = n // HEADS, n % HEADS
                half = slice(64 * (hh % 2), 64 * (hh % 2) + 64)
                if n >= 2:
                    pe.wait_ge(lg_done, n - 1)
                mm(ps[:, n % 2, 0:(t + 1) * P], r_t[half, hh // 2, t * P:(t + 1) * P], r_t[half, 4, 0:(t + 1) * P],
                   start=True, stop=True).then_inc(s_done, 1)

            def probs_transposed(n):
                pe.wait_ge(exp_done, n + 1)
                if n >= 2:
                    pe.wait_ge(pte_done, n - 1)
                for kb in range(n // HEADS + 1):
                    i = nc.tensor.transpose(ps[:, 2 + n % 2, kb * P:(kb + 1) * P], probs[:, n % 2, kb * P:(kb + 1) * P], ident)
                i.then_inc(pt_done, 1)

            def values(n):
                t, hh = n // HEADS, n % HEADS
                pe.wait_ge(pte_done, n + 1)
                if hh == 0 and t >= 2:
                    pe.wait_ge(an_done, t - 1)
                for kb in range(t + 1):
                    i = mm(ps[:, 4 + t % 2, hh * HD:(hh + 1) * HD], probs_t[:, n % 2, kb * P:(kb + 1) * P], uv[:, kb, 0:HD],
                           start=(kb == 0), stop=(kb == t))
                i.then_inc(pv_done, 1)

            def attn_transposed(t):
                pe.wait_ge(an_done, t + 1)
                if t >= 1:
                    pe.wait_ge(alo_done, t)
                for k in range(4):
                    i = nc.tensor.transpose(ps[:, 6, k * P:(k + 1) * P], attn[:, k * P:(k + 1) * P], ident)
                i.then_inc(atp_done, 1)

            pe.wait_ge(glu_done, NJ)
            for n in range(32):
                scores(n)
                if n >= 1:
                    probs_transposed(n - 1)
                if n >= 2:
                    values(n - 2)
                if n % HEADS == 4 and n > HEADS:
                    attn_transposed(n // HEADS - 1)
            probs_transposed(31)
            values(30)
            values(31)
            attn_transposed(NT - 1)
            pe.wait_ge(tap_done, TAPS * NJ)
            for j in range(NJ):
                i = mm(ps[:, 7, :], ones, acc[:, j, :], start=(j == 0), stop=(j == NJ - 1))
            i.then_inc(cs_done, 1)
            pe.wait_ge(alo_done, NT)
            for j in range(NJ):
                pe.wait_ge(csq_done, j + 1)
                i = mm(ps[:, 6, :], ones, sg[:, j, :], start=(j == 0), stop=(j == NJ - 1))
            i.then_inc(cs_done, 1)
            pe.wait_ge(cr_done, 1)
            pe.wait_ge(ahi_done, NT)
            def out_products(c, a, t):
                k, s, o = 2 * (c - 8) + a, c % SPLIT, a * 1024
                tt = slice(t * P, (t + 1) * P)
                return three([ps[:, 2 * t, :], ps[:, 2 * t + 1, :]], t_hi[:, k, tt], t_lo[:, k, tt],
                             [w_hi[:, s, o:o + 512], w_hi[:, s, o + 512:o + 1024]],
                             [w_lo[:, s, o:o + 512], w_lo[:, s, o + 512:o + 1024]], k == 0, k == NK - 1)

            for c in range(8, 11):
                pe.wait_ge(lo_done, c + 1)
                for a in range(2):
                    k = 2 * (c - 8) + a
                    if k >= NJ:
                        pe.wait_ge(mlo_done, k - NJ + 1)
                    for t in range(NT):
                        i = out_products(c, a, t)
                i.then_inc(used, 1)
            pe.wait_ge(lo_done, 12)
            pe.wait_ge(mlo_done, NJ)
            for t in range(NT):
                out_products(11, 0, t)
                out_products(11, 1, t).then_inc(out_done if t < NT - 1 else used, 1)
            pe.wait_ge(s_wr, 32)
            for t in range(NT + 1):
                if t < NT:
                    pe.wait_ge(xn_done, NT + t + 1)
                    transposes(xn[:, t, :], t)
                if t >= 1:
                    pe.wait_ge(thi_done, 2 * NT + 2 * t)
                    for k in range(NK):
                        i = mm(ps[:, 0, (t - 1) * NE:t * NE], r_t[:, k, (t - 1) * P:t * P], wr[:, k, :],
                               start=(k == 0), stop=(k == NK - 1))
            i.then_inc(rlog_done, 1)
            pe.wait_ge(sel_done, 1)
            pe.wait_ge(tri_done, 1)
            for t in range(NT):
                for u in range(t + 1):
                    mm(ps[:, 1, t * NE:(t + 1) * NE], tri_r[:, 0:P] if u == t else tri_r[:, P:2 * P], chosen_r[:, u, :],
                       start=(u == 0), stop=(u == t))
            for u in range(NT):
                i = mm(ps[:, 1, 128:160], tri_r[:, P:2 * P], chosen_r[:, u, :], start=(u == 0), stop=(u == NT - 1))
            i.then_inc(pos_done, 1)
            pe.wait_ge(gates_done, 1)
            for t in range(NT):
                i = nc.tensor.transpose(ps[0:64, 2, t * P:(t + 1) * P], rt[:, 768 + 64 * t:768 + 64 * (t + 1)], ident)
            i.then_inc(gtp_done, 1)

            def gates_bias(t):
                for q in range(2):
                    tt, cols = slice(t * P, (t + 1) * P), slice(q * 512, (q + 1) * 512)
                    mm(ps[:, BIAS[t] + q, :], gt_t[:, tt], bdn_hi[:, cols], start=True, stop=False)
                    i = mm(ps[:, BIAS[t] + q, :], gt_t[:, tt], bdn_lo[:, cols], start=False, stop=True)
                i.then_inc(bd_done, 1)


            def run(b):
                s0 = b * NE
                base = C0 + b * RUN

                def listing(e):
                    pe.wait_ge(oh_done, s0 + e + 1)
                    for t in range(NT):
                        i = mm(ps[:, 6, 0:3], onehot[:, t, :], info[:, t, bass.ds(e, 1), :].rearrange("p o c -> p (o c)"),
                               start=(t == 0), stop=(t == NT - 1))
                    i.then_inc(list_done, 1)

                def x_transposed(e):
                    pe.wait_ge(xg_in, 16 * (s0 + e + 1))
                    for k in range(NK):
                        i = nc.tensor.transpose(ps[:, 6 + k // 4, (k % 4) * P:(k % 4 + 1) * P], xg[:, k * P:(k + 1) * P], ident)
                        if k % 4 == 3:
                            i.then_inc(xt_done, 1)

                def a_transposed(e):
                    pe.wait_ge(act_done, s0 + e + 1)
                    for k in range(NK):
                        i = nc.tensor.transpose(ps[:, 6 + k // 4, (k % 4) * P:(k % 4 + 1) * P], l_sb[:, k * P:(k + 1) * P], ident)
                        if k % 4 == 3:
                            i.then_inc(at_done, 1)

                def up(e, par, u, c, ring):
                    pe.wait_ge(lo_done, c + 1)
                    s = ring % SPLIT
                    cols = [slice(n * 512, (n + 1) * 512) for n in range(4)]
                    three([ps[:, n, :] for n in range(4)], x_hi[:, par, u, :], x_lo[:, par, u, :],
                          [w_hi[:, s, n] for n in cols], [w_lo[:, s, n] for n in cols], False, u == UPC - 1).then_inc(used, 1)

                def down(d, c, ring):
                    pe.wait_ge(lo_done, c + 1)
                    s = ring % SPLIT
                    for a in range(2):
                        k = 2 * d + a
                        cols = [slice(a * 1024 + n * 512, a * 1024 + (n + 1) * 512) for n in range(2)]
                        i = three([ps[:, 4 + n, :] for n in range(2)], a_hi[:, k, :], a_lo[:, k, :],
                                  [w_hi[:, s, n] for n in cols], [w_lo[:, s, n] for n in cols], k == 0, k == NK - 1)
                    i.then_inc(used, 1)

                def downs(e, par, last=False):
                    pe.wait_ge(atlo_done, 2 * (s0 + e + 1))
                    if not (isinstance(e, int) and e == 0 and isinstance(b, int)):
                        pe.wait_ge(y_done, s0 + e)
                    for d in range(DNC):
                        down(d, dn_chunk(base, e, d, last), slot8(par, (0 if last else UPC) + d))

                def one(e, par):
                    first = isinstance(e, int) and e == 0
                    lastp = isinstance(e, int) and e == NE - 1
                    pe.wait_ge(up_free, s0 + e + 1)
                    pe.wait_ge(xlo_done, 2 * (s0 + e + 1))
                    pe.wait_ge(sel_in, s0 + e + 1)
                    for n in range(4):
                        mm(ps[:, n, :], sel[:, :], bup[:, n * 512:(n + 1) * 512], start=True, stop=False)
                    for u in range(UPC):
                        ring = slot8(par, u, first)
                        up(e, par, u, up_chunk(base, e, u, first), ring)
                        if u == 0 and not lastp:
                            listing(e + 1)
                        if u == 2 and not first:
                            if not lastp:
                                pe.wait_ge(idx_done, s0 + e + 2)
                            a_transposed(e - 1)
                        if u == 5 and not lastp:
                            if first:
                                pe.wait_ge(idx_done, s0 + e + 2)
                            else:
                                pe.wait_ge(atlo_done, 2 * (s0 + e))
                            x_transposed(e + 1)
                    if not first:
                        downs(e - 1, par)

                if isinstance(b, int):
                    pe.wait_ge(bup_done, 1)
                else:
                    pe.wait_ge(atlo_done, 2 * s0)
                listing(0)
                if isinstance(b, int):
                    pe.wait_ge(gtlo_done, 1)
                    pe.wait_ge(bdlo_done, 1)
                    for t in range(3):
                        gates_bias(t)
                    pe.wait_ge(bias_done, 1)
                    gates_bias(3)
                pe.wait_ge(idx_done, s0 + 1)
                x_transposed(0)
                pe.wait_ge(xlo_done, 2 * (s0 + 1))
                steps(pe, one)
                a_transposed(NE - 1)
                downs(NE - 1, 0, True)

            more = passes(pe, run)

            base = pe.snap(more * ((NB - 1) * RUN))
            ybase = pe.snap(more * ((NB - 1) * NE))
            pe.wait_ge(s_p, 16)
            pe.wait_ge(atlo_done, ybase * 2 + 2 * NE)
            for n in range(2):
                for t in range(NT):
                    i = nc.tensor.transpose(ps[:, 6 + n, t * P:(t + 1) * P], p_sb[:, t, n * P:(n + 1) * P], ident)
                i.then_inc(ptp_done, 1)
            pe.wait_ge(pplo_done, 2)
            pe.wait_ge(up_free, ybase + (NE + 1))

            def gate_products(outs, k, l_hi, l_lo, r_hi, r_lo, n_k):
                cols = [slice(k % 2 * 1024 + n * 512, k % 2 * 1024 + (n + 1) * 512) for n in range(2)]
                return three(outs, l_hi, l_lo, [r_hi[:, n] for n in cols], [r_lo[:, n] for n in cols], k == 0, k == n_k - 1)

            pe.wait_ge(lo_done, base + (C0 + RUN + 1))
            for t in range(NT):
                if PROJ[t] == 4:
                    pe.wait_ge(y_done, ybase + NE)
                tt = slice(t * P, (t + 1) * P)
                for k in range(2):
                    i = gate_products([ps[:, PROJ[t] + n, :] for n in range(2)], k, p_hi[:, k, tt], p_lo[:, k, tt],
                                      w_hi[:, 0, :], w_lo[:, 0, :], 2)
                i.then_inc(proj_done if t < NT - 1 else used, 1)

            def z_transposed(t):
                pe.wait_ge(xn3_done, t + 1)
                if t < 2:
                    pe.wait_ge(pp_done, NT)
                else:
                    pe.wait_ge(zlo_done, 2 * (t - 1))
                for k in range(NK):
                    i = nc.tensor.transpose(ps[:, 4 + 2 * (t % 2) + k // 4, (k % 4) * P:(k % 4 + 1) * P],
                                            xn3[:, t % 2, k * P:(k + 1) * P], ident)
                    if k % 4 == 3:
                        i.then_inc(zt_done, 1)

            w4_at = {0: (w_hi[:, 1, :], w_lo[:, 1, :]), 1: (w_hi[:, 2, :], w_lo[:, 2, :]),
                     2: (w_hi[:, 0, :], w_lo[:, 0, :]), 3: (w4_hi, w4_lo)}
            z_transposed(0)
            for t in range(NT):
                if t >= 2:
                    pe.wait_ge(sg3_done, t - 1)
                for k in range(NK):
                    if k % 4 == 0:
                        pe.wait_ge(zlo_done, 2 * t + k // 4 + 1)
                    if t == 0 and k < 6 and k % 2 == 0:
                        pe.wait_ge(lo_done, base + (C0 + RUN + 2 + k // 2))
                    if t == 0 and k == 6:
                        pe.wait_ge(w4lo_done, 1)
                    i = gate_products([ps[:, 2 * (t % 2) + n, :] for n in range(2)], k, z_hi[:, t % 2, k, :], z_lo[:, t % 2, k, :],
                                      *w4_at[k // 2], NK)
                    if k == 4 and t + 1 < NT:
                        z_transposed(t + 1)
                i.then_inc(gated, 1)


def constants():
    c = np.zeros((P, NCONST), np.float32)
    r = np.arange(P)
    c[:, IDENT:IDENT + P] = np.eye(P)
    c[:, TRI:TRI + P] = r[:, None] < r[None, :]
    c[:, ONES:ONES + P] = 1.0
    c[:, IOTA:IOTA + P] = r[None, :]
    c[:, CAUS:CAUS + P] = np.where(r[None, :] <= r[:, None], 0.0, NEG)
    inv = np.float32(10000.0) ** (-np.arange(0, HD, 2, dtype=np.float32) / np.float32(HD))
    ang = (np.arange(SEQ, dtype=np.float32)[:, None] * inv[None, :]).astype(np.float32)
    for o, f in ((COS, np.cos), (SIN, np.sin)):
        c[:, o:o + P] = f(ang).reshape(NT, P, 32).transpose(1, 0, 2).reshape(P, NT * 32)
    c[:, TOK:TOK + NT] = np.arange(NT)[None, :] * P + r[:, None]
    c[0:64, EYE:EYE + NE] = (np.arange(64)[:, None] % NE) == np.arange(NE)[None, :]
    return c


_INS = ["x", "p", "w_in", "w_out", "g_mix", "g_ffn", "conv_glu_b", "conv_dw_w", "conv_dw_b", "conv_ln_g", "conv_ln_b",
        "w_router", "b_router", "w_up", "b_up", "w_down", "b_down", "w_ple_proj", "w_ple_gate", "g_ple", "g_final"]


def kernel(**inputs):
    import numpy as _np
    import concourse.bacc as _bacc
    from concourse import mybir as _mybir
    from concourse.bass_utils import run_bass_kernel_spmd as _run

    nc = _bacc.Bacc("TRN2", target_bir_lowering=False, num_devices=1)
    arrays, args = {}, []
    for name in _INS + ["constants"]:
        a = constants() if name == "constants" else _np.ascontiguousarray(inputs[name])
        arrays[f"in_{name}_dram"] = a
        args.append(nc.dram_tensor(f"in_{name}_dram", a.shape, _mybir.dt.from_np(a.dtype), kind="ExternalInput").ap())
    args.append(nc.dram_tensor("out_0_dram", (1, SEQ, D), _mybir.dt.float32, kind="ExternalOutput").ap())
    build(nc, *args)
    r = _run(nc, [arrays], core_ids=[0])
    return r.results[0]["out_0_dram"]
```

```python
from contextlib import ExitStack

import concourse.bass as bass
from concourse import mybir
import numpy as np

F32 = mybir.dt.float32
F32R = mybir.dt.float32r
I32 = mybir.dt.int32
ALU = mybir.AluOpType
ACT = mybir.ActivationFunctionType
AX = mybir.AxisListType

P = 128
SEQ, D = 512, 1024
NT = SEQ // P
NK = D // P
PLE = 256
HEADS, HD = 8, 64
IDX_HEADS = 4
CONV_W, TAPS = 512, 31
NJ = CONV_W // P
IN_W = HEADS * HD + 2 * HD + IDX_HEADS * HD + HD + IDX_HEADS + 2 * CONV_W
ATT_W = IN_W - 2 * CONV_W
REST_W = ATT_W - 512
N_SEL = min(256, SEQ // 4)
NE, TOP = 32, 4
LIMIT, ALPHA, EPS = 7.0, 1.702, 1e-6
NEG = -1e30
TAKEN = -3e38
SKIP = 4096.0
BLK = 128
NB = SEQ // BLK
RAW, SPLIT = 8, 3
RAW1 = 4
C0 = 12
UPC, DNC = 8, 4
PER = UPC + DNC
RUN = PER * NE
POOL_LO = (6, 7, 8, 9)
EARLY = 5
ROUNDS = N_SEL // 8
TAIL = 5

DVE_J, POOL_J = (0, 1), (2, 3)
PRODUCT_SHARES = (10, 16, 18, 16)
TAP_SHARES = (0, 6, 12, 13)
PRODUCTS = [(k, j) for k in range(TAPS) for j in POOL_J]
ROPED = (4, 5, 6, 7, 0, 1, 2, 3)
BIAS = (0, 2, 4, 0)
PROJ = (0, 2, 6, 4)

IDENT, TRI, ONES, IOTA, CAUS, COS, SIN, TOK, EYE = 0, 128, 256, 384, 512, 640, 768, 896, 900
NCONST = 932


def share(shares, n):
    t, hh = n // HEADS, n % HEADS
    return shares[t] * (hh + 1) // HEADS - shares[t] * hh // HEADS


def build(nc, x, p, w_in, w_out, g_mix, g_ffn, conv_glu_b, conv_dw_w, conv_dw_b, conv_ln_g, conv_ln_b,
          w_router, b_router, w_up, b_up, w_down, b_down, w_ple_proj, w_ple_gate, g_ple, g_final,
          consts, out):
    ctx = ExitStack()
    with ctx:
        def sb(name, shape, dt=F32, stack=ctx):
            return stack.enter_context(nc.sbuf_tensor(name, shape, dt))

        def sem(name):
            return ctx.enter_context(nc.semaphore(name))

        xn_rows = nc.dram_tensor("xn_rows", [SEQ, D], F32, kind="Internal").ap()
        y_rows = nc.dram_tensor("y_rows", [TOP * SEQ, D], F32, kind="Internal").ap()

        cst = sb("cst", [P, NCONST])
        par = sb("par", [P, 144])
        gbc = sb("gbc", [P, D])
        h = sb("h", [P, NT, D])
        with ExitStack() as s0:
            sb("under_r_lo", [P, 2, 2048], F32, s0)
            r_lo = sb("r_lo", [P, NK, SEQ], F32R, s0)
        raw_a = sb("raw_a", [P, RAW1, 2048])
        w_hi = sb("w_hi", [P, SPLIT, 2048], F32R)
        w_lo = sb("w_lo", [P, SPLIT, 2048], F32R)
        pos = sb("pos", [P, NT, NB * NE])
        info = sb("info", [P, NT, NE, 3])
        st = sb("st", [P, 2, 16])
        flag = sb("flag", [P, 1], I32)
        brt = sb("brt", [P, NE])

        with ExitStack() as s1:
            tq = sb("tq", [P, 4, 4, SEQ], F32R, s1)
            reg_a = sb("reg_a", [P, 4224], F32, s1)
            r_hi = sb("r_hi", [P, NK, SEQ], F32R, s1)
            tmp = sb("tmp", [P, 2, 1024], F32, s1)
            rl = sb("rl", [P, 4, 512], F32, s1)
            lg = sb("lg", [P, 2, 512], F32, s1)
            uv = sb("uv", [P, NT, 68], F32, s1)
            work = sb("work", [P, 1152], F32, s1)
            mx = sb("mx", [P, 3, 32], F32, s1)
            m8 = sb("m8", [P, 8], F32, s1)
            attn = sb("attn", [P, 512], F32, s1)
            stage = sb("stage", [P, 128], F32, s1)
            stage2 = sb("stage2", [20, 128], F32, s1)
            wr = sb("wr", [P, NK, NE], F32, s1)
            prod1 = sb("prod1", [P, SEQ], F32, s1)
            tri_r = sb("tri_r", [P, 2 * P], F32R, s1)
            chosen_r = sb("chosen_r", [P, NT, NE], F32R, s1)
        xn = reg_a[:, 0:4096].rearrange("p (t n) -> p t n", t=NT)
        roped = xn
        prod = [pos[:, :, :].rearrange("p t n -> p (t n)"), prod1[:, :]]

        def t_hi(k, cols):
            return tq[:, 2 * (k // 4), k % 4, cols]

        def t_lo(k, cols):
            return tq[:, 2 * (k // 4) + 1, k % 4, cols]

        def t_four(low, k0, t):
            return tq[:, 2 * (k0 // 4) + low, :, t * P:(t + 1) * P]

        PADW = 30 + SEQ
        hpad = reg_a[:, 0:4 * PADW].rearrange("p (j n) -> p j n", j=NJ)
        acc = reg_a[:, 4 * PADW:4 * PADW + 2048].rearrange("p (j n) -> p j n", j=NJ)
        sg = tmp[:, :, :].rearrange("p a (b n) -> p (a b) n", b=2)
        probs, probs_t = rl[:, 0:2, :], rl[:, 2:4, :]

        with ExitStack() as s1a:
            sb("under_raw", [P, 8192 + 4224], F32, s1a)
            b_raw = sb("b_raw", [64, 3072], F32, s1a)
        bup_raw, bdn_raw = b_raw[:, 0:2048], b_raw[:, 2048:3072]
        xr_hi = r_hi[:, 0:4, :].rearrange("p a n -> p (a n)").rearrange("p (b k n) -> p b k n", b=2, k=NK)
        xr_lo = r_hi[:, 4:8, :].rearrange("p a n -> p (a n)").rearrange("p (b k n) -> p b k n", b=2, k=NK)
        with ExitStack() as s1b:
            sb("under_tmp", [P, 4 * 4096 + 128], F32, s1b)
            bdn_hi = sb("bdn_hi", [64, D], F32R, s1b)
            bdn_lo = sb("bdn_lo", [64, D], F32R, s1b)
            sb("under_attn", [P, 2048 + 1024 + 272 + 1152 + 96 + 8], F32, s1b)
            gt_t = sb("gt_t", [64, SEQ], F32R, s1b)
        with ExitStack() as s1c:
            sb("under_attn2", [P, 4 * 4096 + 128 + 2048 + 2048 + 1024 + 272 + 1152 + 96 + 8], F32, s1c)
            wr2 = sb("wr2", [P, NK, 2 * NE], F32R, s1c)

        with ExitStack() as s2:
            raw_b = sb("raw_b", [P, RAW - RAW1, 2048], F32, s2)
            g_sb = sb("g_sb", [P, D], F32, s2)
            l_sb = sb("l_sb", [P, D], F32, s2)
            s_sb = sb("s_sb", [P, D], F32, s2)
            a_hi = sb("a_hi", [P, NK, P], F32R, s2)
            sb("under_r_hi", [P, 128], F32, s2)
            onehot = sb("onehot", [P, NT, BLK], F32, s2)
            xg = sb("xg", [P, D], F32, s2)
            x_hi = sb("x_hi", [P, 2, NK, P], F32R, s2)
            x_lo = sb("x_lo", [P, 2, NK, P], F32R, s2)
            sb("under_rl", [P, 512], F32, s2)
            bup = sb("bup", [64, 2048], F32R, s2)
            y_sb = sb("y_sb", [P, D], F32, s2)
            a_lo = sb("a_lo", [P, NK, P], F32R, s2)
            sel = sb("sel", [64, P], F32R, s2)
            pos_e = sb("pos_e", [P, NT], F32, s2)
            gidx = sb("gidx", [P, 1], I32, s2)
            didx = sb("didx", [P, 2, 1], I32, s2)
            dsti = sb("dsti", [P, 2, 1], I32, s2)
            gate = sb("gate", [P, 2, 1], F32, s2)
        with ExitStack() as s3:
            s3.enter_context(nc.sbuf_tensor("hold", [P, RAW - RAW1, 2048], F32))
            xn3 = sb("xn3", [P, 2, D], F32, s3)
            sgm = sb("sgm", [P, D], F32, s3)
            sq3 = sb("sq3", [P, D], F32, s3)
            sb("under_p_sb", [P, 128], F32, s3)
            p_sb = sb("p_sb", [P, NT, PLE], F32, s3)
            sb("under_p_hi", [P, 512], F32, s3)
            p_hi = sb("p_hi", [P, PLE // P, SEQ], F32R, s3)
            p_lo = sb("p_lo", [P, PLE // P, SEQ], F32R, s3)
            w4_hi = sb("w4_hi", [P, 2048], F32R, s3)
            w4_lo = sb("w4_lo", [P, 2048], F32R, s3)
            z_hi = sb("z_hi", [P, 2, NK, P], F32R, s3)
            z_lo = sb("z_lo", [P, 2, NK, P], F32R, s3)
        pp = raw_b[:, 1:3, :].rearrange("p a (b n) -> p (a b) n", b=2)
        yb = [raw_b[:, 3, :].rearrange("p (a n) -> p a n", a=2), raw_a[:, 0, :].rearrange("p (a n) -> p a n", a=2)]
        gfin = raw_a[:, 1, 0:D]
        rt = lg[:, :, :].rearrange("p a n -> p (a n)")

        ps = ctx.enter_context(nc.psum_tensor("ps", [P, 8, 512], F32))

        ident = cst[:, IDENT:IDENT + P]
        ones = cst[:, ONES:ONES + P]

        s_cst, s_stage, s_gbc, s_p = sem("s_cst"), sem("s_stage"), sem("s_gbc"), sem("s_p")
        s_x = [sem(f"s_x{t}") for t in range(NT)]
        s_wr, s_bup, s_bdn = sem("s_wr"), sem("s_bup"), sem("s_bdn")
        raw_in = [sem(f"raw_in{i}") for i in range(RAW)]
        hi_done, lo_done, used = sem("hi_done"), sem("lo_done"), sem("used")
        dve_seq = sem("dve_seq")
        ptap_done, prod_done, conv_done, rest_done, rlo_done, wr2_hi, wr2_lo, xr_done = (sem(n) for n in (
            "ptap_done", "prod_done", "conv_done", "rest_done", "rlo_done", "wr2_hi", "wr2_lo", "xr_done"))
        sq_done, ms_done, rs_done, xn_done = sem("sq_done"), sem("ms_done"), sem("rs_done"), sem("xn_done")
        tp_done, thi_done, tlo_done = sem("tp_done"), sem("thi_done"), sem("tlo_done")
        par_tp, par_in = sem("par_tp"), sem("par_in")
        uv_done, rope_done, rtp_done, rt_done = sem("uv_done"), sem("rope_done"), sem("rtp_done"), sem("rt_done")
        si_done, rl_done = sem("si_done"), sem("rl_done")
        glu_sig, glu_done = sem("glu_sig"), sem("glu_done")
        s_done, lg_done, exp_done, pt_done, pte_done, pv_done = (sem(n) for n in (
            "s_done", "lg_done", "exp_done", "pt_done", "pte_done", "pv_done"))
        an_done, atp_done, ahi_done, alo_done = sem("an_done"), sem("atp_done"), sem("ahi_done"), sem("alo_done")
        tap_done, cs_done, cc_done, csq_done, cv_done = (sem(n) for n in (
            "tap_done", "cs_done", "cc_done", "csq_done", "cv_done"))
        cr_done, crs_done, cz_done, csg_done, mix_done, mhi_done, mlo_done = (sem(n) for n in (
            "cr_done", "crs_done", "cz_done", "csg_done", "mix_done", "mhi_done", "mlo_done"))
        h1_done, out_done = sem("h1_done"), sem("out_done")
        xn_out = sem("xn_out")
        rlog_done, rex_in, rex_out, sel_done, pos_done, gates_done = (sem(n) for n in (
            "rlog_done", "rex_in", "rex_out", "sel_done", "pos_done", "gates_done"))
        gtp_done, gthi_done, gtlo_done = sem("gtp_done"), sem("gthi_done"), sem("gtlo_done")
        bdhi_done, bdlo_done, bd_done, bias_done = (sem(n) for n in ("bdhi_done", "bdlo_done", "bd_done", "bias_done"))
        xg_clear, tri_done = sem("xg_clear"), sem("tri_done")
        tab_done, flag_done = sem("tab_done"), sem("flag_done")
        buphi_done, bup_done = sem("buphi_done"), sem("bup_done")
        pos_e_in, pool_waits = sem("pos_e_in"), sem("pool_waits")
        oh_done, list_done, idx_done, xg_in, sel_in = (sem(n) for n in (
            "oh_done", "list_done", "idx_done", "xg_in", "sel_in"))
        xt_done, xhi_done, xlo_done = sem("xt_done"), sem("xhi_done"), sem("xlo_done")
        up_free, gl_done, gl2_done, sig_done, act_done = (sem(n) for n in (
            "up_free", "gl_done", "gl2_done", "sig_done", "act_done"))
        at_done, athi_done, atlo_done = sem("at_done"), sem("athi_done"), sem("atlo_done")
        dn_free, y_done, y_out = sem("dn_free"), sem("y_done"), sem("y_out")
        s_yb = [sem("s_yb0"), sem("s_yb1")]
        yadd_done, ptp_done, pphi_done, pplo_done = (sem(n) for n in ("yadd_done", "ptp_done", "pphi_done", "pplo_done"))
        s_gfin, w4hi_done, w4lo_done, proj_done, pp_done = (sem(n) for n in (
            "s_gfin", "w4hi_done", "w4lo_done", "proj_done", "pp_done"))
        sq3_done, ms3_done, rs3_done, xn3_done, zt_done, zhi_done, zlo_done, gated, sg3_done = (sem(n) for n in (
            "sq3_done", "ms3_done", "rs3_done", "xn3_done", "zt_done", "zhi_done", "zlo_done", "gated", "sg3_done"))
        h3_done, fin_done = sem("h3_done"), sem("fin_done")
        s_out = [sem("s_out0"), sem("s_out1")]

        block = ctx.enter_context(nc.Block())

        def up_chunk(base, e, u, first=False):
            return base + u if first else base - DNC + PER * e + u

        def dn_chunk(base, e, d, last=False):
            return base - DNC + PER * (e + 1) + (0 if last else UPC) + d

        def slot8(e_par, part, first=False, last=False):
            if first:
                return part
            return (-DNC + PER * e_par + part) % (2 * PER)

        def raw_slot(s):
            s %= RAW
            return raw_a[:, s, :] if s < RAW1 else raw_b[:, s - RAW1, :]

        def raw1(c):
            return c if c < RAW1 else c % 2

        def raw_before(s):
            return sum(raw1(c) == s % RAW for c in range(C0))

        def steps(eng, one):
            one(0, 0)
            one(1, 1)
            with eng.Fori(1, NE // 2 - 1) as j:
                one(2 * j, 0)
                one(2 * j + 1, 1)
            one(NE - 2, 0)
            one(NE - 1, 1)

        def passes(eng, run):
            run(0)
            eng.wait_ge(flag_done, 1)
            more = eng.value_load(flag[0:1, 0:1], min_val=0, max_val=1)
            with eng.If(more > 0):
                with eng.Fori(1, NB) as b:
                    run(b)
            return more

        @block.sync
        def _(sp):
            for t in range(NT):
                sp.dma_start(h[:, t, :], x[0, t * P:(t + 1) * P, :]).then_inc(s_x[t], 16)
                if t == 0:
                    sp.dma_start(gbc[:, :], g_mix[0:1, :].broadcast_to([P, D])).then_inc(s_gbc, 16)
                    sp.dma_start(cst[:, :], consts).then_inc(s_cst, 16)

            def load1(c):
                s = raw1(c)
                if c < 4:
                    dst = raw_a[:, s, 0:2 * ATT_W].rearrange("p (a n) -> p a n", a=2)
                    src = w_in[0, c * 256:(c + 1) * 256, 0:ATT_W]
                elif c < 8:
                    dst = raw_a[:, s, :].rearrange("p (a n) -> p a n", a=4)
                    o = IN_W - CONV_W if c < 6 else ATT_W
                    src = w_in[0, c % 2 * 512:(c % 2 + 1) * 512, o:o + CONV_W]
                else:
                    dst = raw_a[:, s, :].rearrange("p (a n) -> p a n", a=2)
                    src = w_out[0, (c - 8) * 256:(c - 7) * 256, :]
                if c >= RAW1:
                    sp.wait_ge(lo_done, c - 3 if c < 6 else c - 1)
                sp.dma_start(dst, src.rearrange("(a p) n -> p a n", p=P)).then_inc(raw_in[s], 16)

            for c in range(C0):
                load1(c)
                if c == 3:
                    sp.dma_start(wr[:, :, :], w_router[0].rearrange("(k p) n -> p k n", p=P)).then_inc(s_wr, 16)
                    sp.dma_start(brt[:, :], b_router[0:1, :].broadcast_to([P, NE])).then_inc(s_wr, 16)
                    sp.wait_ge(xn_done, NT)
                    sp.dma_start(gbc[:, :], g_ffn[0:1, :].broadcast_to([P, D])).then_inc(s_gbc, 16)

            w_up_c = w_up[0].rearrange("e (k p) n -> (e k) p n", p=P)
            w_dn_c = w_down[0].rearrange("e (c a p) n -> (e c) p a n", p=P, a=2)

            def run(b):
                base = C0 + b * RUN

                def ups(e, par, first=False):
                    for u in range(UPC):
                        ring = slot8(par, u, first)
                        if first and isinstance(b, int):
                            if u < 2:
                                sp.wait_ge(lo_done, C0 - 2 + u + 1)
                            elif u == 2:
                                sp.wait_ge(s_done, 32)
                            elif u == RAW1:
                                for t in range(NT):
                                    sp.wait_ge(xn_done, NT + t + 1)
                                    sp.dma_start(xn_rows[t * P:(t + 1) * P, :], xn[:, t, :]).then_inc(xn_out, 16)
                                sp.wait_ge(used, C0)
                        else:
                            sp.wait_ge(lo_done, up_chunk(base, e, u, first) - RAW + 1)
                        sp.dma_start(raw_slot(ring), w_up_c[bass.ds(e * UPC + u, 1), :, :].rearrange("o p n -> (o p) n")
                                     ).then_inc(raw_in[ring % RAW], 16)

                def downs(e, par, last=False):
                    for d in range(DNC):
                        ring = slot8(par, (0 if last else UPC) + d)
                        sp.wait_ge(lo_done, dn_chunk(base, e, d, last) - RAW + 1)
                        sp.dma_start(raw_slot(ring).rearrange("p (a n) -> p a n", a=2),
                                     w_dn_c[bass.ds(e * DNC + d, 1), :, :, :].rearrange("o p a n -> (o p) a n")
                                     ).then_inc(raw_in[ring % RAW], 16)

                def one(e, par):
                    first = isinstance(e, int) and e == 0
                    ups(e, par, first)
                    if not first:
                        downs(e - 1, par)

                steps(sp, one)
                downs(NE - 1, 0, True)

            more = passes(sp, run)
            base = sp.snap(more * ((NB - 1) * RUN))
            ybase = sp.snap(more * ((NB - 1) * NE))
            sp.dma_start(gbc[:, :], g_ple[0:1, :].broadcast_to([P, D])).then_inc(s_gbc, 16)
            sp.wait_ge(xt_done, ybase * 2 + 2 * NE)
            sp.dma_start(p_sb[:, :, :], p[0, 0].rearrange("(t p) n -> p t n", p=P)).then_inc(s_p, 16)
            for i in range(TAIL):
                sp.wait_ge(lo_done, base + (C0 + RUN + i - RAW + 1))
                src = w_ple_proj[0] if i == 0 else w_ple_gate[0, (i - 1) * 256:i * 256, :]
                sp.dma_start(raw_slot(i).rearrange("p (a n) -> p a n", a=2),
                             src.rearrange("(a p) n -> p a n", p=P)).then_inc(raw_in[i % RAW], 16)
            sp.wait_ge(lo_done, base + (C0 + RUN + 2))
            sp.dma_start(gfin, g_final.rearrange("(a n) -> a n", a=1).broadcast_to([P, D])).then_inc(s_gfin, 16)
            sp.wait_ge(y_out, ybase * 16 + 16 * NE)
            yv = y_rows.rearrange("(g k t p) n -> t g p k n", g=2, k=2, p=P)
            for n in range(NT * 2):
                if n >= 2:
                    sp.wait_ge(yadd_done, 2 * (n - 1))
                sp.dma_start(yb[n % 2], yv[n // 2, n % 2]).then_inc(s_yb[n % 2], 16)
            for t in range(NT):
                sp.wait_ge(fin_done, t + 1)
                sp.dma_start(out[0, t * P:(t + 1) * P, :], pp[:, t, :]).then_inc(s_out[t % 2], 16)
            for q in s_out:
                sp.wait_ge(q, 16 * NT // 2)

        @block.gpsimd
        def _(pool):
            def wait(s, value):
                pool.wait_ge(s, value)
                pool.sem_inc(pool_waits)

            for c in POOL_LO:
                wait(hi_done, c + 1)
                if c == POOL_LO[0]:
                    wait(lo_done, c)
                nc.gpsimd.tensor_tensor(w_lo[:, c % SPLIT, :], raw_a[:, raw1(c), :], w_hi[:, c % SPLIT, :].bitcast(F32),
                                        ALU.subtract).then_inc(lo_done, 1)
            for m in range(len(PRODUCTS)):
                k, j = PRODUCTS[m]
                if k > 0:
                    wait(prod_done, m + 1)
                    if m >= 2 * len(POOL_J):
                        wait(ptap_done, m - 2 * len(POOL_J) + 1)
                    nc.gpsimd.tensor_tensor(acc[:, j, :], acc[:, j, :], prod[m % 2], ALU.add).then_inc(ptap_done, 1)

            def run(b):
                s0 = b * NE
                base = C0 + b * RUN

                def prep(e, par, first=False):
                    if isinstance(e, int) and e == 0 and isinstance(b, int):
                        wait(rlog_done, 1)
                        nc.gpsimd.memset(xg[:, :], 0.0).then_inc(xg_clear, 1)
                        wait(tab_done, 1)
                        pool.sem_inc(pos_e_in)
                        return
                    else:
                        wait(list_done, s0 + e)
                    nc.gpsimd.tensor_copy(pos_e[:, :], pos[:, :, bass.ds(s0 + e, 1)].rearrange("p t o -> p (t o)")).then_inc(pos_e_in, 1)
                    wait(pos_e_in, s0 + e + 1)
                    for t in range(NT):
                        i = nc.gpsimd.tensor_scalar(onehot[:, t, :], cst[:, IOTA:IOTA + P], pos_e[:, t:t + 1], None, ALU.is_equal)
                    i.then_inc(oh_done, 1)

                def gather(e, par):
                    wait(idx_done, s0 + e + 1)
                    if not (isinstance(e, int) and e == 0 and isinstance(b, int)):
                        wait(xt_done, (s0 + e) * 2)
                    else:
                        wait(xn_out, 16 * NT)
                        wait(xg_clear, 1)
                    pool.indirect_dma_start(xg[:, :], None, xn_rows, bass.IndirectOffsetOnAxis(ap=gidx[:, 0:1], axis=0),
                                            bounds_check=SEQ - 1, oob_is_err=False).then_inc(xg_in, 16)

                def selector(e, par):
                    if not (isinstance(e, int) and e == 0 and isinstance(b, int)):
                        c = base if isinstance(e, int) and e == 0 else up_chunk(base, e - 1, UPC, isinstance(e, int) and e == 1)
                        wait(used, c)
                    nc.gpsimd.tensor_copy(sel[:, :], cst[0:64, bass.ds(EYE + e, 1)].broadcast_to([64, P])).then_inc(sel_in, 1)

                def scatter(e, par):
                    wait(y_done, s0 + e + 1)
                    pool.indirect_dma_start(y_rows, bass.IndirectOffsetOnAxis(ap=dsti[:, par, 0:1], axis=0), y_sb[:, :], None,
                                            bounds_check=TOP * SEQ - 1, oob_is_err=False).then_inc(y_out, 16)

                def one(e, par):
                    if not (isinstance(e, int) and e == NE - 1):
                        prep(e + 1, 1 - par)
                    if not (isinstance(e, int) and e < 2):
                        scatter(e - 2, par)
                    if not (isinstance(e, int) and e == NE - 1):
                        gather(e + 1, 1 - par)
                        selector(e + 1, 1 - par)

                prep(0, 0)
                gather(0, 0)
                selector(0, 0)
                steps(pool, one)
                scatter(NE - 2, 0)
                scatter(NE - 1, 1)

            passes(pool, run)

        @block.scalar
        def _(act):
            def squares(n, ready, count):
                act.wait_ge(ready, count)
                if n:
                    act.wait_ge(sq_done, n)
                junk = (rl[:, 0:2, :] if n < NT else lg[:, :, :]).rearrange("p a n -> p (a n)")
                nc.scalar.activation(junk, h[:, n % NT, :], ACT.Square, accum_out=st[:, 0, n % NT:n % NT + 1]).then_inc(sq_done, 1)
                root(n)

            def root(n):
                t = n % NT
                act.wait_ge(ms_done, n + 1)
                nc.scalar.activation(st[:, 0, 8 + t:9 + t], st[:, 0, 4 + t:5 + t], ACT.Sqrt).then_inc(rs_done, 1)

            def hi(c, slot, raw, count, width=2048, fresh=False):
                act.wait_ge(raw_in[slot[0]], count)
                if not fresh:
                    act.wait_ge(used, c - SPLIT + 1)
                nc.scalar.activation(w_hi[:, slot[1], 0:width], raw[:, 0:width], ACT.Copy).then_inc(hi_done, 1)

            def hi1(c):
                s = raw1(c)
                hi(c, (s, c % SPLIT), raw_a[:, s, :], 16 * sum(raw1(i) == s for i in range(c + 1)),
                   2 * ATT_W if c < 4 else 2048, c < SPLIT)

            act.dma_start(stage[0:TAPS * NJ, :], conv_dw_w[0].rearrange("k (j c) -> (k j) c", j=NJ)).then_inc(s_stage, 16)
            for v, r0, r in ((conv_glu_b, 0, 8), (conv_dw_b, 8, 4), (conv_ln_g, 12, 4), (conv_ln_b, 16, 4)):
                act.dma_start(stage2[r0:r0 + r, :], v[0].rearrange("(j c) -> j c", j=r)).then_inc(s_stage, 16)
            for t in range(NT):
                squares(t, s_x[t], 16)
            act.wait_ge(par_tp, 1)
            nc.scalar.activation(par[:, 0:124], ps[:, 7, 0:124], ACT.Copy).then_inc(par_in, 1)
            nc.scalar.activation(par[:, 124:144], ps[:, 7, 128:148], ACT.Copy).then_inc(par_in, 1)
            for n in range(2 * NT):
                if n == 4:
                    hi1(0)
                act.wait_ge(tp_done, n + 1)
                t, k0 = n // 2, 4 * (n % 2)
                nc.scalar.activation(t_four(0, k0, t), ps[:, n, :].rearrange("p (k c) -> p k c", k=4), ACT.Copy).then_inc(thi_done, 1)
            for c in range(1, 6):
                hi1(c)
            act.wait_ge(rest_done, 1)
            nc.scalar.activation(uv[:, :, 0:64], ps[:, 4:8, 64:128], ACT.Copy).then_inc(uv_done, 1)
            nc.scalar.activation(uv[:, :, 64:68], ps[:, 4:8, 448:452], ACT.Copy).then_inc(uv_done, 1)

            def roped_hi(n):
                act.wait_ge(rtp_done, n + 1)
                nc.scalar.activation(r_hi[:, ROPED[n], :], ps[:, (n + 4) % 8, :], ACT.Copy).then_inc(rt_done, 1)

            def relu(t):
                for hh in range(IDX_HEADS):
                    n = (t - 1) * IDX_HEADS + hh
                    act.wait_ge(si_done, n + 1)
                    if t > 1:
                        act.wait_ge(cc_done, (t - 2) * IDX_HEADS + hh + 1)
                    nc.scalar.activation(rl[:, hh, 0:(t + 1) * P], ps[:, 4 + hh, 0:(t + 1) * P], ACT.Relu).then_inc(rl_done, 1)

            for n in range(4):
                roped_hi(n)
            relu(1)
            relu(2)
            for n in range(4, 8):
                roped_hi(n)
            relu(3)
            for c in (6, 7, 8):
                hi1(c)
            act.wait_ge(par_in, 2)
            for j in range(NJ):
                act.wait_ge(used, 6)
                nc.scalar.activation(sg[:, j, :], ps[:, j, :], ACT.Sigmoid, bias=par[:, 128 + j:129 + j]).then_inc(glu_sig, 1)
            hi1(9)
            turn = iter(range(len(PRODUCTS)))

            def products(count):
                for _ in range(count):
                    m = next(turn, None)
                    if m is None:
                        return
                    k, j = PRODUCTS[m]
                    w = par[:, k * NJ + j:k * NJ + j + 1]
                    if k == 0:
                        act.wait_ge(glu_done, j + 1)
                        i = nc.scalar.activation(acc[:, j, :], hpad[:, j, 0:SEQ], ACT.Identity, bias=par[:, 132 + j:133 + j], scale=w)
                    else:
                        if m >= len(POOL_J) + 2:
                            act.wait_ge(ptap_done, m - len(POOL_J) - 1)
                        i = nc.scalar.activation(prod[m % 2], hpad[:, j, k:k + SEQ], ACT.Copy, scale=w)
                    i.then_inc(prod_done, 1)

            products(2)

            def pt_copy(n):
                act.wait_ge(pt_done, n + 1)
                if n >= 2:
                    act.wait_ge(pv_done, n - 1)
                kk = (n // HEADS + 1) * P
                nc.scalar.activation(probs_t[:, n % 2, 0:kk], ps[:, 2 + n % 2, 0:kk], ACT.Copy).then_inc(pte_done, 1)

            def attn_hi(t):
                act.wait_ge(atp_done, t + 1)
                nc.scalar.activation(t_four(0, 0, t),
                                     ps[:, 6, :].rearrange("p (k c) -> p k c", k=4), ACT.Copy).then_inc(ahi_done, 1)

            for n in range(32):
                kk = (n // HEADS + 1) * P
                act.wait_ge(lg_done, n + 1)
                if n >= 2:
                    act.wait_ge(pt_done, n - 1)
                nc.scalar.activation(probs[:, n % 2, 0:kk], lg[:, n % 2, 0:kk], ACT.Exp, bias=mx[:, 1, n:n + 1],
                                     scale=HD ** -0.5, accum_out=mx[:, 2, n:n + 1]).then_inc(exp_done, 1)
                if n >= 1:
                    pt_copy(n - 1)
                if n == 6:
                    hi1(10)
                products(share(PRODUCT_SHARES, n))
                if n % HEADS == 4 and n > HEADS:
                    attn_hi(n // HEADS - 1)
            pt_copy(31)
            products(len(PRODUCTS))
            attn_hi(NT - 1)
            act.wait_ge(s_done, 32)
            for q in range(2):
                act.dma_start(bup_raw[q * NE:(q + 1) * NE, :], b_up[0]).then_inc(s_bup, 16)
                act.dma_start(bdn_raw[q * NE:(q + 1) * NE, :], b_down[0]).then_inc(s_bdn, 16)
            for j in range(NJ):
                act.wait_ge(cv_done, j + 1)
                nc.scalar.activation(sg[:, j, :], acc[:, j, :], ACT.Square).then_inc(csq_done, 1)
            act.wait_ge(cr_done, 1)
            nc.scalar.activation(lg[:, 0, :], lg[:, 1, :], ACT.Sqrt).then_inc(crs_done, 1)
            for j in range(NJ):
                act.wait_ge(cz_done, j + 1)
                nc.scalar.activation(sg[:, j, :], acc[:, j, :], ACT.Sigmoid).then_inc(csg_done, 1)
            for j in range(NJ):
                act.wait_ge(mix_done, j + 1)
                nc.scalar.activation(t_hi(NJ + j, slice(0, SEQ)), acc[:, j, :], ACT.Copy).then_inc(mhi_done, 1)
            hi1(11)
            nc.scalar.activation(tri_r[:, :], cst[:, TRI:TRI + 2 * P], ACT.Copy).then_inc(tri_done, 1)
            act.wait_ge(s_bup, 32)
            nc.scalar.activation(bup[:, :], bup_raw, ACT.Copy).then_inc(buphi_done, 1)
            act.wait_ge(s_bdn, 32)
            nc.scalar.activation(bdn_hi[:, :], bdn_raw, ACT.Copy).then_inc(bdhi_done, 1)
            act.wait_ge(s_wr, 32)
            nc.scalar.activation(wr2[:, :, 0:NE], wr[:, :, :], ACT.Copy).then_inc(wr2_hi, 1)
            for t in range(NT + 2):
                if t >= 2:
                    if t == 2:
                        act.wait_ge(bup_done, 1)
                        act.wait_ge(bdlo_done, 1)
                    for q in range(2):
                        n = 2 * (t - 2) + q
                        act.wait_ge(tp_done, 2 * NT + n + 1)
                        if t >= 4:
                            act.wait_ge(xr_done, t - 3)
                        nc.scalar.activation(xr_hi[:, t % 2, 4 * q:4 * q + 4, :],
                                             ps[:, n, :].rearrange("p (k c) -> p k c", k=4), ACT.Copy).then_inc(thi_done, 1)
                if t < NT:
                    squares(NT + t, h1_done, t + 1)
            act.wait_ge(rex_in, 1)
            nc.scalar.activation(rt[:, 128:256], rt[:, 128:256], ACT.Exp).then_inc(rex_out, 1)
            act.wait_ge(gtp_done, 1)
            nc.scalar.activation(gt_t[:, :], ps[0:64, 2, :], ACT.Copy).then_inc(gthi_done, 1)

            def run(b):
                s0 = b * NE
                base = C0 + b * RUN
                blocks = RUN // RAW

                def split(m, ring, turn):
                    s = ring % RAW
                    hi(base + m, (s, ring % SPLIT), raw_slot(s), 16 * (raw_before(s) + 1 + blocks * b + turn))

                def one(e, par, j=None):
                    def sp_chunk(part):
                        if isinstance(e, int):
                            m = part if e == 0 else PER * e - DNC + part
                            split(m, m % 24, m // RAW)
                        else:
                            m0 = PER * par - DNC + part
                            split(PER * e - DNC + part, m0 % 24, 3 * j + m0 // RAW)

                    first = isinstance(e, int) and e == 0
                    lastp = isinstance(e, int) and e == NE - 1
                    for u in range(UPC):
                        if not (first and u < SPLIT):
                            sp_chunk(u)
                        if u == 2 and not (isinstance(e, int) and e < 2):
                            y_copy(e - 2, par)
                        if u == 5 and not first:
                            a_hi_copy(e - 1)
                    if first:
                        if not lastp:
                            x_hi_copy(e + 1, 1 - par)
                        sig(e)
                        return
                    sp_chunk(UPC)
                    if not lastp:
                        x_hi_copy(e + 1, 1 - par)
                    for d in range(1, DNC):
                        sp_chunk(UPC + d)
                    sig(e)

                def y_copy(e, par):
                    act.wait_ge(used, dn_chunk(base, e, DNC - 1, isinstance(e, int) and e == NE - 1) + 1)
                    if not (isinstance(e, int) and e == 0 and isinstance(b, int)):
                        act.wait_ge(y_out, 16 * (s0 + e))
                    nc.scalar.activation(y_sb[:, :], ps[:, 4:6, :].rearrange("p a n -> p (a n)"), ACT.Copy).then_inc(y_done, 1)

                def a_hi_copy(e):
                    for q in range(2):
                        act.wait_ge(at_done, (s0 + e) * 2 + q + 1)
                        nc.scalar.activation(a_hi[:, 4 * q:4 * q + 4, :],
                                             ps[:, 6 + q, :].rearrange("p (k c) -> p k c", k=4), ACT.Copy).then_inc(athi_done, 1)

                def x_hi_copy(e, par):
                    for q in range(2):
                        act.wait_ge(xt_done, (s0 + e) * 2 + q + 1)
                        nc.scalar.activation(x_hi[:, par, 4 * q:4 * q + 4, :],
                                             ps[:, 6 + q, :].rearrange("p (k c) -> p k c", k=4), ACT.Copy).then_inc(xhi_done, 1)

                def sig(e):
                    act.wait_ge(gl_done, s0 + e + 1)
                    nc.scalar.activation(s_sb[:, :], g_sb[:, :], ACT.Sigmoid, scale=ALPHA).then_inc(sig_done, 1)

                for u in range(SPLIT):
                    split(u, u, 0)
                x_hi_copy(0, 0)
                one(0, 0)
                one(1, 1)
                with act.Fori(1, NE // 2 - 1) as j:
                    one(2 * j, 0, j)
                    one(2 * j + 1, 1, j)
                one(NE - 2, 0)
                one(NE - 1, 1)
                for d in range(DNC):
                    m = PER * NE - DNC + d
                    split(m, m % 24, m // RAW)
                    if d == 2:
                        y_copy(NE - 2, 0)
                        a_hi_copy(NE - 1)
                y_copy(NE - 1, 1)

            more = passes(act, run)

            base = act.snap(more * ((NB - 1) * RUN))
            turns = act.snap(more * (16 * (NB - 1) * RUN // RAW))

            def hi3(i):
                s = i % RAW
                hi(base + (C0 + RUN + i), (s, i % SPLIT), raw_slot(s), turns + 16 * (raw_before(s) + 1 + RUN // RAW))

            hi3(0)
            for n in range(2):
                act.wait_ge(ptp_done, n + 1)
                nc.scalar.activation(p_hi[:, n, :], ps[:, 6 + n, :], ACT.Copy).then_inc(pphi_done, 1)
            hi3(1)
            hi3(2)
            act.wait_ge(raw_in[4], turns + 16 * (raw_before(4) + 1 + RUN // RAW))
            nc.scalar.activation(w4_hi[:, :], raw_slot(4), ACT.Copy).then_inc(w4hi_done, 1)
            def proj_copy(t):
                if t < NT - 1:
                    act.wait_ge(proj_done, t + 1)
                else:
                    act.wait_ge(used, base + (C0 + RUN + 1))
                nc.scalar.activation(pp[:, t, :], ps[:, PROJ[t]:PROJ[t] + 2, :].rearrange("p a n -> p (a n)"), ACT.Copy).then_inc(pp_done, 1)

            def tile_norm(n, t, f):
                if n:
                    act.wait_ge(sq3_done, n)
                nc.scalar.activation(sq3[:, :], h[:, t, :], ACT.Square, accum_out=st[:, f, t:t + 1]).then_inc(sq3_done, 1)
                act.wait_ge(ms3_done, n + 1)
                nc.scalar.activation(st[:, f, 8 + t:9 + t], st[:, f, 4 + t:5 + t], ACT.Sqrt).then_inc(rs3_done, 1)

            def norm_in(n, t):
                act.wait_ge(yadd_done, TOP * (t + 1))
                tile_norm(n, t, 0)

            def norm_out(n, t):
                act.wait_ge(h3_done, t + 1)
                tile_norm(n, t, 1)

            def z_copy(t):
                if t >= 2:
                    act.wait_ge(gated, t - 1)
                for q in range(2):
                    act.wait_ge(zt_done, 2 * t + q + 1)
                    nc.scalar.activation(z_hi[:, t % 2, 4 * q:4 * q + 4, :],
                                         ps[:, 4 + 2 * (t % 2) + q, :].rearrange("p (k c) -> p k c", k=4), ACT.Copy).then_inc(zhi_done, 1)

            def sigmoid(t):
                act.wait_ge(gated, t + 1)
                if t:
                    act.wait_ge(h3_done, t)
                g0 = 2 * (t % 2)
                nc.scalar.activation(sgm[:, :], ps[:, g0:g0 + 2, :].rearrange("p a n -> p (a n)"), ACT.Sigmoid).then_inc(sg3_done, 1)

            for t in range(NT - 1):
                proj_copy(t)
            norm_in(0, 0)
            proj_copy(NT - 1)
            hi3(3)
            z_copy(0)
            norm_in(1, 1)
            z_copy(1)
            norm_in(2, 2)
            sigmoid(0)
            norm_out(3, 0)
            z_copy(2)
            norm_in(4, 3)
            sigmoid(1)
            norm_out(5, 1)
            z_copy(3)
            sigmoid(2)
            norm_out(6, 2)
            sigmoid(3)
            norm_out(7, 3)

        @block.vector
        def _(dve):
            seq = [0]

            def link(ins):
                seq[0] += 1
                ins.then_inc(dve_seq, 1)
                dve.wait_ge(dve_seq, seq[0])

            V = nc.vector

            def rms(n, t, f, sums, inverses, roots):
                dve.wait_ge(sums, n + 1)
                link(V.tensor_scalar(st[:, f, 12 + t:13 + t], st[:, f, t:t + 1], 1.0 / D, EPS, ALU.mult, ALU.add))
                V.reciprocal(st[:, f, 4 + t:5 + t], st[:, f, 12 + t:13 + t]).then_inc(inverses, 1)
                dve.wait_ge(roots, n + 1)

            def normed(dst, t, f, gain):
                return V.scalar_tensor_tensor(out=dst, in0=h[:, t, :], scalar=st[:, f, 8 + t:9 + t], in1=gain,
                                              op0=ALU.mult, op1=ALU.mult)

            def lo(c, slot, raw, width=2048):
                dve.wait_ge(hi_done, c + 1)
                V.tensor_tensor(w_lo[:, slot, 0:width], raw[:, 0:width], w_hi[:, slot, 0:width].bitcast(F32),
                                ALU.subtract).then_inc(lo_done, 1)

            def lo1(c):
                lo(c, c % SPLIT, raw_a[:, raw1(c), :], 2 * ATT_W if c < 4 else 2048)

            dve.wait_ge(s_gbc, 16)
            for t in range(NT):
                rms(t, t, 0, sq_done, ms_done, rs_done)
                normed(xn[:, t, :], t, 0, gbc[:, :]).then_inc(xn_done, 1)
            for n in range(2 * NT):
                if n == 4:
                    lo1(0)
                dve.wait_ge(thi_done, n + 1)
                t, k0 = n // 2, 4 * (n % 2)
                V.tensor_tensor(t_four(1, k0, t), ps[:, n, :].rearrange("p (k c) -> p k c", k=4),
                                t_four(0, k0, t).bitcast(F32), ALU.subtract).then_inc(tlo_done, 1)
            for c in range(1, 6):
                lo1(c)

            def rope(bank, col, heads, at):
                src = ps[:, bank:bank + NT, col:col + heads * HD].rearrange("p t (g d) -> p t g d", d=HD)
                dst = roped[:, :, at:at + heads * HD].rearrange("p t (g d) -> p t g d", d=HD)
                m1 = tmp[:, 0, 0:NT * heads * 32].rearrange("p (t g d) -> p t g d", t=NT, d=32)
                m2 = tmp[:, 1, 0:NT * heads * 32].rearrange("p (t g d) -> p t g d", t=NT, d=32)
                cs, sn = (cst[:, o:o + 128].rearrange("p (t d) -> p t d", t=NT).unsqueeze(2).broadcast_to([P, NT, heads, 32])
                          for o in (COS, SIN))
                x1, x2 = src[:, :, :, 0:32], src[:, :, :, 32:64]
                V.tensor_tensor(m1, x1, cs, ALU.mult)
                link(V.tensor_tensor(m2, x2, sn, ALU.mult))
                link(V.tensor_tensor(dst[:, :, :, 0:32], m1, m2, ALU.subtract))
                V.tensor_tensor(m1, x2, cs, ALU.mult)
                link(V.tensor_tensor(m2, x1, sn, ALU.mult))
                link(V.tensor_tensor(dst[:, :, :, 32:64], m1, m2, ALU.add))

            def twice(at):
                return V.tensor_copy(roped[:, :, at + HD:at + 2 * HD], roped[:, :, at:at + HD])

            def roped_lo(n):
                dve.wait_ge(rt_done, n + 1)
                V.tensor_tensor(r_lo[:, ROPED[n], :], ps[:, (n + 4) % 8, :], r_hi[:, ROPED[n], :].bitcast(F32),
                                ALU.subtract).then_inc(rlo_done, 1)

            OFF = (None, 0, 256, 640)

            def combine(t):
                kk = (t + 1) * P
                wk = work[:, OFF[t]:OFF[t] + kk]
                for hh in range(IDX_HEADS):
                    dve.wait_ge(rl_done, (t - 1) * IDX_HEADS + hh + 1)
                    if hh == 0:
                        i = V.tensor_scalar(wk, rl[:, 0, 0:kk], uv[:, t, 64:65], None, ALU.mult)
                    else:
                        i = V.scalar_tensor_tensor(out=wk, in0=rl[:, hh, 0:kk], scalar=uv[:, t, 64 + hh:65 + hh], in1=wk,
                                                   op0=ALU.mult, op1=ALU.add)
                    i.then_inc(cc_done, 1)
                    dve.wait_ge(cc_done, (t - 1) * IDX_HEADS + hh + 1)
                link(V.tensor_tensor(work[:, OFF[t] + kk - P:OFF[t] + kk], work[:, OFF[t] + kk - P:OFF[t] + kk],
                                     cst[:, CAUS:CAUS + P], ALU.add))

            dve.wait_ge(tp_done, 2 * NT)
            dve.wait_ge(rest_done, 1)
            dve.wait_ge(uv_done, 2)
            rope(4, 128, 5, 640)
            rope(4, 0, 1, 512)
            twice(512).then_inc(rope_done, 1)
            twice(896).then_inc(rope_done, 1)
            for n in range(4):
                roped_lo(n)
            combine(1)
            dve.wait_ge(used, 4)
            rope(0, 0, 8, 0)
            V.engine_nop().then_inc(rope_done, 1)
            combine(2)
            for n in range(4, 8):
                roped_lo(n)
            combine(3)
            dve.wait_ge(rtp_done, 8)
            V.memset(hpad[:, :, 0:30], 0.0)

            def select(t, r):
                wk = work[:, OFF[t]:OFF[t] + (t + 1) * P]
                link(V.max(m8[:, :], wk))
                link(V.match_replace(wk, m8[:, :], wk, TAKEN))
                if r == ROUNDS - 1:
                    link(V.tensor_scalar(wk, wk, 0.5 * (TAKEN + NEG), NEG, ALU.is_gt, ALU.mult))

            for r in range(ROUNDS):
                select(1, r)
            for r in range(ROUNDS):
                select(2, r)
            for r in range(EARLY):
                select(3, r)
            dve.wait_ge(par_in, 2)
            for j in range(NJ):
                if j < NJ - 1:
                    dve.wait_ge(conv_done, j + 1)
                else:
                    dve.wait_ge(used, 8)
                dve.wait_ge(glu_sig, j + 1)
                V.scalar_tensor_tensor(out=hpad[:, j, 30:30 + SEQ], in0=ps[:, 4 + j, :], scalar=par[:, 124 + j:125 + j],
                                       in1=sg[:, j, :], op0=ALU.add, op1=ALU.mult).then_inc(glu_done, 1)

            def tap(k):
                for j in DVE_J:
                    w = par[:, k * NJ + j:k * NJ + j + 1]
                    if k == 0:
                        dve.wait_ge(glu_done, j + 1)
                        i = V.tensor_scalar(acc[:, j, :], hpad[:, j, 0:SEQ], w, par[:, 132 + j:133 + j], ALU.mult, ALU.add)
                    else:
                        dve.wait_ge(tap_done, (k - 1) * len(DVE_J) + j + 1)
                        i = V.scalar_tensor_tensor(out=acc[:, j, :], in0=hpad[:, j, k:k + SEQ], scalar=w, in1=acc[:, j, :],
                                                   op0=ALU.mult, op1=ALU.add)
                    i.then_inc(tap_done, 1)

            def attn_norm(t):
                dve.wait_ge(pv_done, HEADS * (t + 1))
                dve.wait_ge(exp_done, HEADS * (t + 1))
                link(V.reciprocal(mx[:, 2, t * HEADS:(t + 1) * HEADS], mx[:, 2, t * HEADS:(t + 1) * HEADS]))
                if t >= 1:
                    dve.wait_ge(atp_done, t)
                V.tensor_tensor(attn[:, :].rearrange("p (h d) -> p h d", d=HD),
                                ps[:, 4 + t % 2, :].rearrange("p (h d) -> p h d", d=HD),
                                mx[:, 2, t * HEADS:(t + 1) * HEADS].unsqueeze(2).broadcast_to([P, HEADS, HD]),
                                ALU.mult).then_inc(an_done, 1)

            def attn_lo(t):
                dve.wait_ge(ahi_done, t + 1)
                V.tensor_tensor(t_four(1, 0, t), ps[:, 6, :].rearrange("p (k c) -> p k c", k=4),
                                t_four(0, 0, t).bitcast(F32), ALU.subtract).then_inc(alo_done, 1)

            taps = iter(range(TAPS))
            for n in range(32):
                t, kk = n // HEADS, (n // HEADS + 1) * P
                dve.wait_ge(s_done, n + 1)
                if n >= 2:
                    dve.wait_ge(exp_done, n - 1)
                mask = cst[:, CAUS:CAUS + P] if t == 0 else work[:, OFF[t]:OFF[t] + kk]
                link(V.tensor_tensor_reduce(lg[:, n % 2, 0:kk], ps[:, n % 2, 0:kk], mask, 1.0, TAKEN, ALU.add, ALU.max,
                                            mx[:, 0, n:n + 1]))
                V.tensor_scalar(mx[:, 1, n:n + 1], mx[:, 0, n:n + 1], -(HD ** -0.5), None, ALU.mult).then_inc(lg_done, 1)
                if n == 8:
                    dve.wait_ge(lo_done, 10)
                    lo1(10)
                if n < ROUNDS - EARLY:
                    select(3, n + EARLY)
                for _ in range(share(TAP_SHARES, n)):
                    tap(next(taps))
                if n % HEADS == 3 and n > HEADS:
                    attn_norm(t - 1)
                if n % HEADS == 6 and n > HEADS:
                    attn_lo(t - 1)
            attn_norm(NT - 1)
            attn_lo(NT - 1)
            dve.wait_ge(cs_done, 1)
            for j in range(NJ):
                V.scalar_tensor_tensor(out=acc[:, j, :], in0=ps[:, 7, :], scalar=-1.0 / CONV_W, in1=acc[:, j, :],
                                       op0=ALU.mult, op1=ALU.add).then_inc(cv_done, 1)
            dve.wait_ge(cs_done, 2)
            dve.wait_ge(exp_done, 32)
            link(V.tensor_scalar(lg[:, 0, :], ps[:, 6, :], 1.0 / CONV_W, EPS, ALU.mult, ALU.add))
            V.reciprocal(lg[:, 1, :], lg[:, 0, :]).then_inc(cr_done, 1)
            dve.wait_ge(crs_done, 1)
            dve.wait_ge(csq_done, NJ)
            for j in range(NJ):
                link(V.tensor_tensor(acc[:, j, :], acc[:, j, :], lg[:, 0, :], ALU.mult))
                V.tensor_scalar(acc[:, j, :], acc[:, j, :], par[:, 136 + j:137 + j], par[:, 140 + j:141 + j],
                                ALU.mult, ALU.add).then_inc(cz_done, 1)
            for j in range(NJ):
                dve.wait_ge(csg_done, j + 1)
                V.tensor_tensor(acc[:, j, :], acc[:, j, :], sg[:, j, :], ALU.mult).then_inc(mix_done, 1)
            for j in range(NJ):
                dve.wait_ge(mhi_done, j + 1)
                V.tensor_tensor(t_lo(NJ + j, slice(0, SEQ)), acc[:, j, :], t_hi(NJ + j, slice(0, SEQ)).bitcast(F32),
                                ALU.subtract).then_inc(mlo_done, 1)
            lo1(11)
            dve.wait_ge(buphi_done, 1)
            V.tensor_tensor(bup[32:64, :], bup_raw[32:64, :], bup[32:64, :].bitcast(F32), ALU.subtract).then_inc(bup_done, 1)
            dve.wait_ge(bdhi_done, 1)
            V.tensor_tensor(bdn_lo[:, :], bdn_raw, bdn_hi[:, :].bitcast(F32), ALU.subtract).then_inc(bdlo_done, 1)
            dve.wait_ge(wr2_hi, 1)
            V.tensor_tensor(wr2[:, :, NE:2 * NE], wr[:, :, :], wr2[:, :, 0:NE].bitcast(F32), ALU.subtract).then_inc(wr2_lo, 1)
            def xr_lo_copy(t):
                for q in range(2):
                    dve.wait_ge(thi_done, 2 * NT + 2 * t + q + 1)
                    V.tensor_tensor(xr_lo[:, t % 2, 4 * q:4 * q + 4, :], ps[:, 2 * t + q, :].rearrange("p (k c) -> p k c", k=4),
                                    xr_hi[:, t % 2, 4 * q:4 * q + 4, :].bitcast(F32), ALU.subtract).then_inc(tlo_done, 1)

            for t in range(NT + 1):
                if t < NT:
                    if t < NT - 1:
                        dve.wait_ge(out_done, t + 1)
                    else:
                        dve.wait_ge(used, C0)
                    V.tensor_tensor(h[:, t, :], h[:, t, :], ps[:, 2 * t:2 * t + 2, :].rearrange("p a n -> p (a n)"),
                                    ALU.add).then_inc(h1_done, 1)
                if t == 1:
                    dve.wait_ge(s_gbc, 32)
                if t >= 1:
                    rms(NT + t - 1, t - 1, 0, sq_done, ms_done, rs_done)
                    normed(xn[:, t - 1, :], t - 1, 0, gbc[:, :]).then_inc(xn_done, 1)
                if t >= 2:
                    xr_lo_copy(t - 2)
            xr_lo_copy(NT - 1)

            def r4(o):
                return rt[:, o:o + 128].rearrange("p (t e) -> p t e", t=NT)

            lgt, ex, gt, eq, cum = (r4(o) for o in (0, 128, 256, 384, 512))
            chosen = chosen_r[:, :, :].bitcast(F32)
            twin = rt[:, 768:1024].rearrange("p (t a e) -> p t a e", t=NT, a=2)
            top = work[:, 0:32].rearrange("p (t e) -> p t e", t=NT)
            cnt, tot = work[:, 32:36], work[:, 36:40]
            bc = lambda v: v.broadcast_to([P, NT, NE])
            dve.wait_ge(rlog_done, 1)
            dve.wait_ge(s_wr, 32)
            parts = ps[:, 0, 0:2 * NT * NE].rearrange("p (t a e) -> p t a e", t=NT, a=2)
            link(V.tensor_tensor(lgt, parts[:, :, 0, :], brt[:, :].unsqueeze(1).broadcast_to([P, NT, NE]), ALU.add))
            link(V.tensor_tensor(lgt, parts[:, :, 1, :], lgt, ALU.add))
            for t in range(NT):
                i = V.max(top[:, t, :], lgt[:, t, :])
            link(i)
            V.tensor_tensor(ex, lgt, bc(top[:, :, 0:1]), ALU.subtract).then_inc(rex_in, 1)
            V.tensor_tensor(eq, lgt, bc(top[:, :, 3:4]), ALU.is_equal)
            link(V.tensor_tensor(gt, lgt, bc(top[:, :, 3:4]), ALU.is_gt))
            V.reduce_sum(cnt, gt, AX.X)
            for t in range(NT):
                i = V.tensor_tensor_scan(cum[:, t, :], ones[:, 0:NE], eq[:, t, :], 0.0, ALU.mult, ALU.add)
            link(i)
            link(V.tensor_tensor(cum, cum, bc(cnt.unsqueeze(2)), ALU.add))
            link(V.scalar_tensor_tensor(out=eq, in0=cum, scalar=float(TOP), in1=eq, op0=ALU.is_le, op1=ALU.mult))
            link(V.tensor_tensor(chosen_r[:, :, :], gt, eq, ALU.add))
            V.engine_nop().then_inc(sel_done, 1)
            for t in range(NT):
                i = V.tensor_tensor_scan(cum[:, t, :], ones[:, 0:NE], chosen[:, t, :], 0.0, ALU.mult, ALU.add)
            dve.wait_ge(rex_out, 1)
            link(V.tensor_tensor(ex, ex, chosen, ALU.mult))
            link(V.reduce_sum(tot, ex, AX.X))
            link(V.reciprocal(tot, tot))
            V.tensor_tensor(info[:, :, :, 2], ex, bc(tot.unsqueeze(2)), ALU.mult)
            V.tensor_scalar(gt, cum, float(SEQ), -float(SEQ) - SKIP, ALU.mult, ALU.add)
            V.tensor_scalar(info[:, :, :, 0], bc(cst[:, TOK:TOK + NT].unsqueeze(2)), -SKIP, None, ALU.add)
            V.tensor_tensor(twin[:, :, 0, :], ex, bc(tot.unsqueeze(2)), ALU.mult)
            link(V.tensor_tensor(twin[:, :, 1, :], ex, bc(tot.unsqueeze(2)), ALU.mult))
            V.tensor_tensor(info[:, :, :, 1], gt, bc(cst[:, TOK:TOK + NT].unsqueeze(2)), ALU.add).then_inc(gates_done, 1)
            dve.wait_ge(pos_done, 1)
            V.tensor_scalar(work[:, 64:96], ps[:, 1, 128:160], 1.0, None, ALU.mult)
            link(V.scalar_tensor_tensor(out=cum, in0=ps[:, 1, 0:128].rearrange("p (t e) -> p t e", t=NT), scalar=1.0,
                                        in1=chosen, op0=ALU.add, op1=ALU.mult))
            for b in range(NB):
                i = V.tensor_scalar(pos[:, :, b * NE:(b + 1) * NE], cum, -1.0 - BLK * b, None, ALU.add)
            link(i)
            V.engine_nop().then_inc(tab_done, 1)
            link(V.reduce_max(work[:, 96:97], work[:, 64:96], AX.X))
            V.tensor_scalar(flag[:, :], work[:, 96:97], BLK + 0.5, None, ALU.is_gt).then_inc(flag_done, 1)
            for t in range(NT):
                i = V.tensor_scalar(onehot[:, t, :], cst[:, IOTA:IOTA + P], pos[:, t, 0:1], None, ALU.is_equal)
            i.then_inc(oh_done, 1)
            dve.wait_ge(gthi_done, 1)
            V.tensor_tensor(gt_t[32:64, :], ps[32:64, 2, :], gt_t[32:64, :].bitcast(F32), ALU.subtract).then_inc(gtlo_done, 1)

            def gates_bias(t):
                dve.wait_ge(bd_done, t + 1)
                V.tensor_tensor(h[:, t, :], h[:, t, :], ps[:, BIAS[t]:BIAS[t] + 2, :].rearrange("p a n -> p (a n)"),
                                ALU.add).then_inc(bias_done if t < NT - 1 else up_free, 1)

            def run(b):
                s0 = b * NE
                base = C0 + b * RUN

                def indices(e, par):
                    dve.wait_ge(list_done, s0 + e + 1)
                    if not (isinstance(e, int) and e == 0 and isinstance(b, int)):
                        dve.wait_ge(xg_in, 16 * (s0 + e))
                    V.tensor_scalar(gidx[:, :], ps[:, 6, 0:1], SKIP, None, ALU.add)
                    V.tensor_scalar(didx[:, par, :], ps[:, 6, 1:2], SKIP, None, ALU.add)
                    V.tensor_copy(gate[:, par, :], ps[:, 6, 2:3]).then_inc(idx_done, 1)

                def x_lo_copy(e, par):
                    for q in range(2):
                        dve.wait_ge(xhi_done, (s0 + e) * 2 + q + 1)
                        V.tensor_tensor(x_lo[:, par, 4 * q:4 * q + 4, :], ps[:, 6 + q, :].rearrange("p (k c) -> p k c", k=4),
                                        x_hi[:, par, 4 * q:4 * q + 4, :].bitcast(F32), ALU.subtract).then_inc(xlo_done, 1)

                def a_lo_copy(e):
                    for q in range(2):
                        dve.wait_ge(athi_done, (s0 + e) * 2 + q + 1)
                        V.tensor_tensor(a_lo[:, 4 * q:4 * q + 4, :], ps[:, 6 + q, :].rearrange("p (k c) -> p k c", k=4),
                                        a_hi[:, 4 * q:4 * q + 4, :].bitcast(F32), ALU.subtract).then_inc(atlo_done, 1)

                def glu_in(e, par, first=False):
                    dve.wait_ge(used, up_chunk(base, e, UPC, first))
                    V.tensor_scalar(g_sb[:, :], ps[:, 0:2, :].rearrange("p a n -> p (a n)"), LIMIT, None,
                                    ALU.min).then_inc(gl_done, 1)
                    V.tensor_scalar(l_sb[:, :], ps[:, 2:4, :].rearrange("p a n -> p (a n)"), -LIMIT, LIMIT,
                                    ALU.max, ALU.min).then_inc(up_free, 1)
                    if isinstance(e, int) and e < 2 and isinstance(b, int):
                        pass
                    else:
                        dve.wait_ge(y_out, 16 * (s0 + e - 1))
                    V.tensor_copy(dsti[:, par, :], didx[:, par, :])
                    dve.wait_ge(up_free, s0 + e + 2)
                    V.scalar_tensor_tensor(out=l_sb[:, :], in0=l_sb[:, :], scalar=1.0, in1=g_sb[:, :],
                                           op0=ALU.add, op1=ALU.mult).then_inc(gl2_done, 1)

                def glu_out(e, par):
                    dve.wait_ge(sig_done, s0 + e + 1)
                    dve.wait_ge(gl2_done, s0 + e + 1)
                    V.scalar_tensor_tensor(out=l_sb[:, :], in0=l_sb[:, :], scalar=gate[:, par, :], in1=s_sb[:, :],
                                           op0=ALU.mult, op1=ALU.mult).then_inc(act_done, 1)

                def one(e, par):
                    first = isinstance(e, int) and e == 0
                    lastp = isinstance(e, int) and e == NE - 1

                    def split(part):
                        ring = part if first else (PER * par - DNC + part) % 24
                        lo(base + part if first else base + PER * e - DNC + part, ring % SPLIT, raw_slot(ring))

                    for u in range(UPC):
                        if not (first and u < SPLIT):
                            split(u)
                        if u == 3 and not lastp:
                            indices(e + 1, 1 - par)
                        if u == 5 and not first:
                            a_lo_copy(e - 1)
                    if first:
                        x_lo_copy(e + 1, 1 - par)
                        glu_in(e, par, True)
                        glu_out(e, par)
                        return
                    split(UPC)
                    if not lastp:
                        x_lo_copy(e + 1, 1 - par)
                    split(UPC + 1)
                    split(UPC + 2)
                    glu_in(e, par)
                    split(UPC + 3)
                    glu_out(e, par)

                indices(0, 0)
                if isinstance(b, int):
                    for t in range(NT):
                        gates_bias(t)
                lo(base, 0, raw_slot(0))
                x_lo_copy(0, 0)
                for u in range(1, SPLIT):
                    lo(base + u, u, raw_slot(u))
                steps(dve, one)
                for d in range(DNC):
                    m = PER * NE - DNC + d
                    lo(base + m, m % SPLIT, raw_slot(m))
                    if d == 2:
                        a_lo_copy(NE - 1)

            more = passes(dve, run)

            base = dve.snap(more * ((NB - 1) * RUN))

            def lo3(i):
                lo(base + (C0 + RUN + i), i % SPLIT, raw_slot(i))

            lo3(0)
            for n in range(2):
                dve.wait_ge(pphi_done, n + 1)
                V.tensor_tensor(p_lo[:, n, :], ps[:, 6 + n, :], p_hi[:, n, :].bitcast(F32), ALU.subtract).then_inc(pplo_done, 1)
            lo3(1)
            lo3(2)
            dve.wait_ge(w4hi_done, 1)
            V.tensor_tensor(w4_lo[:, :], raw_slot(4), w4_hi[:, :].bitcast(F32), ALU.subtract).then_inc(w4lo_done, 1)

            def y_add(t, half):
                for q in (2 * half, 2 * half + 1):
                    m = 2 * t + half
                    dve.wait_ge(s_yb[m % 2], 16 * (m // 2 + 1))
                    if q:
                        dve.wait_ge(yadd_done, TOP * t + q)
                    V.tensor_tensor(h[:, t, :], h[:, t, :], yb[m % 2][:, q % 2, :], ALU.add).then_inc(yadd_done, 1)

            def norm_in(n, t):
                rms(n, t, 0, sq3_done, ms3_done, rs3_done)
                if t >= 2:
                    dve.wait_ge(zt_done, 2 * (t - 1))
                normed(xn3[:, t % 2, :], t, 0, gbc[:, :]).then_inc(xn3_done, 1)

            def z_lo_copy(t):
                for q in range(2):
                    dve.wait_ge(zhi_done, 2 * t + q + 1)
                    V.tensor_tensor(z_lo[:, t % 2, 4 * q:4 * q + 4, :], ps[:, 4 + 2 * (t % 2) + q, :].rearrange("p (k c) -> p k c", k=4),
                                    z_hi[:, t % 2, 4 * q:4 * q + 4, :].bitcast(F32), ALU.subtract).then_inc(zlo_done, 1)

            def finish(n, t):
                dve.wait_ge(sg3_done, t + 1)
                dve.wait_ge(pp_done, t + 1)
                link(V.tensor_tensor(pp[:, t, :], pp[:, t, :], sgm[:, :], ALU.mult))
                V.tensor_tensor(h[:, t, :], h[:, t, :], pp[:, t, :], ALU.add).then_inc(h3_done, 1)
                rms(n, t, 1, sq3_done, ms3_done, rs3_done)
                normed(pp[:, t, :], t, 1, gfin).then_inc(fin_done, 1)

            dve.wait_ge(s_gbc, 48)
            y_add(0, 0)
            y_add(0, 1)
            norm_in(0, 0)
            y_add(1, 0)
            z_lo_copy(0)
            lo3(3)
            y_add(1, 1)
            norm_in(1, 1)
            y_add(2, 0)
            z_lo_copy(1)
            y_add(2, 1)
            norm_in(2, 2)
            dve.wait_ge(s_gfin, 16)
            finish(3, 0)
            y_add(3, 0)
            z_lo_copy(2)
            y_add(3, 1)
            norm_in(4, 3)
            finish(5, 1)
            z_lo_copy(3)
            finish(6, 2)
            finish(7, 3)

        @block.tensor
        def _(pe):
            mm = nc.tensor.matmul

            def three(outs, l_hi, l_lo, r_hi, r_lo, start, stop):
                for o, r in zip(outs, r_hi):
                    mm(o, l_hi, r, start=start, stop=False)
                for o, r in zip(outs, r_lo):
                    mm(o, l_hi, r, start=False, stop=False)
                for o, r in zip(outs, r_hi):
                    i = mm(o, l_lo, r, start=False, stop=stop)
                return i

            def transposes(src, t):
                for k in range(NK):
                    i = nc.tensor.transpose(ps[:, 2 * t + k // 4, (k % 4) * P:(k % 4 + 1) * P],
                                            src[:, k * P:(k + 1) * P], ident)
                    if k % 4 == 3:
                        i.then_inc(tp_done, 1)

            pe.wait_ge(s_cst, 16)
            pe.wait_ge(s_stage, 16 * 5)
            nc.tensor.transpose(ps[:, 7, 0:124], stage[0:124, :], cst[0:124, IDENT:IDENT + 124])
            nc.tensor.transpose(ps[:, 7, 128:148], stage2[:, :], cst[0:20, IDENT:IDENT + 20]).then_inc(par_tp, 1)
            for t in range(NT):
                pe.wait_ge(xn_done, t + 1)
                if t == NT - 1:
                    pe.wait_ge(par_in, 2)
                transposes(xn[:, t, :], t)
            pe.wait_ge(tlo_done, 2 * NT)
            def att_products(c, a, t, rest, q):
                k, s, o = 2 * c + a, c % SPLIT, a * ATT_W
                tt = slice(t * P, (t + 1) * P)
                outs, r_h, r_l = [], [], []
                if q:
                    outs, r_h, r_l = [ps[:, t, :]], [w_hi[:, s, o:o + 512]], [w_lo[:, s, o:o + 512]]
                if rest:
                    outs, r_h, r_l = (outs + [ps[:, 4 + t, 0:REST_W]], r_h + [w_hi[:, s, o + 512:o + ATT_W]],
                                      r_l + [w_lo[:, s, o + 512:o + ATT_W]])
                return three(outs, t_hi(k, tt), t_lo(k, tt), r_h, r_l, k == 0, k == NK - 1)

            for c in range(3):
                pe.wait_ge(lo_done, c + 1)
                for a in range(2):
                    for t in range(NT):
                        i = att_products(c, a, t, True, True)
                i.then_inc(used, 1)
            pe.wait_ge(lo_done, 4)
            for rest in (True, False):
                for a in range(2):
                    for t in range(NT):
                        i = att_products(3, a, t, rest, not rest)
                i.then_inc(rest_done if rest else used, 1)

            def roped_transposed(n):
                for t in range(NT):
                    i = nc.tensor.transpose(ps[:, (n + 4) % 8, t * P:(t + 1) * P], roped[:, t, ROPED[n] * P:(ROPED[n] + 1) * P], ident)
                i.then_inc(rtp_done, 1)

            def split_scores(out, half, a, a_cols, b, b_cols):
                mm(out, r_hi[half, a, a_cols], r_hi[half, b, b_cols], start=True, stop=False)
                mm(out, r_hi[half, a, a_cols], r_lo[half, b, b_cols], start=False, stop=False)
                return mm(out, r_lo[half, a, a_cols], r_hi[half, b, b_cols], start=False, stop=True)

            pe.wait_ge(rope_done, 2)
            for n in range(4):
                roped_transposed(n)
            def indexer(t):
                for hh in range(IDX_HEADS):
                    half = slice(64 * (hh % 2), 64 * (hh % 2) + 64)
                    if t > 1:
                        pe.wait_ge(rl_done, (t - 2) * IDX_HEADS + hh + 1)
                    split_scores(ps[:, 4 + hh, 0:(t + 1) * P], half, 5 + hh // 2, slice(t * P, (t + 1) * P),
                                 7, slice(0, (t + 1) * P)).then_inc(si_done, 1)

            pe.wait_ge(rlo_done, 4)
            indexer(1)
            indexer(2)
            pe.wait_ge(rope_done, 3)
            for n in range(4, 8):
                roped_transposed(n)
            indexer(3)
            every = slice(0, SEQ)

            def conv_products(c, a, j):
                k, s, o = 4 * (c % 2) + a, c % SPLIT, a * CONV_W + j * P
                return three([ps[:, j if c < 6 else 4 + j, :]], w_hi[:, s, o:o + P], w_lo[:, s, o:o + P],
                             [t_hi(k, every)], [t_lo(k, every)], k == 0, k == NK - 1)

            pe.wait_ge(rlo_done, 8)
            for c in (4, 5, 6):
                pe.wait_ge(lo_done, c + 1)
                if c == 6:
                    pe.wait_ge(rl_done, 3 * IDX_HEADS)
                for a in range(4):
                    for j in range(NJ):
                        i = conv_products(c, a, j)
                i.then_inc(used, 1)
            pe.wait_ge(lo_done, 8)
            for j in range(NJ):
                for a in range(4):
                    i = conv_products(7, a, j)
                i.then_inc(conv_done if j < NJ - 1 else used, 1)

            def scores(n):
                t, hh = n // HEADS, n % HEADS
                half = slice(64 * (hh % 2), 64 * (hh % 2) + 64)
                if n >= 2:
                    pe.wait_ge(lg_done, n - 1)
                split_scores(ps[:, n % 2, 0:(t + 1) * P], half, hh // 2, slice(t * P, (t + 1) * P),
                             4, slice(0, (t + 1) * P)).then_inc(s_done, 1)

            def probs_transposed(n):
                pe.wait_ge(exp_done, n + 1)
                if n >= 2:
                    pe.wait_ge(pte_done, n - 1)
                for kb in range(n // HEADS + 1):
                    i = nc.tensor.transpose(ps[:, 2 + n % 2, kb * P:(kb + 1) * P], probs[:, n % 2, kb * P:(kb + 1) * P], ident)
                i.then_inc(pt_done, 1)

            def values(n):
                t, hh = n // HEADS, n % HEADS
                pe.wait_ge(pte_done, n + 1)
                if hh == 0 and t >= 2:
                    pe.wait_ge(an_done, t - 1)
                for kb in range(t + 1):
                    i = mm(ps[:, 4 + t % 2, hh * HD:(hh + 1) * HD], probs_t[:, n % 2, kb * P:(kb + 1) * P], uv[:, kb, 0:HD],
                           start=(kb == 0), stop=(kb == t))
                i.then_inc(pv_done, 1)

            def attn_transposed(t):
                pe.wait_ge(an_done, t + 1)
                if t >= 1:
                    pe.wait_ge(alo_done, t)
                for k in range(4):
                    i = nc.tensor.transpose(ps[:, 6, k * P:(k + 1) * P], attn[:, k * P:(k + 1) * P], ident)
                i.then_inc(atp_done, 1)

            pe.wait_ge(glu_sig, NJ)
            for n in range(32):
                scores(n)
                if n == 1:
                    pe.wait_ge(glu_done, NJ)
                if n >= 1:
                    probs_transposed(n - 1)
                if n >= 2:
                    values(n - 2)
                if n % HEADS == 4 and n > HEADS:
                    attn_transposed(n // HEADS - 1)
            probs_transposed(31)
            values(30)
            values(31)
            attn_transposed(NT - 1)
            def out_products(c, a, t):
                k, s, o = 2 * (c - 8) + a, c % SPLIT, a * 1024
                tt = slice(t * P, (t + 1) * P)
                return three([ps[:, 2 * t, :], ps[:, 2 * t + 1, :]], t_hi(k, tt), t_lo(k, tt),
                             [w_hi[:, s, o:o + 512], w_hi[:, s, o + 512:o + 1024]],
                             [w_lo[:, s, o:o + 512], w_lo[:, s, o + 512:o + 1024]], k == 0, k == NK - 1)

            def attention_part(c, tiles):
                for a in range(2):
                    for t in tiles:
                        i = out_products(c, a, t)
                return i

            pe.wait_ge(tap_done, TAPS * len(DVE_J))
            pe.wait_ge(ptap_done, (TAPS - 1) * len(POOL_J))
            for j in range(NJ):
                i = mm(ps[:, 7, :], ones, acc[:, j, :], start=(j == 0), stop=(j == NJ - 1))
            i.then_inc(cs_done, 1)
            pe.wait_ge(alo_done, NT)
            pe.wait_ge(lo_done, 9)
            attention_part(8, range(3))
            for j in range(NJ):
                pe.wait_ge(csq_done, j + 1)
                i = mm(ps[:, 6, :], ones, sg[:, j, :], start=(j == 0), stop=(j == NJ - 1))
            i.then_inc(cs_done, 1)
            pe.wait_ge(lo_done, 10)
            attention_part(9, range(3))
            pe.wait_ge(cr_done, 1)
            attention_part(8, (3,)).then_inc(used, 1)
            attention_part(9, (3,)).then_inc(used, 1)
            pe.wait_ge(lo_done, 11)
            for a in range(2):
                pe.wait_ge(mlo_done, a + 1)
                for t in range(NT):
                    i = out_products(10, a, t)
            i.then_inc(used, 1)
            pe.wait_ge(lo_done, 12)
            pe.wait_ge(mlo_done, NJ)
            for t in range(NT):
                out_products(11, 0, t)
                out_products(11, 1, t).then_inc(out_done if t < NT - 1 else used, 1)
            pe.wait_ge(wr2_lo, 1)
            for t in range(NT + 1):
                if t < NT:
                    pe.wait_ge(xn_done, NT + t + 1)
                    transposes(xn[:, t, :], t)
                if t >= 1:
                    pe.wait_ge(tlo_done, 2 * NT + 2 * t)
                    o, b = (t - 1) * 2 * NE, (t - 1) % 2
                    for k in range(NK):
                        mm(ps[:, 0, o:o + 2 * NE], xr_hi[:, b, k, :], wr2[:, k, :], start=(k == 0), stop=False)
                        i = mm(ps[:, 0, o:o + NE], xr_lo[:, b, k, :], wr2[:, k, 0:NE], start=False, stop=(k == NK - 1))
                    i.then_inc(xr_done if t < NT else rlog_done, 1)
            pe.wait_ge(sel_done, 1)
            pe.wait_ge(tri_done, 1)
            for t in range(NT):
                for u in range(t + 1):
                    mm(ps[:, 1, t * NE:(t + 1) * NE], tri_r[:, 0:P] if u == t else tri_r[:, P:2 * P], chosen_r[:, u, :],
                       start=(u == 0), stop=(u == t))
            for u in range(NT):
                i = mm(ps[:, 1, 128:160], tri_r[:, P:2 * P], chosen_r[:, u, :], start=(u == 0), stop=(u == NT - 1))
            i.then_inc(pos_done, 1)
            pe.wait_ge(gates_done, 1)
            for t in range(NT):
                i = nc.tensor.transpose(ps[0:64, 2, t * P:(t + 1) * P], rt[:, 768 + 64 * t:768 + 64 * (t + 1)], ident)
            i.then_inc(gtp_done, 1)

            def gates_bias(t):
                for q in range(2):
                    tt, cols = slice(t * P, (t + 1) * P), slice(q * 512, (q + 1) * 512)
                    mm(ps[:, BIAS[t] + q, :], gt_t[:, tt], bdn_hi[:, cols], start=True, stop=False)
                    i = mm(ps[:, BIAS[t] + q, :], gt_t[:, tt], bdn_lo[:, cols], start=False, stop=True)
                i.then_inc(bd_done, 1)


            def run(b):
                s0 = b * NE
                base = C0 + b * RUN

                def listing(e):
                    pe.wait_ge(oh_done, s0 + e + 1)
                    for t in range(NT):
                        i = mm(ps[:, 6, 0:3], onehot[:, t, :], info[:, t, bass.ds(e, 1), :].rearrange("p o c -> p (o c)"),
                               start=(t == 0), stop=(t == NT - 1))
                    i.then_inc(list_done, 1)

                def x_transposed(e):
                    pe.wait_ge(xg_in, 16 * (s0 + e + 1))
                    for k in range(NK):
                        i = nc.tensor.transpose(ps[:, 6 + k // 4, (k % 4) * P:(k % 4 + 1) * P], xg[:, k * P:(k + 1) * P], ident)
                        if k % 4 == 3:
                            i.then_inc(xt_done, 1)

                def a_transposed(e):
                    pe.wait_ge(act_done, s0 + e + 1)
                    for k in range(NK):
                        i = nc.tensor.transpose(ps[:, 6 + k // 4, (k % 4) * P:(k % 4 + 1) * P], l_sb[:, k * P:(k + 1) * P], ident)
                        if k % 4 == 3:
                            i.then_inc(at_done, 1)

                def up(e, par, u, c, ring):
                    pe.wait_ge(lo_done, c + 1)
                    s = ring % SPLIT
                    cols = [slice(n * 512, (n + 1) * 512) for n in range(4)]
                    three([ps[:, n, :] for n in range(4)], x_hi[:, par, u, :], x_lo[:, par, u, :],
                          [w_hi[:, s, n] for n in cols], [w_lo[:, s, n] for n in cols], False, u == UPC - 1).then_inc(used, 1)

                def down(d, c, ring):
                    pe.wait_ge(lo_done, c + 1)
                    s = ring % SPLIT
                    for a in range(2):
                        k = 2 * d + a
                        cols = [slice(a * 1024 + n * 512, a * 1024 + (n + 1) * 512) for n in range(2)]
                        i = three([ps[:, 4 + n, :] for n in range(2)], a_hi[:, k, :], a_lo[:, k, :],
                                  [w_hi[:, s, n] for n in cols], [w_lo[:, s, n] for n in cols], k == 0, k == NK - 1)
                    i.then_inc(used, 1)

                def downs(e, par, last=False):
                    pe.wait_ge(atlo_done, 2 * (s0 + e + 1))
                    if not (isinstance(e, int) and e == 0 and isinstance(b, int)):
                        pe.wait_ge(y_done, s0 + e)
                    for d in range(DNC):
                        down(d, dn_chunk(base, e, d, last), slot8(par, (0 if last else UPC) + d))

                def one(e, par):
                    first = isinstance(e, int) and e == 0
                    lastp = isinstance(e, int) and e == NE - 1
                    pe.wait_ge(up_free, s0 + e + 1)
                    pe.wait_ge(xlo_done, 2 * (s0 + e + 1))
                    pe.wait_ge(sel_in, s0 + e + 1)
                    for n in range(4):
                        mm(ps[:, n, :], sel[:, :], bup[:, n * 512:(n + 1) * 512], start=True, stop=False)
                    for u in range(UPC):
                        ring = slot8(par, u, first)
                        up(e, par, u, up_chunk(base, e, u, first), ring)
                        if u == 0 and not lastp:
                            listing(e + 1)
                        if u == 2 and not first:
                            if not lastp:
                                pe.wait_ge(idx_done, s0 + e + 2)
                            a_transposed(e - 1)
                        if u == 5 and not lastp:
                            if first:
                                pe.wait_ge(idx_done, s0 + e + 2)
                            else:
                                pe.wait_ge(atlo_done, 2 * (s0 + e))
                            x_transposed(e + 1)
                    if not first:
                        downs(e - 1, par)

                if isinstance(b, int):
                    pe.wait_ge(bup_done, 1)
                else:
                    pe.wait_ge(atlo_done, 2 * s0)
                listing(0)
                if isinstance(b, int):
                    pe.wait_ge(gtlo_done, 1)
                    pe.wait_ge(bdlo_done, 1)
                    for t in range(3):
                        gates_bias(t)
                    pe.wait_ge(bias_done, 1)
                    gates_bias(3)
                pe.wait_ge(idx_done, s0 + 1)
                x_transposed(0)
                pe.wait_ge(xlo_done, 2 * (s0 + 1))
                steps(pe, one)
                a_transposed(NE - 1)
                downs(NE - 1, 0, True)

            more = passes(pe, run)

            base = pe.snap(more * ((NB - 1) * RUN))
            ybase = pe.snap(more * ((NB - 1) * NE))
            pe.wait_ge(s_p, 16)
            pe.wait_ge(atlo_done, ybase * 2 + 2 * NE)
            for n in range(2):
                for t in range(NT):
                    i = nc.tensor.transpose(ps[:, 6 + n, t * P:(t + 1) * P], p_sb[:, t, n * P:(n + 1) * P], ident)
                i.then_inc(ptp_done, 1)
            pe.wait_ge(pplo_done, 2)
            pe.wait_ge(up_free, ybase + (NE + 1))

            def gate_products(outs, k, l_hi, l_lo, r_hi, r_lo, n_k):
                cols = [slice(k % 2 * 1024 + n * 512, k % 2 * 1024 + (n + 1) * 512) for n in range(2)]
                return three(outs, l_hi, l_lo, [r_hi[:, n] for n in cols], [r_lo[:, n] for n in cols], k == 0, k == n_k - 1)

            pe.wait_ge(lo_done, base + (C0 + RUN + 1))
            for t in range(NT):
                if PROJ[t] == 4:
                    pe.wait_ge(y_done, ybase + NE)
                tt = slice(t * P, (t + 1) * P)
                for k in range(2):
                    i = gate_products([ps[:, PROJ[t] + n, :] for n in range(2)], k, p_hi[:, k, tt], p_lo[:, k, tt],
                                      w_hi[:, 0, :], w_lo[:, 0, :], 2)
                i.then_inc(proj_done if t < NT - 1 else used, 1)

            def z_transposed(t):
                pe.wait_ge(xn3_done, t + 1)
                if t < 2:
                    pe.wait_ge(pp_done, NT)
                else:
                    pe.wait_ge(zlo_done, 2 * (t - 1))
                for k in range(NK):
                    i = nc.tensor.transpose(ps[:, 4 + 2 * (t % 2) + k // 4, (k % 4) * P:(k % 4 + 1) * P],
                                            xn3[:, t % 2, k * P:(k + 1) * P], ident)
                    if k % 4 == 3:
                        i.then_inc(zt_done, 1)

            w4_at = {0: (w_hi[:, 1, :], w_lo[:, 1, :]), 1: (w_hi[:, 2, :], w_lo[:, 2, :]),
                     2: (w_hi[:, 0, :], w_lo[:, 0, :]), 3: (w4_hi, w4_lo)}
            z_transposed(0)
            for t in range(NT):
                if t >= 2:
                    pe.wait_ge(sg3_done, t - 1)
                for k in range(NK):
                    if k % 4 == 0:
                        pe.wait_ge(zlo_done, 2 * t + k // 4 + 1)
                    if t == 0 and k < 6 and k % 2 == 0:
                        pe.wait_ge(lo_done, base + (C0 + RUN + 2 + k // 2))
                    if t == 0 and k == 6:
                        pe.wait_ge(w4lo_done, 1)
                    i = gate_products([ps[:, 2 * (t % 2) + n, :] for n in range(2)], k, z_hi[:, t % 2, k, :], z_lo[:, t % 2, k, :],
                                      *w4_at[k // 2], NK)
                    if k == 4 and t + 1 < NT:
                        z_transposed(t + 1)
                i.then_inc(gated, 1)


def constants():
    c = np.zeros((P, NCONST), np.float32)
    r = np.arange(P)
    c[:, IDENT:IDENT + P] = np.eye(P)
    c[:, TRI:TRI + P] = r[:, None] < r[None, :]
    c[:, ONES:ONES + P] = 1.0
    c[:, IOTA:IOTA + P] = r[None, :]
    c[:, CAUS:CAUS + P] = np.where(r[None, :] <= r[:, None], 0.0, NEG)
    inv = np.float32(10000.0) ** (-np.arange(0, HD, 2, dtype=np.float32) / np.float32(HD))
    ang = (np.arange(SEQ, dtype=np.float32)[:, None] * inv[None, :]).astype(np.float32)
    for o, f in ((COS, np.cos), (SIN, np.sin)):
        c[:, o:o + P] = f(ang).reshape(NT, P, 32).transpose(1, 0, 2).reshape(P, NT * 32)
    c[:, TOK:TOK + NT] = np.arange(NT)[None, :] * P + r[:, None]
    c[0:64, EYE:EYE + NE] = (np.arange(64)[:, None] % NE) == np.arange(NE)[None, :]
    return c


_INS = ["x", "p", "w_in", "w_out", "g_mix", "g_ffn", "conv_glu_b", "conv_dw_w", "conv_dw_b", "conv_ln_g", "conv_ln_b",
        "w_router", "b_router", "w_up", "b_up", "w_down", "b_down", "w_ple_proj", "w_ple_gate", "g_ple", "g_final"]


def kernel(**inputs):
    import numpy as _np
    import concourse.bacc as _bacc
    from concourse import mybir as _mybir
    from concourse.bass_utils import run_bass_kernel_spmd as _run

    nc = _bacc.Bacc("TRN2", target_bir_lowering=False, num_devices=1)
    arrays, args = {}, []
    for name in _INS + ["constants"]:
        a = constants() if name == "constants" else _np.ascontiguousarray(inputs[name])
        arrays[f"in_{name}_dram"] = a
        args.append(nc.dram_tensor(f"in_{name}_dram", a.shape, _mybir.dt.from_np(a.dtype), kind="ExternalInput").ap())
    args.append(nc.dram_tensor("out_0_dram", (1, SEQ, D), _mybir.dt.float32, kind="ExternalOutput").ap())
    build(nc, *args)
    r = _run(nc, [arrays], core_ids=[0])
    return r.results[0]["out_0_dram"]
```
